# Optimizing a Trainium2 kernel written in Bass

```python
import math
import jax, jax.numpy as jnp
from jax import lax
import numpy as np

D_MODEL = 1024
BATCH = 1
SEQ = 512
DEPTH = 1

HEAD_DIM = 64
N_ATTN_HEADS = 8
N_DELTA_HEADS = 8
ATTN_WIDTH = N_ATTN_HEADS * HEAD_DIM
DELTA_WIDTH = N_DELTA_HEADS * HEAD_DIM
MIX_WIDTH = ATTN_WIDTH + DELTA_WIDTH
DILATED_BRANCHES = ((128, 1), (512, 4), (2048, 16))
PAD_UNIT = 2048
N_BUCKETS = 32
MAX_DISTANCE = 2048
CONV_WIDTH = 4
CHUNK = 64
D_FF = (8 * D_MODEL + 3 * 256 - 1) // (3 * 256) * 256
IN_WIDTH = 3 * ATTN_WIDTH + 4 * DELTA_WIDTH + 2 * N_DELTA_HEADS
EPS = 1e-6
NEG_INF = -1e30


def _rmsnorm(x, g):
    x32 = x.astype(jnp.float32)
    y = x32 * lax.rsqrt(jnp.mean(x32 * x32, axis=-1, keepdims=True) + EPS)
    return (y * g.astype(jnp.float32)).astype(x.dtype)

def _l2norm(x):
    return x * lax.rsqrt(jnp.sum(x * x, axis=-1, keepdims=True) + EPS)

def _t5_bucket(distance):
    max_exact = N_BUCKETS // 2
    dist_f = jnp.maximum(distance, 1).astype(jnp.float32)
    large = max_exact + (jnp.log(dist_f / max_exact) / math.log(MAX_DISTANCE / max_exact)
                         * (N_BUCKETS - max_exact)).astype(jnp.int32)
    return jnp.where(distance < max_exact, distance, jnp.minimum(large, N_BUCKETS - 1))

def _dilated_branch(q, k, v, rel_bias, window, dilation):
    b, h, p, dh = q.shape
    band = window // dilation
    length = p // dilation
    n_blocks = length // band

    def to_blocks(t):
        t = t.reshape(b, h, length, dilation, dh).transpose(0, 1, 3, 2, 4)
        return t.reshape(b, h, dilation, n_blocks, band, dh)

    qb, kb, vb = to_blocks(q), to_blocks(k), to_blocks(v)

    def with_prev(t):
        prev = jnp.pad(t, ((0, 0), (0, 0), (0, 0), (1, 0), (0, 0), (0, 0)))[:, :, :, :-1]
        return jnp.concatenate([prev, t], axis=-2)

    kw, vw = with_prev(kb), with_prev(vb)
    qi = jnp.arange(band)[:, None]
    kj = jnp.arange(2 * band)[None, :]
    steps = qi + band - kj
    in_window = (steps >= 0) & (steps <= band)
    not_before_start = (jnp.arange(n_blocks)[:, None, None] > 0) | (kj >= band)[None]
    valid = in_window[None] & not_before_start
    bias = rel_bias.astype(jnp.float32)[_t5_bucket(jnp.maximum(steps, 0) * dilation)]
    bias = bias.transpose(2, 0, 1)
    s = jnp.einsum('bhrnqd,bhrnkd->bhrnqk', qb * dh ** -0.5, kw) + bias[None, :, None, None]
    s = jnp.where(valid, s, NEG_INF)
    m = jnp.max(s, axis=-1, keepdims=True)
    e = jnp.exp(s - m)
    denom = jnp.sum(e, axis=-1, keepdims=True)
    o = jnp.einsum('bhrnqk,bhrnkd->bhrnqd', e, vw) / denom
    lse = (m + jnp.log(denom))[..., 0]
    o = o.reshape(b, h, dilation, length, dh).transpose(0, 1, 3, 2, 4).reshape(b, h, p, dh)
    lse = lse.reshape(b, h, dilation, length).transpose(0, 1, 3, 2).reshape(b, h, p)
    return o, lse

def _dilated_attention(q, k, v, rel_bias):
    b, s, h, dh = q.shape
    p = (s + PAD_UNIT - 1) // PAD_UNIT * PAD_UNIT

    def to_bhpd(t):
        t = jnp.pad(t.astype(jnp.float32), ((0, 0), (0, p - s), (0, 0), (0, 0)))
        return t.transpose(0, 2, 1, 3)

    q, k, v = to_bhpd(q), to_bhpd(k), to_bhpd(v)
    outs, lses = [], []
    for window, dilation in DILATED_BRANCHES:
        o_i, lse_i = _dilated_branch(q, k, v, rel_bias, window, dilation)
        outs.append(o_i)
        lses.append(lse_i)
    w = jax.nn.softmax(jnp.stack(lses), axis=0)
    o = jnp.sum(w[..., None] * jnp.stack(outs), axis=0)
    return o[:, :, :s].transpose(0, 2, 1, 3).reshape(b, s, h * dh)

def _causal_conv(x, w):
    return lax.conv_general_dilated(x, w[:, None, :], window_strides=(1,),
                                    padding=((CONV_WIDTH - 1, 0),),
                                    dimension_numbers=('NWC', 'WIO', 'NWC'),
                                    feature_group_count=x.shape[-1])

def _chunk_gated_delta_rule(q, k, v, g, beta):
    b, s, h, dk = q.shape
    dv = v.shape[-1]
    nc = s // CHUNK

    def chunks(t):
        return t.reshape(b, nc, CHUNK, h, t.shape[-1]).transpose(1, 0, 3, 2, 4)

    qc, kc, vc = chunks(q), chunks(k), chunks(v)
    gcum = jnp.cumsum(g.reshape(b, nc, CHUNK, h).transpose(1, 0, 3, 2), axis=-1)
    bc = beta.reshape(b, nc, CHUNK, h).transpose(1, 0, 3, 2)
    causal = jnp.tril(jnp.ones((CHUNK, CHUNK), dtype=bool))
    strict = jnp.tril(jnp.ones((CHUNK, CHUNK), dtype=bool), k=-1)
    diff = gcum[..., :, None] - gcum[..., None, :]
    decay = jnp.where(causal, jnp.exp(jnp.where(causal, diff, 0.0)), 0.0)
    k_beta = kc * bc[..., None]
    a_mat = jnp.where(strict, jnp.einsum('nbhcd,nbhed->nbhce', k_beta, kc) * decay, 0.0)
    rhs = jnp.concatenate([vc * bc[..., None], k_beta * jnp.exp(gcum)[..., None]], axis=-1)
    sol = lax.linalg.triangular_solve(a_mat + jnp.eye(CHUNK, dtype=a_mat.dtype), rhs,
                                      left_side=True, lower=True, unit_diagonal=True)
    u, w = sol[..., :dv], sol[..., dv:]
    qk = jnp.where(causal, jnp.einsum('nbhcd,nbhed->nbhce', qc, kc) * decay, 0.0)

    def step(state, xs):
        q_i, k_i, u_i, w_i, g_i, qk_i = xs
        v_new = u_i - jnp.einsum('bhck,bhkv->bhcv', w_i, state)
        o_i = (jnp.einsum('bhck,bhkv->bhcv', q_i * jnp.exp(g_i)[..., None], state)
               + jnp.einsum('bhce,bhev->bhcv', qk_i, v_new))
        g_last = g_i[..., -1]
        k_dec = k_i * jnp.exp(g_last[..., None] - g_i)[..., None]
        state = state * jnp.exp(g_last)[..., None, None] + jnp.einsum('bhck,bhcv->bhkv', k_dec, v_new)
        return state, o_i

    state0 = jnp.zeros((b, h, dk, dv), jnp.float32)
    _, o = lax.scan(step, state0, (qc, kc, u, w, gcum, qk))
    return o.transpose(1, 0, 3, 2, 4).reshape(b, s, h, dv)

def _gated_deltanet(q, k, v, z, b_logit, a_logit, conv_w, a_log, dt_bias, norm_g):
    bsz, s, _ = q.shape
    qkv = jax.nn.silu(_causal_conv(jnp.concatenate([q, k, v], axis=-1), conv_w))
    q, k, v = jnp.split(qkv.astype(jnp.float32), 3, axis=-1)
    shp = (bsz, s, N_DELTA_HEADS, HEAD_DIM)
    q = _l2norm(q.reshape(shp)) * HEAD_DIM ** -0.5
    k = _l2norm(k.reshape(shp))
    v = v.reshape(shp)
    beta = jax.nn.sigmoid(b_logit.astype(jnp.float32))
    g = -jnp.exp(a_log.astype(jnp.float32)) * jax.nn.softplus(
        a_logit.astype(jnp.float32) + dt_bias.astype(jnp.float32))
    o = _chunk_gated_delta_rule(q, k, v, g, beta)
    o = _rmsnorm(o, norm_g) * jax.nn.silu(z.astype(jnp.float32).reshape(shp))
    return o.reshape(bsz, s, DELTA_WIDTH).astype(z.dtype)

def first_inputs(seed: int = 0) -> dict:
    key = jax.random.key(seed)
    ks = jax.random.split(key, 20)
    f32 = jnp.float32

    def nrm(k, shape, scale):
        return jax.random.normal(k, shape, f32) * scale

    dt = jnp.exp(jax.random.uniform(ks[9], (DEPTH, N_DELTA_HEADS), f32,
                                    minval=math.log(1e-3), maxval=math.log(1e-1)))
    return {
        'x': nrm(ks[0], (BATCH, SEQ, D_MODEL), 1.0),
        'c': nrm(ks[1], (BATCH, D_MODEL), 1.0),
        'w_ada': nrm(ks[2], (DEPTH, D_MODEL, 6 * D_MODEL), 0.5 * D_MODEL ** -0.5),
        'b_ada': nrm(ks[3], (DEPTH, 6 * D_MODEL), 0.02),
        'norm_attn_g': 1.0 + nrm(ks[4], (DEPTH, D_MODEL), 0.05),
        'w_in': nrm(ks[5], (DEPTH, D_MODEL, IN_WIDTH), D_MODEL ** -0.5),
        'rel_bias': nrm(ks[6], (N_BUCKETS, N_ATTN_HEADS), 0.5),
        'conv_w': nrm(ks[7], (DEPTH, CONV_WIDTH, 3 * DELTA_WIDTH), CONV_WIDTH ** -0.5),
        'a_log': jnp.log(jax.random.uniform(ks[8], (DEPTH, N_DELTA_HEADS), f32, minval=1.0, maxval=16.0)),
        'dt_bias': dt + jnp.log(-jnp.expm1(-dt)),
        'delta_norm_g': 1.0 + nrm(ks[10], (DEPTH, HEAD_DIM), 0.05),
        'w_out': nrm(ks[11], (DEPTH, MIX_WIDTH, D_MODEL), MIX_WIDTH ** -0.5),
        'norm_ffn_g': 1.0 + nrm(ks[12], (DEPTH, D_MODEL), 0.05),
        'w_gate': nrm(ks[13], (DEPTH, D_MODEL, D_FF), D_MODEL ** -0.5),
        'w_up': nrm(ks[14], (DEPTH, D_MODEL, D_FF), D_MODEL ** -0.5),
        'w_down': nrm(ks[15], (DEPTH, D_FF, D_MODEL), D_FF ** -0.5),
        'final_norm_g': 1.0 + nrm(ks[16], (D_MODEL,), 0.05),
    }

def first_block(x, c, w_ada, b_ada, norm_attn_g, w_in, rel_bias, conv_w, a_log, dt_bias,
              delta_norm_g, w_out, norm_ffn_g, w_gate, w_up, w_down, final_norm_g):
    bsz, s, _ = x.shape
    split_points = np.cumsum([ATTN_WIDTH] * 3 + [DELTA_WIDTH] * 4 + [N_DELTA_HEADS])
    c_act = jax.nn.silu(c)
    for l in range(DEPTH):
        mod = c_act @ w_ada[l] + b_ada[l]
        sh1, sc1, g1, sh2, sc2, g2 = [m[:, None, :] for m in jnp.split(mod, 6, axis=-1)]
        h = _rmsnorm(x, norm_attn_g[l]) * (1.0 + sc1) + sh1
        proj = h @ w_in[l]
        q_a, k_a, v_a, q_d, k_d, v_d, z_d, b_d, a_d = jnp.split(proj, split_points, axis=-1)
        hs = (bsz, s, N_ATTN_HEADS, HEAD_DIM)
        y_attn = _dilated_attention(q_a.reshape(hs), k_a.reshape(hs), v_a.reshape(hs), rel_bias).astype(x.dtype)
        y_delta = _gated_deltanet(q_d, k_d, v_d, z_d, b_d, a_d, conv_w[l], a_log[l], dt_bias[l], delta_norm_g[l])
        y = jnp.concatenate([y_attn, y_delta], axis=-1) @ w_out[l]
        x = x + g1 * y
        h = _rmsnorm(x, norm_ffn_g[l]) * (1.0 + sc2) + sh2
        y = (jax.nn.silu(h @ w_gate[l]) * (h @ w_up[l])) @ w_down[l]
        x = x + g2 * y
    return _rmsnorm(x, final_norm_g)


DEPTH_2 = 2

A_HEADS = 4
A_DK = 128
A_DV = 128
A_WIDTH = A_HEADS * A_DV
B_HEADS = 4
B_DK = 64
B_DV = 128
B_QK = B_HEADS * B_DK
B_WIDTH = B_HEADS * B_DV
C_HEADS = 4
C_DK = 64
C_DV = 128
C_QK = C_HEADS * C_DK
C_WIDTH = C_HEADS * C_DV
GLA_RANK = 16
GLA_TAU = 16.0
N_BRANCH = 3
SPLIT_SIZES = (
    A_WIDTH, A_HEADS * A_DK, A_HEADS * A_DK, A_WIDTH, A_WIDTH,
    B_QK, B_QK, B_WIDTH, B_WIDTH,
    C_QK, C_QK, C_WIDTH, C_WIDTH,
    2 * GLA_RANK,
    D_MODEL, D_MODEL, D_MODEL,
)
N_IN = 5 * A_WIDTH + 2 * B_QK + 2 * B_WIDTH + 2 * C_QK + 2 * C_WIDTH + 2 * GLA_RANK + N_BRANCH * D_MODEL
D_FF_2 = ((8 * D_MODEL + 3 * 256 - 1) // (3 * 256)) * 256
ROPE_BASE = 10000.0
TINY = 1e-30


def rms_norm(x, gain):
    x32 = x.astype(jnp.float32)
    y = x32 * lax.rsqrt(jnp.mean(x32 * x32, axis=-1, keepdims=True) + EPS)
    return (y * gain.astype(jnp.float32)).astype(x.dtype)

def head_rms(o):
    return o * lax.rsqrt(jnp.mean(o * o, axis=-1, keepdims=True) + EPS)

def head_group_norm(o):
    mu = jnp.mean(o, axis=-1, keepdims=True)
    var = jnp.mean(jnp.square(o - mu), axis=-1, keepdims=True)
    return (o - mu) * lax.rsqrt(var + EPS)

def rotary(x):
    seqlen, d = x.shape[1], x.shape[-1]
    pos = jnp.arange(seqlen, dtype=jnp.float32)
    inv_freq = ROPE_BASE ** (-jnp.arange(0, d, 2, dtype=jnp.float32) / d)
    ang = pos[:, None] * inv_freq[None, :]
    cos = jnp.cos(ang)[None, :, None, :]
    sin = jnp.sin(ang)[None, :, None, :]
    x32 = x.astype(jnp.float32)
    x1, x2 = x32[..., : d // 2], x32[..., d // 2:]
    return jnp.concatenate([x1 * cos - x2 * sin, x1 * sin + x2 * cos], axis=-1).astype(x.dtype)

def chunked_gated_linear_attention(q, k, v, log_g, inclusive):
    bsz, seqlen, heads, dk = q.shape
    dv = v.shape[-1]
    n = seqlen // CHUNK

    def blocks(a):
        a = a.astype(jnp.float32).reshape(bsz, n, CHUNK, heads, a.shape[-1])
        return a.transpose(1, 0, 3, 2, 4)

    mask = jnp.tril(jnp.ones((CHUNK, CHUNK), dtype=bool), k=0 if inclusive else -1)[:, :, None]

    def step(state, inp):
        qb, kb, vb, gb = inp
        cum = jnp.cumsum(gb, axis=2)
        last = cum[:, :, -1:, :]
        diff = jnp.where(mask, cum[:, :, :, None, :] - cum[:, :, None, :, :], 0.0)
        rel = jnp.where(mask, jnp.exp(diff), 0.0)
        scores = jnp.einsum('bhid,bhjd,bhijd->bhij', qb, kb, rel)
        out = (jnp.einsum('bhij,bhjv->bhiv', scores, vb)
               + jnp.einsum('bhid,bhdv->bhiv', qb * jnp.exp(cum), state))
        state = (state * jnp.exp(last[:, :, 0, :, None])
                 + jnp.einsum('bhjd,bhjv->bhdv', kb * jnp.exp(last - cum), vb))
        return state, out

    init = jnp.zeros((bsz, heads, dk, dv), jnp.float32)
    _, out = lax.scan(step, init, (blocks(q), blocks(k), blocks(v), blocks(log_g)))
    return out.transpose(1, 0, 3, 2, 4).reshape(bsz, seqlen, heads, dv)

def bidirectional_scan(q, k_fwd, k_bwd, v, log_g_fwd, log_g_bwd):
    fwd = chunked_gated_linear_attention(q, k_fwd, v, log_g_fwd, True)
    flip = lambda a: jnp.flip(a, axis=1)
    bwd = flip(chunked_gated_linear_attention(flip(q), flip(k_bwd), flip(v), flip(log_g_bwd), False))
    return fwd + bwd

def retention_log_decay(reverse):
    h = jnp.arange(B_HEADS, dtype=jnp.float32)
    if reverse:
        h = h[::-1]
    return jnp.log1p(-jnp.exp2(-5.0 - h))

def hgrn2_lower_bounds(lb_logits):
    p = jax.nn.softmax(lb_logits.astype(jnp.float32), axis=0)
    return jnp.maximum(jnp.cumsum(p, axis=0) - p[0:1], 0.0)

def mixer_sublayer(h, lb, norm_a_g, norm_b_g, norm_c_g, w_in, w_alpha, b_alpha, w_pa, w_pb, w_pc, w_out):
    bsz, seqlen, _ = h.shape
    dt = h.dtype
    z = h @ w_in
    idx = np.cumsum(SPLIT_SIZES)[:-1]
    (a_q, a_ff, a_fb, a_i, a_g, b_q, b_k, b_v, b_g, c_q, c_k, c_v, c_g, c_lr,
     gate_a, gate_b, gate_c) = jnp.split(z, idx, axis=-1)
    heads = lambda t, n: t.reshape(bsz, seqlen, n, -1)

    lb32 = lb.astype(jnp.float32).reshape(A_HEADS, A_DK)
    def forget(zf):
        zf = heads(zf, A_HEADS).astype(jnp.float32)
        f = lb32 + (1.0 - lb32) * jax.nn.sigmoid(zf)
        log_f = jnp.log(jnp.maximum(f, TINY))
        key = (1.0 - lb32) * jax.nn.sigmoid(-zf)
        return log_f, key
    log_f_fwd, key_fwd = forget(a_ff)
    log_f_bwd, key_bwd = forget(a_fb)
    qa = heads(jax.nn.silu(a_q), A_HEADS)
    o_a = bidirectional_scan(qa, key_fwd, key_bwd, heads(a_i, A_HEADS), log_f_fwd, log_f_bwd)
    y_a = (head_rms(o_a).reshape(bsz, seqlen, A_WIDTH) * norm_a_g).astype(dt) * jax.nn.sigmoid(a_g)

    qb = rotary(heads(b_q, B_HEADS))
    kb = rotary(heads(b_k, B_HEADS)) * (B_DK ** -0.5)
    shape_b = (bsz, seqlen, B_HEADS, B_DK)
    lg_fwd = jnp.broadcast_to(retention_log_decay(False)[None, None, :, None], shape_b)
    lg_bwd = jnp.broadcast_to(retention_log_decay(True)[None, None, :, None], shape_b)
    o_b = bidirectional_scan(qb, kb, kb, heads(b_v, B_HEADS), lg_fwd, lg_bwd)
    y_b = (head_group_norm(o_b).reshape(bsz, seqlen, B_WIDTH) * norm_b_g).astype(dt) * jax.nn.silu(b_g)

    lr = c_lr.reshape(bsz, seqlen, 2, GLA_RANK)
    alpha_logits = jnp.einsum('btnr,nrk->btnk', lr, w_alpha) + b_alpha
    log_alpha = jax.nn.log_sigmoid(alpha_logits.astype(jnp.float32)) / GLA_TAU
    la_fwd = heads(log_alpha[:, :, 0], C_HEADS)
    la_bwd = heads(log_alpha[:, :, 1], C_HEADS)
    qc = heads(c_q, C_HEADS) * (C_DK ** -0.5)
    kc = heads(c_k, C_HEADS)
    o_c = bidirectional_scan(qc, kc, kc, heads(c_v, C_HEADS), la_fwd, la_bwd)
    y_c = (head_rms(o_c).reshape(bsz, seqlen, C_WIDTH) * norm_c_g).astype(dt) * jax.nn.silu(c_g)

    merged = (jax.nn.sigmoid(gate_a) * (y_a @ w_pa)
              + jax.nn.sigmoid(gate_b) * (y_b @ w_pb)
              + jax.nn.sigmoid(gate_c) * (y_c @ w_pc))
    return merged @ w_out

def second_inputs(seed: int = 0) -> dict:
    key = jax.random.key(seed)
    ks = jax.random.split(key, 24)
    f32 = jnp.float32
    nrm = lambda k, shape, scale: jax.random.normal(k, shape, f32) * scale
    gain = lambda k, shape: 1.0 + 0.01 * jax.random.normal(k, shape, f32)
    return {
        "x": jax.random.normal(ks[0], (BATCH, SEQ, D_MODEL), f32),
        "c": jax.random.normal(ks[1], (BATCH, D_MODEL), f32),
        "norm1_g": gain(ks[2], (DEPTH_2, D_MODEL)),
        "w_ada": nrm(ks[3], (DEPTH_2, D_MODEL, 6 * D_MODEL), D_MODEL ** -0.5),
        "b_ada": nrm(ks[4], (DEPTH_2, 6 * D_MODEL), 0.01),
        "w_in": nrm(ks[5], (DEPTH_2, D_MODEL, N_IN), D_MODEL ** -0.5),
        "lb_logits": nrm(ks[6], (DEPTH_2, A_HEADS * A_DK), 0.5),
        "norm_a_g": gain(ks[7], (DEPTH_2, A_WIDTH)),
        "norm_b_g": gain(ks[8], (DEPTH_2, B_WIDTH)),
        "norm_c_g": gain(ks[9], (DEPTH_2, C_WIDTH)),
        "w_alpha": nrm(ks[10], (DEPTH_2, 2, GLA_RANK, C_QK), GLA_RANK ** -0.5),
        "b_alpha": nrm(ks[11], (DEPTH_2, 2, C_QK), 0.1),
        "w_pa": nrm(ks[12], (DEPTH_2, A_WIDTH, D_MODEL), A_WIDTH ** -0.5),
        "w_pb": nrm(ks[13], (DEPTH_2, B_WIDTH, D_MODEL), B_WIDTH ** -0.5),
        "w_pc": nrm(ks[14], (DEPTH_2, C_WIDTH, D_MODEL), C_WIDTH ** -0.5),
        "w_out": nrm(ks[15], (DEPTH_2, D_MODEL, D_MODEL), D_MODEL ** -0.5),
        "norm2_g": gain(ks[16], (DEPTH_2, D_MODEL)),
        "w_ffn_in": nrm(ks[17], (DEPTH_2, D_MODEL, 2 * D_FF_2), D_MODEL ** -0.5),
        "w_ffn_out": nrm(ks[18], (DEPTH_2, D_FF_2, D_MODEL), D_FF_2 ** -0.5),
        "norm_f_g": gain(ks[19], (D_MODEL,)),
    }

def second_block(x, c, norm1_g, w_ada, b_ada, w_in, lb_logits, norm_a_g, norm_b_g, norm_c_g,
              w_alpha, b_alpha, w_pa, w_pb, w_pc, w_out, norm2_g, w_ffn_in, w_ffn_out, norm_f_g):
    lower_bounds = hgrn2_lower_bounds(lb_logits)
    c_act = jax.nn.silu(c)
    for l in range(DEPTH_2):
        mod = c_act @ w_ada[l] + b_ada[l]
        sh1, sc1, g1, sh2, sc2, g2 = [m[:, None, :] for m in jnp.split(mod, 6, axis=-1)]
        h = rms_norm(x, norm1_g[l]) * (1.0 + sc1) + sh1
        x = x + g1 * mixer_sublayer(h, lower_bounds[l], norm_a_g[l], norm_b_g[l], norm_c_g[l], w_in[l],
                                    w_alpha[l], b_alpha[l], w_pa[l], w_pb[l], w_pc[l], w_out[l])
        h2 = rms_norm(x, norm2_g[l]) * (1.0 + sc2) + sh2
        gate, up = jnp.split(h2 @ w_ffn_in[l], 2, axis=-1)
        x = x + g2 * ((jax.nn.silu(gate) * up) @ w_ffn_out[l])
    return rms_norm(x, norm_f_g)


_first_inputs = second_inputs


def second_inputs(seed=0):
    import zlib

    import numpy as np

    out = dict(_first_inputs(seed))
    spreads = {}
    factors = {'norm1_g': 4.961,
     'lb_logits': 40.41,
     'norm_a_g': 64.0,
     'norm_b_g': 31.465,
     'norm_c_g': 28.783,
     'norm2_g': 16.697,
     'norm_f_g': 31.409}
    for name, (base, spread) in spreads.items():
        noise = np.random.default_rng([zlib.crc32(name.encode()), seed]).standard_normal(out[name].shape)
        drawn = base * np.exp(spread * noise) if base else spread * noise
        out[name] = __import__('jax').numpy.asarray(drawn.astype(out[name].dtype))
    for name, factor in factors.items():
        out[name] = (out[name] * factor).astype(out[name].dtype)
    return out


_narrow_inputs = second_inputs


def second_inputs(seed=0):
    out = dict(_narrow_inputs(seed))
    wider = {'lb_logits': 3.29, 'norm_a_g': 12.0, 'norm_b_g': 4.6, 'norm_c_g': 4.56, 'norm_f_g': 6.39}
    for name, times in wider.items():
        mean = out[name].mean()
        out[name] = (mean + times * (out[name] - mean)).astype(out[name].dtype)
    return out


def setup_inputs(seed=0):
    out = dict(first_inputs(seed))
    for name, value in second_inputs(seed + 1).items():
        if name != "x":
            out[name + "_2"] = value
    return out


def reference(
    x, c, w_ada, b_ada, norm_attn_g, w_in, rel_bias, conv_w, a_log, dt_bias, delta_norm_g,
    w_out, norm_ffn_g, w_gate, w_up, w_down, final_norm_g, c_2, norm1_g_2, w_ada_2, b_ada_2,
    w_in_2, lb_logits_2, norm_a_g_2, norm_b_g_2, norm_c_g_2, w_alpha_2, b_alpha_2, w_pa_2,
    w_pb_2, w_pc_2, w_out_2, norm2_g_2, w_ffn_in_2, w_ffn_out_2, norm_f_g_2,
):
    x = first_block(
        x, c, w_ada, b_ada, norm_attn_g, w_in, rel_bias, conv_w, a_log, dt_bias, delta_norm_g,
        w_out, norm_ffn_g, w_gate, w_up, w_down, final_norm_g,
    )
    return second_block(
        x, c_2, norm1_g_2, w_ada_2, b_ada_2, w_in_2, lb_logits_2, norm_a_g_2, norm_b_g_2,
        norm_c_g_2, w_alpha_2, b_alpha_2, w_pa_2, w_pb_2, w_pc_2, w_out_2, norm2_g_2,
        w_ffn_in_2, w_ffn_out_2, norm_f_g_2,
    )


_drawn_inputs = setup_inputs


def setup_inputs(seed=0):
    import zlib

    import numpy as np

    out = dict(_drawn_inputs(seed))
    spreads = {}
    factors = {}
    for name, (base, spread) in spreads.items():
        noise = np.random.default_rng([zlib.crc32(name.encode()), seed]).standard_normal(out[name].shape)
        drawn = base * np.exp(spread * noise) if base else spread * noise
        out[name] = __import__('jax').numpy.asarray(drawn.astype(out[name].dtype))
    for name, factor in factors.items():
        out[name] = (out[name] * factor).astype(out[name].dtype)
    return out
```

```python
import math
from contextlib import ExitStack

import numpy as np

import concourse.bass as bass
from concourse import mybir

F32 = mybir.dt.float32
F32R = mybir.dt.float32r
U8 = mybir.dt.uint8
ALU = mybir.AluOpType
ACT = mybir.ActivationFunctionType

P = 128
S = 512
D = 1024
KD = D // P
NT = S // P
FF = 2816
KF = FF // P
CW = 256
UNITS = 8
SLOT = UNITS * CW
ADA_COLS = 1024
LAYERS2 = 2
EPS = 1e-6
NEG = -1e30
TINY = 1e-30
TOEP = P + S
RAW = 3
KB = 1024 // 4

PARAM = {}


def _param_columns():
    at = 0
    for name, n in (("c", 24), ("b_ada", 144), ("g_attn", 8), ("g_ffn", 8), ("g_final", 8), ("g1", 16),
                    ("g2", 16), ("g_out", 8), ("conv", 48), ("lb", 8), ("norm", 24), ("b_alpha", 8),
                    ("delta_g", 1), ("a_log", 8), ("dt_bias", 8)):
        PARAM[name] = (at, n)
        at += n
    return at


NPARAM = _param_columns()

IN1 = ["qa", "qa", "ka", "ka", "va", "va"] + ["conv"] * 6 + ["zd", "zd"]


def plan():
    steps, filled = [], {}
    ada = [(layer, g, c) for layer in range(3) for g in range(6) for c in range(4)]
    pending = []

    def ada_chunk():
        if pending:
            steps.append(("mod",) + pending.pop())
        if ada:
            layer, g, c = ada.pop(0)
            steps.append(("ada", layer, g, c))
            if c == 3:
                pending.append((layer, g))

    def job(kind, layer, i, every=2):
        steps.append(("job", kind, layer, i))
        whole = kind != "down" or i % 3 == 2
        if whole and (kind == "down" or sum(x[0] == "job" for x in steps) % every == 0):
            ada_chunk()

    def mix(kind, layer, i, fill=()):
        start = len(steps)
        for k, c in fill:
            steps.append(("job", k, layer, c))
        filled[("mix", kind, layer, i)] = list(range(start, len(steps)))
        steps.append(("mix", kind, layer, i))

    def ffn(layer):
        for f in range(11):
            job("gate", layer, f)
            job("up", layer, f)
        for c in range(4):
            for part in range(3):
                job("down", layer, 3 * c + part)

    for _ in range(8):
        ada_chunk()
    steps.append(("mod",) + pending.pop())
    steps.append(("norm", 0))
    for i, kind in enumerate(IN1):
        job(kind, 0, i, every=1)
        if kind == "conv":
            steps.append(("conv", i - 6))
    job("ba", 0, 0)
    for h in range(9):
        steps.append(("attn", h))
    steps.append(("delta",))
    for c in range(4):
        job("wout", 0, c)
    steps.append(("norm", 1))
    ffn(0)
    steps.append(("norm", "renorm"))
    for L in range(1, LAYERS2 + 1):
        steps.append(("norm", 2 * L))
        for kind in ("aqf", "abg", "av"):
            job(kind, L, 0)
        mix("a", L, 0, (("aqf", 1), ("abg", 1)))
        mix("a", L, 1, (("aqf", 2), ("abg", 2), ("av", 1)))
        mix("a", L, 2, (("aqf", 3), ("abg", 3)))
        mix("a", L, 3, (("ga", 0), ("ga", 1), ("ga", 2), ("ga", 3)))
        for c in range(4):
            job("pa", L, c)
        for kind in ("bq", "bk", "bv", "bg"):
            job(kind, L, 0)
        steps.append(("rotary", L))
        for h, fill in enumerate((("bv", 1), ("bg", 1), ("gb", 0), ("gb", 1))):
            mix("b", L, h, (fill,))
        for kind, c in (("pb", 0), ("pb", 1), ("cq", 0), ("ck", 0), ("cl", 0), ("cv", 0), ("cg", 0)):
            job(kind, L, c)
        mix("c", L, 0, (("gb", 2), ("pb", 2), ("gb", 3), ("pb", 3), ("cv", 1)))
        job("cg", L, 1)
        mix("c", L, 1, (("gc", 0), ("gc", 1), ("gc", 2)))
        for kind, c in (("pc", 0), ("pc", 1), ("pc", 2), ("gc", 3), ("pc", 3)):
            job(kind, L, c)
        steps.append(("merge", L))
        for c in range(4):
            job("wout", L, c)
        steps.append(("norm", 1 + 2 * L))
        ffn(L)
    assert not ada and not pending
    steps.append(("norm", "final"))
    return steps, filled


SLOTS = {"a": 11, "b": 6, "c": 10}
PARTS = 4


SPLIT2 = {"aq": 0, "af": 512, "ab": 1024, "av": 1536, "ag": 2048, "bq": 2560, "bk": 2816, "bv": 3072,
          "bg": 3584, "cq": 4096, "ck": 4352, "cv": 4608, "cg": 5120, "cl": 5632, "ga": 5664, "gb": 6688,
          "gc": 7712}
GATE_AT = {"a": [38, 40, 42, 44, 46, 48, 50, 52], "b": [38, 42, 54, 56, 32, 34, 32, 34],
           "c": [48, 50, 38, 42, 46, 88, 32, 34]}
TOKEN_MAJOR = {"va", "ba", "av", "bv", "cv"}


def source(kind, layer, i):
    w = "" if layer == 0 else "_2"
    l2 = max(layer - 1, 0)
    if kind in ("qa", "ka", "va", "conv", "zd"):
        return "w_in", 0, 0, 8, (CW * i,), CW
    if kind == "ba":
        return "w_in", 0, 0, 8, (CW * len(IN1),), 16
    if kind == "cl":
        return "w_in_2", l2, 0, 8, (SPLIT2["cl"],), 32
    if kind in ("aqf", "abg"):
        return "w_in_2", l2, 0, 8, tuple(SPLIT2["a" + x] + P * i for x in kind[1:]), CW
    if kind in SPLIT2:
        return "w_in_2", l2, 0, 8, (SPLIT2[kind] + CW * i,), CW
    if kind in ("pa", "pb", "pc"):
        return f"w_{kind}_2", l2, 0, 4, (CW * i,), CW
    if kind == "wout":
        return "w_out" + w, l2, 0, 8, (CW * i,), CW
    if kind in ("gate", "up"):
        if layer == 0:
            return "w_" + kind, 0, 0, 8, (CW * i,), CW
        return "w_ffn_in_2", l2, 0, 8, (CW * i + (FF if kind == "up" else 0),), CW
    c, part = divmod(i, 3)
    return ("w_down" if layer == 0 else "w_ffn_out_2"), l2, 1024 * part, (8, 8, 6)[part], (CW * c,), CW


class Job:
    w = None


def jobs_of(steps):
    by_step, freed = {}, []
    w = bank = ada = 0
    act = dve = 0
    for n, s in enumerate(steps):
        if s[0] not in ("job", "ada", "mod"):
            continue
        j = Job()
        by_step[n] = j
        if s[0] == "mod":
            j.kind, j.bank = "mod", bank
            bank += 1
            dve += 1
            freed.append(("dve", dve))
            j.dve = dve
            continue
        if s[0] == "ada":
            j.kind, j.size = "ada", SLOT
            j.src = ("ada",) + s[1:]
            j.ada = ada
            ada += 1
            continue
        _, kind, layer, i = s
        j.kind, j.layer, j.i = kind, layer, i
        j.src = source(kind, layer, i)
        j.units, j.width = j.src[3], j.src[5]
        j.size, j.w = j.units * j.width, w
        w += 1
        j.first = kind != "down" or i % 3 == 0
        j.last = kind != "down" or i % 3 == 2
        j.bank = bank
        j.act0, j.dve0 = act, dve
        if j.last:
            bank += 1
            if kind in ("up", "pa", "pb", "pc", "wout", "down"):
                dve += 2
                freed.append(("dve", dve))
            else:
                act += {"aqf": 3, "abg": 3, "ba": 1, "cl": 1}.get(kind, 2)
                freed.append(("act", act))
        j.act, j.dve = act, dve
    products = [j for j in by_step.values() if j.w is not None]
    loads, at = [], 0
    for n, s in enumerate(steps):
        if s[0] == "ada":
            loads.append(by_step[n])
        elif s == ("norm", 0):
            loads.append(products[0])
        elif s[0] == "job" and by_step[n].w + 1 < len(products):
            loads.append(products[by_step[n].w + 1])
    for li, j in enumerate(loads):
        j.load, j.at = li, at
        at += j.size
    return loads, by_step, products, freed, at


STEPS, FILLED = plan()
EMBEDDED = {n for x in FILLED.values() for n in x}
LOADS, JOBS, PRODUCTS, FREED, WTOTAL = jobs_of(STEPS)


CONST = {}


def constants():
    p = np.arange(P)
    blocks = {"ident": np.eye(P), "blockones": (p[:, None] // 64 == p[None] // 64),
              "upto": (p[:, None] <= p[None])}
    perm = np.zeros((P, P))
    for d in range(P):
        if d % 64 < 32:
            perm[d + 32, d] = -1.0
        else:
            perm[d - 32, d] = 1.0
    blocks["perm"] = perm
    inv = (10000.0 ** (-np.arange(0, 64, 2, dtype=np.float32) / np.float32(64))).astype(np.float32)
    ang = (np.arange(S, dtype=np.float32)[None] * inv[:, None]).astype(np.float32).astype(np.float64)
    blocks["cos"] = np.cos(ang)[p % 32]
    blocks["sin"] = np.sin(ang)[p % 32]
    gamma = np.zeros((P, 4, 896))
    dist = np.arange(896)[None] - p[:, None] - 384
    for h in range(4):
        fwd, bwd = (math.log1p(-2.0 ** (-5.0 - x)) for x in (h, 3 - h))
        gamma[:, h] = np.exp(np.where(dist >= 0, fwd * dist, -bwd * dist))
    blocks["gamma"] = gamma.reshape(P, -1)
    onehot = np.zeros((P, TOEP))
    for x in range(TOEP):
        dd = 511 - x
        n = (dd <= 128) + (dd % 4 == 0) + (dd % 16 == 0) if dd >= 0 else 0
        if n:
            b = dd if dd < 16 else min(31, 16 + int(np.float32(np.log(np.float32(dd / 16))) / np.float32(
                math.log(128)) * np.float32(16)))
            onehot[b, x] = 1.0
            onehot[32, x] = math.log(n)
        else:
            onehot[32, x] = NEG
    blocks["onehot"] = onehot
    masks = np.zeros((P, 7, P))
    r, c = p[:, None], p[None]
    for l in range(7):
        b = 2 ** l
        masks[:, l] = (r // (2 * b) == c // (2 * b)) & (r // b != c // b)
    blocks["sibling"] = masks.reshape(P, -1)
    blocks["before"] = (masks * (r < c)[:, None]).reshape(P, -1)
    at = 0
    for k, v in blocks.items():
        CONST[k] = (at, v.shape[1])
        at += v.shape[1]
    return np.concatenate([v.astype(np.float32) for v in blocks.values()], 1)


CONST_ARRAY = constants()


def program(nc, wstream, x_in, params_in, relb_in, walpha_in, const_in, out):
    ctx = ExitStack()
    with ctx:
        def sem(name):
            return ctx.enter_context(nc.semaphore(name))

        base = [16512]

        def sb(name, shape, dt=F32):
            t = nc.alloc_sbuf_tensor_at(name, [P] + list(shape), dt, offset=base[0])
            n = int(np.prod(shape)) * (1 if dt == U8 else 4)
            base[0] += (n + 31) // 32 * 32
            return t

        xT = sb("xT", [KD, S])
        HH = sb("HH", [KD, S], F32R)
        HL = sb("HL", [KD, S], F32R)
        raw = sb("raw", [RAW, SLOT])
        WH = sb("WH", [2, SLOT], F32R)
        WL = sb("WL", [2, SLOT], F32R)
        ada_acc = sb("ada_acc", [ADA_COLS])
        params = sb("params", [NPARAM])
        ident = sb("ident", [P])
        ones = sb("ones", [P])
        masks = sb("masks", [7, P], U8)
        mod = sb("mod", [3, 6, KD])
        lbound = sb("lbound", [2, 4])
        rest = sb("rest", [2, 4])
        cact = sb("cact", [24])
        acol = sb("acol", [KD])
        eps = sb("eps", [1])
        small = sb("small", [8, 4])
        ARENA = base[0]

        def arena(name, kb, shape, dt=F32):
            off = ARENA + int(round(kb * 1024))
            assert off % 32 == 0
            assert off + int(np.prod(shape)) * 4 <= 229344, (name, off, ARENA)
            return nc.alloc_sbuf_tensor_at(name, [P] + list(shape), dt, offset=off)

        CVP = S + 3
        relb = arena("relb", 0, [8, P])
        onehot = arena("onehot", 4, [TOEP])
        bias_row = arena("bias_row", 8, [2, TOEP])
        zs = arena("zs", 0, [4, S])
        cvb = arena("cvb", 8, [2, 2, CVP])
        CO = arena("CO", 16.25, [12, S])
        sibling = arena("sibling", 16.25, [7, P])
        qa = arena("qa", 40.25, [4, S])
        ka = arena("ka", 48.25, [4, S])
        va = arena("va", 56.25, [NT, S])
        toep = arena("toep", 64.25, [3, S])
        Sx = arena("Sx", 70.25, [2, 1280])
        PT = arena("PT", 80.25, [2, 1280])
        ba = arena("ba", 90.25, [NT, 16])
        amax = arena("amax", 90.5, [2, 4])
        anmax = arena("anmax", 90.5625, [2, 4])
        asum = arena("asum", 90.625, [2, 4])
        arsum = arena("arsum", 90.6875, [2, 4])
        blockones = arena("blockones", 92, [P])
        upto = arena("upto", 92.5, [P])
        dcol = arena("dcol", 93, [12, 32])
        before03 = arena("before03", 76.25, [4, P])
        before46 = arena("before46", 90.25, [3, P])
        ktok = arena("ktok", 40.25, [NT, S])
        vtok = arena("vtok", 48.25, [NT, S])
        dset = []
        for e in range(2):
            names = ["ER", "ET", "kbT", "AT", "QKT", "Dm", "DT", "X", "MT"]
            where = [56.25 + 2 * i for i in range(9)] if e == 0 else \
                [8 + 2 * i for i in range(4)] + [78.25 + 2 * i for i in range(5)]
            d = {n: arena(f"{n}{e}", w, [S]) for n, w in zip(names, where)}
            w0 = 74.25 if e == 0 else 88.25
            d["kbe"] = arena(f"kbe{e}", w0, [NT, 64])
            d["kdec"] = arena(f"kdec{e}", w0 + 1, [NT, 64])
            dset.append(d)
        YH = arena("YH", 0, [4, S], F32R)
        YL = arena("YL", 8, [4, S], F32R)
        macc = arena("macc", 16, [KD, S])
        sqt = arena("sqt", 32, [S])
        rrt = arena("rrt", 34, [S])
        ttt = arena("ttt", 36, [S])
        agate = arena("agate", 16, [4, S])
        aslot = []
        for e in range(2):
            o = 38 + 28 * e
            aslot.append({n: arena(f"a_{n}{e}", o + w, sh) for n, w, sh in (
                ("q", 0, [S]), ("QQ", 2, [2, S]), ("KK", 6, [2, S]), ("G1", 10, [2, S]), ("GT", 14, [1024]),
                ("ST", 18, [NT, S]))})
        avb = [arena(f"av{x}", 24 + 4 * x, [NT, CW]) for x in range(2)]
        bq = arena("bq", 38, [2, S])
        bk = arena("bk", 42, [2, S])
        bv = arena("bv", 46, [NT, S])
        bg = arena("bg", 54, [4, S])
        bgam = arena("bgam", 62, [4, 896])
        bST = [arena(f"bST{e}", 76.25 + 8 * e, [NT, S]) for e in range(2)]
        brot = arena("brot", 76.25, [2 * S + P])
        btmp = arena("btmp", 84.25, [S])
        cq = arena("cq", 38, [2, S])
        ck = arena("ck", 42, [2, S])
        clr = arena("clr", 46, [S])
        cvb2 = [arena("cv0", 48, [NT, CW]), arena("cv1", 90, [NT, CW])]
        cg = arena("cg", 52, [2, S])
        cG1 = arena("cG1", 56, [2, S])
        cQQ = arena("cQQ", 60, [2, S])
        cKK = arena("cKK", 64, [2, S])
        cGT = arena("cGT", 68, [1024])
        cST = [arena(f"cST{e}", 72 + 8 * e, [NT, S]) for e in range(2)]
        aw = arena("aw", 88, [2, CW])
        c_x = arena("c_x", 72, [2, S])
        c_e = arena("c_e", 80, [2, S])
        gate_at = {kb: arena(f"gate_at_{kb}", kb, [S]) for kb in sorted({x for v in GATE_AT.values() for x in v})}
        AH = arena("AH", 0, [KF, S], F32R)
        AL = arena("AL", 44, [KF, S], F32R)
        SG = arena("SG", 88, [2, S])
        nsq = arena("nsq", 88, [2, S])
        nr = arena("nr", 80, [S])
        nt = arena("nt", 82, [2, S])
        ost = arena("ost", 0, [KD, S])

        bank = [ctx.enter_context(nc.psum_tensor(f"bank{i}", [P, 512], F32)) for i in range(8)]
        bias_dram = nc.dram_tensor("bias_dram", [8, P, TOEP], F32).ap()

        names = """const_in before_in ones_set raw0 raw1 raw2 w_rounded w_split gemm_done ada_mac ada_start
            mod_ready act_evac dve_evac cact_ready lb_max lb_exp lb_dve bias_ps bias_rows bias_stored toep0 toep1 toep2
            n_square n_sum n_ln n_rstd n_acol n_scaled n_high n_low renormed out_ready out_stored
            conv_pad conv_step conv_silu
            a_scores a_biased a_nmax a_exp a_rsum a_norm a_turned a_turn_copied a_out a_high a_low
            f_act f_high f_low
            dn_sq dn_sum dn_ln dn_r dn_scaled dt_turn dt_copy dg_act dg_pool dg_ps dg_cum dg_cols
            d_rows d_er d_et d_etexp d_etmask d_kb d_kk d_at d_qk d_m d_dt0 d_tr d_dm0 d_x d_xc d_y d_upd
            d_tok d_qe d_uw d_uwc d_ws d_vn d_sp d_sn d_o df_sq df_sum df_ln df_r df_t df_y df_high df_low
            prep lanes levels decayed scores_put scores_copied mixed
            h_sq h_sum h_ln h_r h_t h_y h_high h_low h_cp h_mean h_cent
            r_in r_rot r_ps r_t b_scores b_decay_in
            c_in c_logit c_act c_dve c_lanes c_kcopy
            m_gate m_mul m_add m_high m_low""".split()
        s = {n: sem(n) for n in names}
        raw_in = [s["raw0"], s["raw1"], s["raw2"]]
        toep_in = [s["toep0"], s["toep1"], s["toep2"]]

        def par(name, i=0, n=1):
            a = PARAM[name][0]
            return params[:, a + i:a + i + n]

        def bc(ap, *dims):
            return bass.AP(ap.tensor, ap.offset, [list(ap.ap[0])] + [list(d) for d in dims])

        def lanes(t, b):
            return bc(t[:, :, :], [2 * b, S // (2 * b)], [S + b, 2], [1, b])

        def lane_gates(g1, gt, b, keys):
            n = S // b
            g = g1[:, :, :] if b == 1 else gt[:, :]
            at = 0 if b == 1 else tree_at(b)
            off, step = (n + 1, -(n + 1)) if keys else (1, n - 1)
            return bass.AP(g.tensor, g.offset + at + off, [list(g.ap[0]), [2, n // 2], [step, 2], [0, b]])

        def tree_at(b):
            return sum(2 * (S // x) for x in (2, 4, 8, 16, 32, 64, 128) if x < b)

        def tree_step(g1, gt, b):
            n = S // b
            g = g1[:, :, :] if b == 1 else gt[:, :]
            at = 0 if b == 1 else tree_at(b)
            src = [bass.AP(g.tensor, g.offset + at + x, [list(g.ap[0]), [n, 2], [2, n // 2]]) for x in (0, 1)]
            t = gt[:, :]
            dst = bass.AP(t.tensor, t.offset + tree_at(2 * b), [list(t.ap[0]), [n // 2, 2], [1, n // 2]])
            return dst, src[0], src[1]

        units, heads = {}, {}
        nu = nh = 0
        for st in STEPS:
            if st[0] == "mix":
                kind, layer, i = st[1:]
                k = 2 if kind == "c" else 1
                if kind != "b":
                    units[st] = nu
                    nu += 1
                heads[st] = nh
                nh += k
        scan_before, b_before = {}, {}
        ns = nb = 0
        for st in STEPS:
            if st[0] == "mix":
                scan_before[st] = ns
                b_before[st] = nb
                if st[1] == "b":
                    nb += 1
                else:
                    ns += 2 if st[1] == "c" else 1

        def heads_done(n):
            return sum((2 if x[1] == "c" else 1) for x in STEPS[:n] if x[0] == "mix")

        def adds_before(n):
            return sum(2 for x in STEPS[:n] if x[0] == "job" and x[1] in ("pa", "pb", "pc"))

        def gemm_before(n):
            return sum(1 for x in STEPS[:n] if x[0] == "job")

        NORM_MOD = [(0, 0), (0, 3), None, (1, 0), (1, 3), (2, 0), (2, 3), None]
        NORM_G = [("g_attn", 0), ("g_ffn", 0), ("g_final", 0), ("g1", 0), ("g2", 0), ("g1", 8), ("g2", 8),
                  ("g_out", 0)]
        RENORM, FINAL = 2, 7

        def modulated(r):
            return r - (r > RENORM)

        def ffns(r):
            return (0, 0, 1, 1, 1, 2, 2, 3)[r]


        def tile_count(n, k):
            js = [JOBS[m] for m in range(n) if m in JOBS and JOBS[m].kind in ("wout", "down")
                  and JOBS[m].last][-4:]
            if not js:
                return 0
            return js[k // 2].dve - 1 + k % 2

        def mods_before(n):
            return sum(1 for x in STEPS[:n] if x[0] == "mod")

        def mod_ready_count(layer, group):
            for m, x in enumerate(STEPS):
                if x[:3] == ("mod", layer, group):
                    return JOBS[m].dve
            raise KeyError

        def parts(st, slot):
            jobs, slots = FILLED[st], SLOTS[st[1]]
            total = PARTS * len(jobs)
            if slot < 0 or slot >= slots:
                return []
            return [(jobs[x // PARTS], x % PARTS) for x in range(total * slot // slots, total * (slot + 1) // slots)]

        def evacuated(*job):
            return JOBS[STEPS.index(("job",) + job)].act

        NCONST = 8
        block = ctx.enter_context(nc.Block())

        @block.sync
        def _(sp):
            def const(name, dst):
                a, n = CONST[name]
                return dst, const_in[:, a:a + n]

            sp.dma_start(params[:, :], params_in).then_inc(s["const_in"], 16)

            def load(li):
                j = LOADS[li]
                if li >= RAW:
                    o = LOADS[li - RAW]
                    if o.kind == "ada":
                        sp.wait_ge(s["ada_mac"], 2 * (o.ada + 1))
                    else:
                        sp.wait_ge(s["w_split"], o.w + 1)
                sp.dma_start(raw[:, li % RAW, 0:j.size],
                             wstream[j.at * P:(j.at + j.size) * P].rearrange("(p n) -> p n", p=P)
                             ).then_inc(raw_in[li % RAW], 16)

            nxt = 0
            for _ in range(RAW):
                load(nxt)
                nxt += 1
            sp.dma_start(xT[:, :, :], x_in).then_inc(s["const_in"], 16)
            for dst, src in (const("ident", ident[:, :]), const("sibling", sibling[:, :, :].rearrange("p l j -> p (l j)")),
                             (relb[0:33, :, :], relb_in),
                             const("onehot", onehot[:, :]), const("blockones", blockones[:, :]),
                             const("upto", upto[:, :])):
                sp.dma_start(dst, src).then_inc(s["const_in"], 16)
            while nxt < len(LOADS):
                load(nxt)
                nxt += 1
            sp.wait_ge(s["out_ready"], 8)
            sp.dma_start(out, ost[:, :, :]).then_inc(s["out_stored"], 16)
            sp.wait_ge(s["out_stored"], 16)

        @block.gpsimd
        def _(pool):
            pool.memset(ones[:, :], 1.0).then_inc(s["ones_set"], 1)
            pool.memset(eps[:, :], EPS).then_inc(s["ones_set"], 1)
            pool.wait_ge(s["const_in"], 16 * NCONST)
            pool.tensor_copy(masks[:, :, :], sibling[:, :, :]).then_inc(s["ones_set"], 1)
            for h in range(8):
                pool.wait_ge(s["bias_rows"], 2 * (h + 1))
                pool.dma_start(bias_dram[h], bias_row[:, h % 2, :]).then_inc(s["bias_stored"], 16)
                pool.wait_ge(s["bias_stored"], 16 * (h + 1))

            def toeplitz(h):
                if h >= 3:
                    pool.wait_ge(s["a_biased"], 4 * (h - 2))
                skew = bass.AP(bias_dram.tensor, bias_dram.offset + h * P * TOEP + P - 1,
                               [[TOEP - 1, P], [1, S]])
                pool.dma_start(toep[:, h % 3, :], skew).then_inc(s[f"toep{h % 3}"], 16)

            def lane_products(u, st, g1, gt, q, QQ):
                pool.tensor_tensor(QQ[:, :, :], bc(q, [0, 2], [1, S]), g1[:, :, :], ALU.mult
                                   ).then_inc(s["lanes"], 1)
                b = 1
                for k in range(7):
                    if k:
                        pool.wait_ge(s["lanes"], 8 * u + 1 + k)
                    dst, i0, i1 = tree_step(g1, gt, b)
                    pool.tensor_tensor(dst, i0, i1, ALU.mult).then_inc(s["lanes"], 1)
                    b *= 2

            for n, st in enumerate(STEPS):
                if st[0] == "conv" and st[1] == 0:
                    for h in range(3):
                        toeplitz(h)
                if st[:2] == ("job", "bq"):
                    pool.wait_ge(s["mixed"], heads_done(n))
                    pool.wait_ge(s["h_low"], heads_done(n))
                    for name, dst in (("gamma", bgam[:, :, :].rearrange("p h u -> p (h u)")),
                                      ("cos", brot[:, 0:S]), ("sin", brot[:, S:2 * S]),
                                      ("perm", brot[:, 2 * S:2 * S + P])):
                        a, c = CONST[name]
                        pool.dma_start(dst, const_in[:, a:a + c]).then_inc(s["r_in"], 16)
                if st[:2] == ("job", "cq"):
                    pool.wait_ge(s["mixed"], heads_done(n))
                    pool.wait_ge(s["h_low"], heads_done(n))
                    pool.dma_start(aw[0:32, :, :], walpha_in[st[2] - 1]).then_inc(s["c_in"], 16)
                if st[0] == "attn" and st[1] < 8:
                    h = st[1]
                    if h >= 1 and h + 2 < 8:
                        toeplitz(h + 2)
                if st[0] == "delta":
                    a, c = CONST["before"]
                    pool.wait_ge(s["a_turned"], 8)
                    pool.wait_ge(s["dg_act"], 1)
                    pool.wait_ge(s["dg_pool"], 1)
                    pool.dma_start(before03[:, :, :].rearrange("p l j -> p (l j)"), const_in[:, a:a + 4 * P]
                                   ).then_inc(s["before_in"], 16)
                    pool.dma_start(before46[:, :, :].rearrange("p l j -> p (l j)"), const_in[:, a + 4 * P:a + 7 * P]
                                   ).then_inc(s["before_in"], 16)
                    pool.wait_ge(s["before_in"], 32)
                    for p in range(4):
                        for e in range(2):
                            h, d = 2 * p + e, dset[e]
                            pool.wait_ge(s["d_etexp"], h + 1)
                            pool.tensor_tensor(d["ET"][:, :].rearrange("p (n i) -> p n i", n=4),
                                               d["ET"][:, :].rearrange("p (n i) -> p n i", n=4),
                                               bc(upto[:, :], [0, 4], [1, P]), ALU.mult
                                               ).then_inc(s["d_etmask"], 1)
                        for l in range(7):
                            for e in range(2):
                                h, d = 2 * p + e, dset[e]
                                pool.wait_ge(s["d_at"], h + 1)
                                if l == 1:
                                    pool.wait_ge(s["d_dt0"], h + 1)
                                elif l > 1:
                                    pool.wait_ge(s["d_x"], 12 * p + 2 * (l - 2) + e + 1)
                                pool.tensor_tensor(d["MT"][:, :].rearrange("p (n i) -> p n i", n=4),
                                                   d["AT"][:, :].rearrange("p (n i) -> p n i", n=4),
                                                   bc((before03[:, l, :] if l < 4 else before46[:, l - 4, :]), [0, 4],
                                                      [1, P]), ALU.mult
                                                   ).then_inc(s["d_m"], 1)
                if st[0] == "mix" and st[1] == "a":
                    layer, h = st[2:]
                    u, a = units[st], aslot[h % 2]
                    up = sum(1 for x in STEPS[:n] if x[0] == "mix" and x[1] == "a")
                    pool.wait_ge(s["act_evac"], evacuated("abg", layer, h))
                    pool.wait_ge(s["lb_dve"], 10)
                    lo, om = (t[:, layer - 1, h:h + 1] for t in (lbound, rest))
                    pool.tensor_scalar(a["G1"][:, :, :], a["G1"][:, :, :], om, lo, ALU.mult, ALU.add
                                       ).then_inc(s["prep"], 1)
                    pool.tensor_scalar(a["KK"][:, :, :], a["KK"][:, :, :], om, None, ALU.mult
                                       ).then_inc(s["prep"], 1)
                    pool.wait_ge(s["prep"], 3 * up + 1)
                    pool.tensor_scalar(a["G1"][:, :, :], a["G1"][:, :, :], TINY, None, ALU.max
                                       ).then_inc(s["prep"], 1)
                    pool.wait_ge(s["prep"], 3 * up + 3)
                    lane_products(u, st, a["G1"], a["GT"], a["q"][:, :], a["QQ"])
                if st[0] == "mix" and st[1] == "c":
                    layer, pr = st[2:]
                    u = units[st]
                    cu = 2 * (layer - 1) + pr
                    pool.wait_ge(s["c_lanes"], 2 * cu + 2)
                    lane_products(u, st, cG1, cGT, cq[:, pr, :], cQQ)

        @block.scalar
        def _(act):
            A = act.activation

            def split(wi):
                j = PRODUCTS[wi]
                act.wait_ge(raw_in[j.load % RAW], 16 * (j.load // RAW + 1))
                if wi > 1:
                    act.wait_ge(s["gemm_done"], wi - 1)
                A(WH[:, wi % 2, 0:j.size], raw[:, j.load % RAW, 0:j.size], ACT.Copy).then_inc(s["w_rounded"], 1)

            act.wait_ge(s["const_in"], 16 * NCONST)
            act.wait_ge(s["ones_set"], 2)
            A(cact[:, :], par("c", 0, 24), ACT.Silu).then_inc(s["cact_ready"], 1)
            act.wait_ge(s["lb_dve"], 2)
            A(small[:, 2:4, :], small[:, 0:2, :], ACT.Exp).then_inc(s["lb_exp"], 1)
            for h in range(8):
                act.wait_ge(s["bias_ps"], h + 1)
                if h >= 2:
                    act.wait_ge(s["bias_stored"], 16 * (h - 1))
                A(bias_row[:, h % 2, 0:512], bank[4 + 2 * (h % 2)][:, :], ACT.Copy).then_inc(s["bias_rows"], 1)
                A(bias_row[:, h % 2, 512:TOEP], bank[5 + 2 * (h % 2)][:, 0:P], ACT.Copy
                  ).then_inc(s["bias_rows"], 1)

            def norm(n, r):
                for k in range(KD):
                    if tile_count(n, k) > 0:
                        act.wait_ge(s["dve_evac"], tile_count(n, k))
                    if r == RENORM + 1:
                        act.wait_ge(s["renormed"], k + 1)
                    if k >= 2:
                        act.wait_ge(s["n_sum"], 8 * r + k - 1)
                    elif r:
                        if ffns(r):
                            act.wait_ge(s["f_low"], 22 * ffns(r))
                    A(nsq[:, k % 2, :], xT[:, k, :], ACT.Square).then_inc(s["n_square"], 1)
                act.wait_ge(s["n_sum"], 8 * r + 8)
                A(nr[:, :], bank[4][:, :], ACT.Ln, bias=eps[:, :], scale=1.0 / D).then_inc(s["n_ln"], 1)
                act.wait_ge(s["n_ln"], r + 1)
                A(nr[:, :], nr[:, :], ACT.Exp, scale=-0.5).then_inc(s["n_rstd"], 1)
                if NORM_MOD[r]:
                    layer, g = NORM_MOD[r]
                    if gemm_before(n):
                        act.wait_ge(s["gemm_done"], gemm_before(n))
                    for k in range(KD):
                        act.wait_ge(s["n_scaled"], 8 * modulated(r) + k + 1)
                        A(HH[:, k, :], nt[:, k % 2, :], ACT.Identity, bias=mod[:, layer, g, k:k + 1]
                          ).then_inc(s["n_high"], 1)

            def evacuate(n, j, kind, layer, i):
                act.wait_ge(s["gemm_done"], j.w + 1)

                def put(dst, src, f=ACT.Copy, scale=1.0):
                    A(dst, src, f, scale=scale).then_inc(s["act_evac"], 1)

                o = [bank[2 * (j.bank % 2) + m] for m in range(2)]
                if kind in ("qa", "ka"):
                    t = qa if kind == "qa" else ka
                    for m in range(2):
                        put(t[:, 2 * (i % 2) + m, :], o[m][:, :], scale=0.125 if kind == "qa" else 1.0)
                elif kind == "va":
                    for m in range(2):
                        put(va[:, 2 * m:2 * m + 2, CW * (i - 4):CW * (i - 3)],
                            o[m][:, :].rearrange("p (t c) -> p t c", t=2))
                elif kind == "conv":
                    c = i - 6
                    if c == 0:
                        act.wait_ge(s["bias_stored"], 16 * 8)
                    act.wait_ge(s["conv_pad"], 1)
                    if c >= 2:
                        act.wait_ge(s["conv_step"], 8 * (c - 1))
                    for m in range(2):
                        put(cvb[:, c % 2, m, 3:CVP], o[m][:, :])
                elif kind == "zd":
                    for m in range(2):
                        put(zs[:, 2 * (i - 12) + m, :], o[m][:, :], ACT.Silu)
                elif kind == "ba":
                    put(ba[:, :, :], o[0][:, 0:64].rearrange("p (t c) -> p t c", t=4))
                elif kind == "gate":
                    f = 11 * layer + i
                    if f:
                        act.wait_ge(s["f_low"], 2 * f)
                    for m in range(2):
                        put(SG[:, m, :], o[m][:, :], ACT.Silu)
                elif kind in ("aqf", "abg", "av"):
                    if heads_done(n):
                        act.wait_ge(s["mixed"], heads_done(n))
                        act.wait_ge(s["h_low"], heads_done(n))
                    a = aslot[i % 2]
                    if kind == "aqf":
                        put(a["q"][:, :], o[0][:, :], ACT.Silu)
                        put(a["G1"][:, 1, :], o[1][:, :], ACT.Sigmoid)
                        put(a["KK"][:, 0, :], o[1][:, :], ACT.Sigmoid, -1.0)
                    elif kind == "abg":
                        put(a["G1"][:, 0, :], o[0][:, :], ACT.Sigmoid)
                        put(a["KK"][:, 1, :], o[0][:, :], ACT.Sigmoid, -1.0)
                        put(agate[:, i, :], o[1][:, :], ACT.Sigmoid)
                    else:
                        for m in range(2):
                            put(avb[i][:, 2 * m:2 * m + 2, :], o[m][:, :].rearrange("p (t c) -> p t c", t=2))
                elif kind in ("bq", "bk"):
                    act.wait_ge(s["m_add"], adds_before(n))
                    act.wait_ge(s["mixed"], heads_done(n))
                    act.wait_ge(s["h_low"], heads_done(n))
                    for m in range(2):
                        put((bq if kind == "bq" else bk)[:, m, :], o[m][:, :],
                            scale=1.0 if kind == "bq" else 0.125)
                elif kind == "bv":
                    for m in range(2):
                        put(bv[:, 2 * m:2 * m + 2, CW * i:CW * i + CW],
                            o[m][:, :].rearrange("p (t c) -> p t c", t=2))
                elif kind == "bg":
                    for m in range(2):
                        put(bg[:, 2 * i + m, :], o[m][:, :], ACT.Silu)
                elif kind in ("cq", "ck"):
                    act.wait_ge(s["m_add"], adds_before(n))
                    act.wait_ge(s["mixed"], heads_done(n))
                    act.wait_ge(s["h_low"], heads_done(n))
                    for m in range(2):
                        put((cq if kind == "cq" else ck)[:, m, :], o[m][:, :],
                            scale=0.125 if kind == "cq" else 1.0)
                elif kind == "cl":
                    put(clr[0:32, :], o[0][0:32, :])
                elif kind == "cv":
                    act.wait_ge(s["mixed"], heads_done(n))
                    for m in range(2):
                        put(cvb2[i][:, 2 * m:2 * m + 2, :], o[m][:, :].rearrange("p (t c) -> p t c", t=2))
                elif kind == "cg":
                    act.wait_ge(s["h_low"], heads_done(n))
                    for m in range(2):
                        put(cg[:, m, :], o[m][:, :], ACT.Silu)
                elif kind in ("ga", "gb", "gc"):
                    if adds_before(n):
                        act.wait_ge(s["m_add"], adds_before(n))
                    act.wait_ge(s["mixed"], heads_done(n))
                    act.wait_ge(s["h_low"], heads_done(n))
                    for m in range(2):
                        put(gate_at[GATE_AT[kind[1]][2 * i + m]][:, :], o[m][:, :], ACT.Sigmoid)

            def begin(n):
                if JOBS[n].w + 1 < len(PRODUCTS):
                    split(JOBS[n].w + 1)

            def end(n):
                j = JOBS[n]
                _, kind, layer, i = STEPS[n]
                if j.last and kind not in ("wout", "down", "up", "pa", "pb", "pc"):
                    evacuate(n, j, kind, layer, i)
                if kind == "up":
                    f = 11 * layer + i
                    for m in range(2):
                        act.wait_ge(s["dve_evac"], j.dve0 + m + 1)
                        if i == 0:
                            act.wait_ge(s["gemm_done"], gemm_before(n))
                        A(AH[:, 2 * i + m, :], SG[:, m, :], ACT.Copy).then_inc(s["f_high"], 1)

            def fill(st, slot):
                for n, part in parts(st, slot):
                    if part == 0:
                        begin(n)
                for n, part in parts(st, slot - 1):
                    if part == PARTS - 1:
                        end(n)

            def attention(h):
                if h < 8:
                    for i in range(NT):
                        act.wait_ge(s["a_nmax"], h + 1)
                        seg = slice(SEG[i], SEG[i] + P * (i + 1))
                        A(Sx[:, h % 2, seg], Sx[:, h % 2, seg], ACT.Exp, bias=anmax[:, h % 2, i:i + 1],
                          accum_out=asum[:, h % 2, i:i + 1]).then_inc(s["a_exp"], 1)
                if h >= 1:
                    g = h - 1
                    act.wait_ge(s["a_turned"], g + 1)
                    if g >= 2:
                        act.wait_ge(s["a_out"], g - 1)
                    for b, a, e in ((0, 0, 512), (1, 512, 1024), (2, 1024, 1280)):
                        A(PT[:, g % 2, a:e], bank[b][:, 0:e - a], ACT.Copy).then_inc(s["a_turn_copied"], 1)
                    if g % 2:
                        act.wait_ge(s["a_out"], g + 1)
                        if g == 1:
                            act.wait_ge(s["gemm_done"], 15)
                        A(HH[:, g // 2, :], bank[3 if g // 2 % 2 else 7][:, :], ACT.Copy
                          ).then_inc(s["a_high"], 1)

            def delta():
                dc = dcol
                for i in range(8):
                    if i == 0:
                        act.wait_ge(s["conv_silu"], 12)
                        act.wait_ge(s["a_out"], 8)
                    if i >= 2:
                        act.wait_ge(s["dn_sum"], i - 1)
                    A(dset[1]["Dm"][:, :] if i % 2 else dset[1]["QKT"][:, :], CO[:, i, :], ACT.Square
                      ).then_inc(s["dn_sq"], 1)
                    act.wait_ge(s["dn_sum"], i + 1)
                    if i:
                        act.wait_ge(s["dn_scaled"], i)
                    A(dset[1]["DT"][:, :], bank[i % 2][:, :], ACT.Ln, bias=eps[:, :]).then_inc(s["dn_ln"], 1)
                    act.wait_ge(s["dn_ln"], i + 1)
                    A(dset[1]["DT"][:, :], dset[1]["DT"][:, :], ACT.Exp, scale=-0.5).then_inc(s["dn_r"], 1)
                for i in range(8):
                    act.wait_ge(s["dt_turn"], i + 1)
                    t = ktok if i < 4 else vtok
                    A(t[:, :, P * (i % 4):P * (i % 4) + P],
                      bank[4 + i % 2][:, :].rearrange("p (n c) -> p n c", n=4), ACT.Copy
                      ).then_inc(s["dt_copy"], 1)
                act.wait_ge(s["act_evac"], BA_DONE)

                def g4(k):
                    return dc[:, k, :].rearrange("p (n h) -> p n h", n=4)

                A(g4(0), ba[:, :, 0:8], ACT.Sigmoid).then_inc(s["dg_act"], 1)
                A(dc[:, 11, 0:8], par("a_log", 0, 8), ACT.Exp).then_inc(s["dg_act"], 1)
                act.wait_ge(s["dg_pool"], 1)
                A(dc[:, 2, :], dc[:, 1, :], ACT.Abs).then_inc(s["dg_act"], 1)
                act.wait_ge(s["dg_act"], 3)
                A(dc[:, 2, :], dc[:, 2, :], ACT.Exp, scale=-1.0).then_inc(s["dg_act"], 1)
                act.wait_ge(s["dg_act"], 4)
                A(dc[:, 2, :], dc[:, 2, :], ACT.Ln, bias=1.0).then_inc(s["dg_act"], 1)
                act.wait_ge(s["dg_ps"], 1)
                A(dc[:, 4, :], bank[6][:, 0:32], ACT.Copy).then_inc(s["dg_cum"], 1)
                A(dc[:, 6, :], bank[6][:, 32:64], ACT.Copy).then_inc(s["dg_cum"], 1)
                A(dc[:, 5, :], bank[6][:, 0:32], ACT.Exp).then_inc(s["dg_cum"], 1)
                A(dc[:, 9, :], bank[6][:, 32:64], ACT.Exp).then_inc(s["dg_cum"], 1)
                act.wait_ge(s["dg_pool"], 5)
                A(dc[:, 8, :], dc[:, 7, :], ACT.Exp).then_inc(s["dg_cum"], 1)
                for p in range(4):
                    for e in range(2):
                        h, d = 2 * p + e, dset[e]
                        act.wait_ge(s["d_rows"], h + 1)
                        if p:
                            act.wait_ge(s["d_o"], 4 * p)
                        A(d["ER"][:, :], bank[4 * e][:, :], ACT.Exp).then_inc(s["d_er"], 1)
                        act.wait_ge(s["d_et"], 4 * h + 4)
                        A(d["ET"][:, :], d["ET"][:, :], ACT.Exp).then_inc(s["d_etexp"], 1)
                    for e in range(2):
                        h, d = 2 * p + e, dset[e]
                        act.wait_ge(s["d_tr"], h + 1)
                        A(d["Dm"][:, :], bank[4 * e][:, :], ACT.Copy).then_inc(s["d_dm0"], 1)
                    for l in range(6):
                        for e in range(2):
                            h, d = 2 * p + e, dset[e]
                            act.wait_ge(s["d_x"], 12 * p + 2 * l + e + 1)
                            if l:
                                act.wait_ge(s["d_y"], 12 * p + 2 * (l - 1) + e + 1)
                            A(d["X"][:, :], bank[4 * e + 1][:, :], ACT.Copy).then_inc(s["d_xc"], 1)
                    for e in range(2):
                        h, d = 2 * p + e, dset[e]
                        off = 64 * e
                        act.wait_ge(s["d_uw"], h + 1)
                        A(dset[e]["MT"][:, 0:256], bank[4 * e][:, 0:256], ACT.Copy).then_inc(s["d_uwc"], 1)
                        A(d["X"][off:off + 64, :], bank[4 * e + 1][off:off + 64, :], ACT.Copy
                          ).then_inc(s["d_uwc"], 1)
                    act.wait_ge(s["d_o"], 4 * p + 4)
                    A(dset[1]["AT"][:, :], bank[0][:, :], ACT.Square).then_inc(s["df_sq"], 1)
                    act.wait_ge(s["df_sum"], p + 1)
                    A(dset[1]["Dm"][:, :], bank[5][:, :], ACT.Ln, bias=eps[:, :], scale=1.0 / 64
                      ).then_inc(s["df_ln"], 1)
                    act.wait_ge(s["df_ln"], p + 1)
                    A(dset[1]["Dm"][:, :], dset[1]["Dm"][:, :], ACT.Exp, scale=-0.5).then_inc(s["df_r"], 1)
                    act.wait_ge(s["df_y"], p + 1)
                    A(HH[:, 4 + p, :], dset[0]["Dm"][:, :], ACT.Copy).then_inc(s["df_high"], 1)

            def copy_scores(u, e, ST, level):
                b0, b1 = bank[4 + 2 * e], bank[5 + 2 * e]
                act.wait_ge(s["levels"], 10 * u + level + 1)
                st = ST[:, :, :]
                if level == 0:
                    A(bc(st, [640, 4], [1, P]), b0[:, :].rearrange("p (j t) -> p j t", j=4), ACT.Copy
                      ).then_inc(s["scores_copied"], 1)
                elif level == 8:
                    dst = bass.AP(st.tensor, st.offset + 128, [list(st.ap[0]), [1280, 2], [384, 2], [1, P]])
                    A(dst, b0[:, :].rearrange("p (a b t) -> p a b t", a=2, b=2), ACT.Copy
                      ).then_inc(s["scores_copied"], 1)
                else:
                    for x, b, off in ((0, b0, 256), (1, b1, 1024)):
                        dst = bass.AP(st.tensor, st.offset + off, [list(st.ap[0]), [512, 2], [1, 256]])
                        A(dst, b[:, :].rearrange("p (a t) -> p a t", a=2), ACT.Copy
                          ).then_inc(s["scores_copied"], 1)

            def finish(st, e, hd, group, y):
                b0, b1 = bank[4 + 2 * e], bank[5 + 2 * e]
                act.wait_ge(s["mixed"], hd + 1)
                if hd:
                    act.wait_ge(s["h_low"], hd)
                if ADDS[0]:
                    act.wait_ge(s["m_add"], ADDS[0])
                bi = b_before[st]
                if group:
                    A(ttt[:, :], b0[:, :], ACT.Copy).then_inc(s["h_cp"], 1)
                    fill(st, 5)
                    act.wait_ge(s["h_cent"], bi + 1)
                    A(sqt[:, :], ttt[:, :], ACT.Square).then_inc(s["h_sq"], 1)
                else:
                    A(sqt[:, :], b0[:, :], ACT.Square).then_inc(s["h_sq"], 1)
                act.wait_ge(s["h_sum"], hd + 1)
                A(rrt[:, :], b1[:, :], ACT.Ln, bias=eps[:, :], scale=1.0 / P).then_inc(s["h_ln"], 1)
                act.wait_ge(s["h_ln"], hd + 1)
                A(rrt[:, :], rrt[:, :], ACT.Exp, scale=-0.5).then_inc(s["h_r"], 1)
                act.wait_ge(s["h_y"], hd + 1)
                act.wait_ge(s["gemm_done"], GB[0])
                A(YH[:, y, :], ttt[:, :], ACT.Copy).then_inc(s["h_high"], 1)

            GB, ADDS = [0], [0]
            BA_DONE = next(JOBS[m].act for m, x in enumerate(STEPS) if x[:2] == ("job", "ba"))
            nrm = 0
            for n, st in enumerate(STEPS):
                GB[0], ADDS[0] = gemm_before(n), adds_before(n)
                if st[0] == "norm":
                    if nrm == 0:
                        split(0)
                    norm(n, nrm)
                    nrm += 1
                elif st[0] == "job":
                    if n not in EMBEDDED:
                        begin(n)
                        end(n)
                elif st[0] == "conv":
                    c = st[1]
                    for m in range(2):
                        act.wait_ge(s["conv_step"], 8 * c + 4 * m + 4)
                        A(CO[:, 2 * c + m, :], CO[:, 2 * c + m, :], ACT.Silu).then_inc(s["conv_silu"], 1)
                elif st[0] == "attn":
                    attention(st[1])
                elif st[0] == "delta":
                    delta()
                elif st[0] == "merge":
                    r = st[1] - 1
                    act.wait_ge(s["gemm_done"], gemm_before(n))
                    for k in range(KD):
                        act.wait_ge(s["m_add"], 24 * r + 16 + k + 1)
                        A(HH[:, k, :], macc[:, k, :], ACT.Copy).then_inc(s["m_high"], 1)
                elif st[0] == "mix":
                    _, kind, layer, i = st
                    hd = heads[st]
                    if kind == "b":
                        for slot in range(5):
                            fill(st, slot)
                        finish(st, i % 2, hd, True, i)
                        fill(st, 6)
                        continue
                    u = units[st]
                    if kind == "c":
                        cu = 2 * (layer - 1) + i
                        for dr in range(2):
                            pl = 1 - dr
                            act.wait_ge(s["c_logit"], 2 * cu + dr + 1)
                            bcol = par("b_alpha", 4 * (layer - 1) + 2 * dr + i)
                            A(c_x[:, pl, :], bank[4 + 2 * dr][:, :], ACT.Identity, bias=bcol
                              ).then_inc(s["c_act"], 1)
                        act.wait_ge(s["c_act"], 5 * cu + 2)
                        A(c_e[:, :, :], c_x[:, :, :], ACT.Abs).then_inc(s["c_act"], 1)
                        act.wait_ge(s["c_act"], 5 * cu + 3)
                        A(c_e[:, :, :], c_e[:, :, :], ACT.Exp, scale=-1.0).then_inc(s["c_act"], 1)
                        act.wait_ge(s["c_act"], 5 * cu + 4)
                        A(c_e[:, :, :], c_e[:, :, :], ACT.Ln, bias=1.0).then_inc(s["c_act"], 1)
                        act.wait_ge(s["c_dve"], cu + 1)
                        A(cG1[:, :, :], c_x[:, :, :], ACT.Exp, scale=1.0 / 16).then_inc(s["c_lanes"], 1)
                        A(cKK[:, :, :], bc(ck[:, i, :], [0, 2], [1, S]), ACT.Copy).then_inc(s["c_lanes"], 1)
                        hs = [(0, cST[0]), (1, cST[1])]
                    else:
                        hs = [(i % 2, aslot[i % 2]["ST"])]
                    for level in range(10):
                        if level in (0, 8, 9):
                            for e, ST in hs:
                                copy_scores(u, e, ST, level)
                        fill(st, level)
                    fill(st, 10)
                    for x, (e, ST) in enumerate(hs):
                        finish(st, e, hd + x, False, (2 * i + x) if kind == "c" else i)
                    fill(st, 11)

        @block.vector
        def _(dve):
            TT, TS, STT = dve.tensor_tensor, dve.tensor_scalar, dve.scalar_tensor_tensor

            def split(wi):
                j = PRODUCTS[wi]
                dve.wait_ge(s["w_rounded"], wi + 1)
                TT(WL[:, wi % 2, 0:j.size], raw[:, j.load % RAW, 0:j.size],
                   WH[:, wi % 2, 0:j.size].bitcast(F32), ALU.subtract).then_inc(s["w_split"], 1)

            dve.wait_ge(s["const_in"], 16 * NCONST)
            dve.wait_ge(s["ones_set"], 3)
            l0, l1 = par("lb", 0, 4), par("lb", 4, 4)
            TT(small[:, 4, :], l0, l1, ALU.max).then_inc(s["lb_max"], 1)
            dve.wait_ge(s["lb_max"], 1)
            TT(small[:, 0, :], l0, small[:, 4, :], ALU.subtract).then_inc(s["lb_dve"], 1)
            TT(small[:, 1, :], l1, small[:, 4, :], ALU.subtract).then_inc(s["lb_dve"], 1)
            dve.wait_ge(s["lb_exp"], 1)
            TT(small[:, 5, :], small[:, 2, :], small[:, 3, :], ALU.add).then_inc(s["lb_dve"], 1)
            dve.wait_ge(s["lb_dve"], 3)
            dve.reciprocal(small[:, 6, :], small[:, 5, :]).then_inc(s["lb_dve"], 1)
            dve.wait_ge(s["lb_dve"], 4)
            TT(small[:, 2:4, :], small[:, 2:4, :], bc(small[:, 6, :], [0, 2], [1, 4]), ALU.mult
               ).then_inc(s["lb_dve"], 1)
            dve.wait_ge(s["lb_dve"], 5)
            TT(small[:, 7, :], small[:, 2, :], small[:, 3, :], ALU.add).then_inc(s["lb_dve"], 1)
            dve.wait_ge(s["lb_dve"], 6)
            TT(lbound[:, 0, :], small[:, 2, :], small[:, 2, :], ALU.subtract).then_inc(s["lb_dve"], 1)
            TT(lbound[:, 1, :], small[:, 7, :], small[:, 2, :], ALU.subtract).then_inc(s["lb_dve"], 1)
            dve.wait_ge(s["lb_dve"], 8)
            TS(lbound[:, :, :], lbound[:, :, :], 0.0, None, ALU.max).then_inc(s["lb_dve"], 1)
            dve.wait_ge(s["lb_dve"], 9)
            TS(rest[:, :, :], lbound[:, :, :], -1.0, 1.0, ALU.mult, ALU.add).then_inc(s["lb_dve"], 1)
            dve.wait_ge(s["cact_ready"], 1)
            dve.wait_ge(s["bias_stored"], 16 * 8)
            dve.memset(cvb[:, :, :, :], 0.0).then_inc(s["conv_pad"], 1)

            def ada_chunk(j):
                _, layer, g, c = j.src
                dve.wait_ge(raw_in[j.load % RAW], 16 * (j.load // RAW + 1))
                if c == 0:
                    if layer or g:
                        dve.wait_ge(s["mod_ready"], 6 * layer + g)
                for t in range(2):
                    if j.ada or t:
                        dve.wait_ge(s["ada_mac"], 2 * j.ada + t)
                    src = raw[:, j.load % RAW, ADA_COLS * t:ADA_COLS * (t + 1)]
                    col = cact[:, 8 * layer + 2 * c + t:8 * layer + 2 * c + t + 1]
                    if c == 0 and t == 0:
                        i = TS(ada_acc[:, :], src, col, None, ALU.mult)
                    else:
                        i = STT(ada_acc[:, :], src, col, ada_acc[:, :], ALU.mult, ALU.add)
                    i.then_inc(s["ada_mac"], 1)

            def norm(n, r):
                name, at = NORM_G[r]
                q = modulated(r)
                if NORM_MOD[r]:
                    layer, g = NORM_MOD[r]
                    dve.wait_ge(s["dve_evac"], mod_ready_count(layer, g + 1))
                    STT(acol[:, :], mod[:, layer, g + 1, :], 1.0, par(name, at, 8), ALU.add, ALU.mult
                        ).then_inc(s["n_acol"], 1)
                    dve.wait_ge(s["n_acol"], q + 1)
                dve.wait_ge(s["n_rstd"], r + 1)
                for k in range(KD):
                    if r == RENORM:
                        STT(xT[:, k, :], xT[:, k, :], par(name, k), nr[:, :], ALU.mult, ALU.mult
                            ).then_inc(s["renormed"], 1)
                        continue
                    if r == FINAL:
                        STT(ost[:, k, :], xT[:, k, :], par("g_out", k), nr[:, :], ALU.mult, ALU.mult
                            ).then_inc(s["out_ready"], 1)
                        continue
                    if k >= 2:
                        dve.wait_ge(s["n_low"], 8 * q + k - 1)
                    STT(nt[:, k % 2, :], xT[:, k, :],
                        (acol[:, k:k + 1]),
                        nr[:, :], ALU.mult, ALU.mult).then_inc(s["n_scaled"], 1)
                    dve.wait_ge(s["n_high"], 8 * q + k + 1)
                    STT(HL[:, k, :], nt[:, k % 2, :], mod[:, layer, g, k:k + 1], HH[:, k, :].bitcast(F32),
                        ALU.add, ALU.subtract).then_inc(s["n_low"], 1)

            def evacuate(n, j, kind, layer, i):
                dve.wait_ge(s["gemm_done"], j.w + 1)
                o = [bank[2 * (j.bank % 2) + m] for m in range(2)]
                for m in range(2):
                    if kind in ("wout", "down"):
                        g = 2 if kind == "wout" else 5
                        k = 2 * (i if kind == "wout" else i // 3) + m
                        dve.wait_ge(s["dve_evac"], mod_ready_count(layer, g))
                        STT(xT[:, k, :], o[m][:, :], mod[:, layer, g, k:k + 1], xT[:, k, :],
                            ALU.mult, ALU.add).then_inc(s["dve_evac"], 1)
                    elif kind == "up":
                        dve.wait_ge(s["act_evac"], j.act0)
                        TT(SG[:, m, :], SG[:, m, :], o[m][:, :], ALU.mult).then_inc(s["dve_evac"], 1)
                    else:
                        gate = gate_at[GATE_AT[kind[1]][2 * i + m]]
                        dve.wait_ge(s["act_evac"], evacuated("g" + kind[1], layer, i))
                        TT(gate[:, :], gate[:, :], o[m][:, :], ALU.mult).then_inc(s["dve_evac"], 1)
                if kind == "up":
                    f = 11 * layer + i
                    for m in range(2):
                        dve.wait_ge(s["f_high"], 2 * f + m + 1)
                        TT(AL[:, 2 * i + m, :], SG[:, m, :], AH[:, 2 * i + m, :].bitcast(F32), ALU.subtract
                           ).then_inc(s["f_low"], 1)
                if kind in ("pa", "pb", "pc"):
                    x = "abc".index(kind[1])
                    r = layer - 1
                    for m in range(2):
                        k = 2 * i + m
                        gate = gate_at[GATE_AT[kind[1]][k]]
                        dve.wait_ge(s["dve_evac"], j.dve0 + m + 1)
                        if x == 0:
                            dve.tensor_copy(macc[:, k, :], gate[:, :]).then_inc(s["m_add"], 1)
                        else:
                            dve.wait_ge(s["m_add"], 24 * r + 8 * (x - 1) + k + 1)
                            TT(macc[:, k, :], macc[:, k, :], gate[:, :], ALU.add).then_inc(s["m_add"], 1)
                    dve.wait_ge(s["m_add"], 24 * r + 8 * x + 2 * i + 2)

            def begin(n):
                if JOBS[n].w + 1 < len(PRODUCTS):
                    split(JOBS[n].w + 1)

            def end(n):
                j = JOBS[n]
                _, kind, layer, i = STEPS[n]
                if j.last and kind in ("wout", "down", "up", "pa", "pb", "pc"):
                    evacuate(n, j, kind, layer, i)

            def fill(st, slot):
                for n, part in parts(st, slot):
                    if part == 0:
                        begin(n)
                for n, part in parts(st, slot - 1):
                    if part == PARTS - 1:
                        end(n)

            def attention(h):
                if h < 8:
                    dve.wait_ge(s["a_scores"], h + 1)
                    dve.wait_ge(toep_in[h % 3], 16 * (h // 3 + 1))
                    if h >= 2:
                        dve.wait_ge(s["a_turned"], h - 1)
                    for i in range(NT):
                        b, c0 = SBANK[i]
                        seg = slice(SEG[i], SEG[i] + P * (i + 1))
                        dve.tensor_tensor_reduce(Sx[:, h % 2, seg], bank[b][:, c0:c0 + P * (i + 1)],
                                                 toep[:, h % 3, 384 - P * i:512], 1.0, -3.0e38,
                                                 ALU.add, ALU.max, amax[:, h % 2, i:i + 1]
                                                 ).then_inc(s["a_biased"], 1)
                    dve.wait_ge(s["a_biased"], 4 * h + 4)
                    TS(anmax[:, h % 2, :], amax[:, h % 2, :], -1.0, None, ALU.mult).then_inc(s["a_nmax"], 1)
                    dve.wait_ge(s["a_exp"], 4 * h + 4)
                    dve.reciprocal(arsum[:, h % 2, :], asum[:, h % 2, :]).then_inc(s["a_rsum"], 1)
                    dve.wait_ge(s["a_rsum"], h + 1)
                    for i in range(NT):
                        seg = slice(SEG[i], SEG[i] + P * (i + 1))
                        TS(Sx[:, h % 2, seg], Sx[:, h % 2, seg], arsum[:, h % 2, i:i + 1], None, ALU.mult
                           ).then_inc(s["a_norm"], 1)
                if h >= 1 and (h - 1) % 2:
                    g = (h - 1) // 2
                    dve.wait_ge(s["a_high"], g + 1)
                    TT(HL[:, g, :], bank[3 if g % 2 else 7][:, :], HH[:, g, :].bitcast(F32), ALU.subtract
                       ).then_inc(s["a_low"], 1)

            def delta():
                dc = dcol
                for i in range(8):
                    dve.wait_ge(s["dn_r"], i + 1)
                    STT(CO[:, i, :], CO[:, i, :], 0.125 if i < 4 else 1.0, dset[1]["DT"][:, :],
                        ALU.mult, ALU.mult).then_inc(s["dn_scaled"], 1)

                def g4(k):
                    return dc[:, k, :].rearrange("p (n h) -> p n h", n=4)

                dve.wait_ge(s["dg_act"], 2)
                TT(g4(1), ba[:, :, 8:16], bc(par("dt_bias", 0, 8), [0, 4], [1, 8]), ALU.add
                   ).then_inc(s["dg_pool"], 1)
                dve.wait_ge(s["dg_act"], 5)
                STT(dc[:, 3, :], dc[:, 1, :], 0.0, dc[:, 2, :], ALU.max, ALU.add).then_inc(s["dg_pool"], 1)
                dve.wait_ge(s["dg_pool"], 2)
                STT(g4(3), g4(3), -1.0, bc(dc[:, 11, 0:8], [0, 4], [1, 8]), ALU.mult, ALU.mult
                    ).then_inc(s["dg_pool"], 1)
                dve.wait_ge(s["dg_cum"], 4)
                TT(dc[:, 10, :], dc[:, 0, :], dc[:, 5, :], ALU.mult).then_inc(s["dg_pool"], 1)
                TT(dc[:, 7, :], dc[:, 6, :], dc[:, 4, :], ALU.subtract).then_inc(s["dg_pool"], 1)
                dve.wait_ge(s["dg_cum"], 5)
                dve.wait_ge(s["dt_copy"], 8)

                def v4(t):
                    return t[:, :].rearrange("p (n i) -> p n i", n=4)

                for p in range(4):
                    for e in range(2):
                        h, d, off = 2 * p + e, dset[e], 64 * e
                        dve.wait_ge(s["d_rows"], h + 1)
                        if p:
                            dve.wait_ge(s["d_o"], 4 * p)
                        dve.wait_ge(s["d_er"], h + 1)
                        for n in range(4):
                            col = 8 * n + h
                            TS(d["ET"][:, P * n:P * n + P], bank[4 * e][:, P * n:P * n + P],
                               dc[:, 4, col:col + 1], 0.0, ALU.subtract, ALU.min).then_inc(s["d_et"], 1)
                        TT(d["kbT"][off:off + 64, :], CO[off:off + 64, 4 + p, :], bank[4 * e + 1][off:off + 64, :],
                           ALU.mult).then_inc(s["d_kb"], 1)
                    for e in range(2):
                        h, d, off = 2 * p + e, dset[e], 64 * e
                        dve.wait_ge(s["d_kk"], h + 1)
                        dve.wait_ge(s["d_etmask"], h + 1)
                        TT(d["AT"][:, :], bank[4 * e + 2][:, :], d["ET"][:, :], ALU.mult).then_inc(s["d_at"], 1)
                        TT(d["QKT"][:, :], bank[4 * e + 3][:, :], d["ET"][:, :], ALU.mult).then_inc(s["d_qk"], 1)
                    for e in range(2):
                        h, d, off = 2 * p + e, dset[e], 64 * e
                        dve.wait_ge(s["d_m"], 14 * p + e + 1)
                        TT(v4(d["DT"]), bc(ident[:, :], [0, 4], [1, P]), v4(d["MT"]), ALU.subtract
                           ).then_inc(s["d_dt0"], 1)
                        for x, (t, dst, k) in enumerate(((vtok, "bv", 0), (ktok, "kbe", 10), (ktok, "kdec", 8))):
                            if dst == "bv":
                                dve.wait_ge(s["d_qk"], h + 1)
                            out_ = v4s(d["ET"]) if dst == "bv" else d[dst][:, :, :]
                            TT(out_, t[:, :, 64 * h:64 * h + 64],
                               bass.AP(dc[:, k, :].tensor, dc[:, k, :].offset + h,
                                       [list(dc[:, k, :].ap[0]), [8, 4], [0, 64]]), ALU.mult
                               ).then_inc(s["d_tok"], 1)
                        dve.wait_ge(s["d_er"], h + 1)
                        TT(d["kbT"][off:off + 64, :], CO[off:off + 64, p, :], d["ER"][off:off + 64, :], ALU.mult
                           ).then_inc(s["d_qe"], 1)
                    for l in range(6):
                        for e in range(2):
                            h, d = 2 * p + e, dset[e]
                            dve.wait_ge(s["d_y"], 12 * p + 2 * l + e + 1)
                            if l < 5:
                                TT(d["Dm"][:, :], d["Dm"][:, :], bank[4 * e + 2][:, :], ALU.subtract
                                   ).then_inc(s["d_upd"], 1)
                            TT(d["DT"][:, :], d["DT"][:, :], bank[4 * e + 3][:, :], ALU.subtract
                               ).then_inc(s["d_upd"], 1)
                    for n in range(4):
                        for e in range(2):
                            h, d, off = 2 * p + e, dset[e], 64 * e
                            U = d["MT"][:, 64 * n:64 * n + 64]
                            V = d["MT"][:, 256 + 64 * (n % 2):320 + 64 * (n % 2)]
                            dve.wait_ge(s["d_uwc"], 2 * h + 2)
                            if n:
                                dve.wait_ge(s["d_ws"], 6 * p + 2 * (n - 1) + e + 1)
                                TT(V, U, bank[4 * e + 2][:, 64 * n:64 * n + 64], ALU.subtract
                                   ).then_inc(s["d_vn"], 1)
                            else:
                                dve.tensor_copy(V, U).then_inc(s["d_vn"], 1)
                        if n < 3:
                            for e in range(2):
                                h, d, off = 2 * p + e, dset[e], 64 * e
                                st_ = d["ER"][off:off + 64, 64 * (n % 2):64 * (n % 2) + 64]
                                so = d["ER"][off:off + 64, 64 * (1 - n % 2):64 * (1 - n % 2) + 64]
                                dve.wait_ge(s["d_sp"], 6 * p + 2 * n + e + 1)
                                ps = bank[4 * e + 3][off:off + 64, 64 * n:64 * n + 64]
                                if n:
                                    dve.wait_ge(s["d_sn"], 6 * p + 2 * (n - 1) + e + 1)
                                    STT(st_, so, dc[off:off + 64, 9, 8 * n + h:8 * n + h + 1], ps,
                                        ALU.mult, ALU.add).then_inc(s["d_sn"], 1)
                                else:
                                    dve.tensor_copy(st_, ps).then_inc(s["d_sn"], 1)
                    dve.wait_ge(s["d_o"], 4 * p + 4)
                    T = dset[0]["Dm"]
                    dve.wait_ge(s["df_sq"], p + 1)
                    STT(T[:, :], bank[0][:, :], par("delta_g"), zs[:, p, :], ALU.mult, ALU.mult
                        ).then_inc(s["df_t"], 1)
                    dve.wait_ge(s["df_r"], p + 1)
                    dve.wait_ge(s["df_t"], p + 1)
                    TT(T[:, :], T[:, :], dset[1]["Dm"][:, :], ALU.mult).then_inc(s["df_y"], 1)
                    dve.wait_ge(s["df_high"], p + 1)
                    TT(HL[:, 4 + p, :], T[:, :], HH[:, 4 + p, :].bitcast(F32), ALU.subtract
                       ).then_inc(s["df_low"], 1)

            def v4s(t):
                return t[:, 0:256].rearrange("p (n c) -> p n c", n=4)

            def scan(st, u, hd, QQ, KK, g1, gt, hs):
                sc0 = 7 * scan_before[st]
                fill(st, 0)
                dve.wait_ge(s["lanes"], 8 * u + 8)
                for level in range(1, 9):
                    b = 2 ** (level - 1)
                    dve.wait_ge(s["levels"], 10 * u + level + 1)
                    if level > 1:
                        dve.wait_ge(s["decayed"], 16 * u + 2 * (level - 1))
                    TT(lanes(QQ, b), lanes(QQ, b), lane_gates(g1, gt, b, False), ALU.mult
                       ).then_inc(s["decayed"], 1)
                    TT(lanes(KK, b), lanes(KK, b), lane_gates(g1, gt, b, True), ALU.mult
                       ).then_inc(s["decayed"], 1)
                    if level < 8:
                        for x, (e, ST) in enumerate(hs):
                            if level == 1:
                                dve.wait_ge(s["scores_copied"], 4 * scan_before[st] + x + 1)
                            else:
                                dve.wait_ge(s["scores_put"], sc0 + len(hs) * (level - 2) + x + 1)
                            dve.copy_predicated(bc(ST[:, :, :], [640, 4], [1, P]),
                                                bc(masks[:, level - 1, :], [0, 4], [1, P]),
                                                bank[4 + 2 * e + level % 2][:, :].rearrange("p (j t) -> p j t", j=4)
                                                ).then_inc(s["scores_put"], 1)
                    fill(st, level)
                fill(st, 9)
                fill(st, 10)

            def finish(st, e, hd, group, y, gate, layer):
                x = "abc".index(st[1])
                bi = b_before[st]
                b0 = bank[4 + 2 * e]
                dve.wait_ge(s["mixed"], hd + 1)
                col = par("norm", 12 * (layer - 1) + 4 * x + y)
                if group:
                    dve.wait_ge(s["h_mean"], bi + 1)
                    STT(ttt[:, :], bank[5 + 2 * e][:, :], -1.0 / P, ttt[:, :], ALU.mult, ALU.add
                        ).then_inc(s["h_cent"], 1)
                    fill(st, 5)
                    dve.wait_ge(s["h_sq"], hd + 1)
                    STT(ttt[:, :], ttt[:, :], col, gate, ALU.mult, ALU.mult).then_inc(s["h_t"], 1)
                else:
                    dve.wait_ge(s["h_sq"], hd + 1)
                    STT(ttt[:, :], b0[:, :], col, gate, ALU.mult, ALU.mult).then_inc(s["h_t"], 1)
                dve.wait_ge(s["h_r"], hd + 1)
                dve.wait_ge(s["h_t"], hd + 1)
                TT(ttt[:, :], ttt[:, :], rrt[:, :], ALU.mult).then_inc(s["h_y"], 1)
                dve.wait_ge(s["h_high"], hd + 1)
                TT(YL[:, y, :], ttt[:, :], YH[:, y, :].bitcast(F32), ALU.subtract).then_inc(s["h_low"], 1)

            CONV_EVAC = [JOBS[m].act for m, x in enumerate(STEPS) if x[:2] == ("job", "conv")]
            nrm = 0
            for n, st in enumerate(STEPS):
                if st[0] == "ada":
                    ada_chunk(JOBS[n])
                elif st[0] == "mod":
                    _, layer, g = st
                    j = JOBS[n]
                    dve.wait_ge(s["mod_ready"], 6 * layer + g + 1)
                    TT(mod[:, layer, g, :], bank[2 * (j.bank % 2)][:, 0:8],
                       par("b_ada", 48 * layer + 8 * g, 8), ALU.add).then_inc(s["dve_evac"], 1)
                elif st[0] == "norm":
                    if nrm == 0:
                        split(0)
                    norm(n, nrm)
                    nrm += 1
                elif st[0] == "job":
                    if n not in EMBEDDED:
                        begin(n)
                        end(n)
                elif st[0] == "conv":
                    c = st[1]
                    for m in range(2):
                        t = 2 * c + m
                        dve.wait_ge(s["act_evac"], CONV_EVAC[c] - 1 + m)
                        for k in range(4):
                            src = cvb[:, c % 2, m, k:k + S]
                            wc = par("conv", 4 * t + k)
                            if k == 0:
                                TS(CO[:, t, :], src, wc, None, ALU.mult).then_inc(s["conv_step"], 1)
                            else:
                                dve.wait_ge(s["conv_step"], 8 * c + 4 * m + k)
                                STT(CO[:, t, :], src, wc, CO[:, t, :], ALU.mult, ALU.add
                                    ).then_inc(s["conv_step"], 1)
                elif st[0] == "attn":
                    attention(st[1])
                elif st[0] == "delta":
                    delta()
                elif st[0] == "rotary":
                    r = st[1] - 1
                    dve.wait_ge(s["r_in"], 64 * (r + 1))
                    for x in range(4):
                        t = (bq if x < 2 else bk)[:, x % 2, :]
                        dve.wait_ge(s["r_rot"], 4 * r + x + 1)
                        TT(btmp[:, :], bank[4 + x][:, :], brot[:, S:2 * S], ALU.mult).then_inc(s["r_t"], 1)
                        TT(t, t, brot[:, 0:S], ALU.mult).then_inc(s["r_t"], 1)
                        dve.wait_ge(s["r_t"], 12 * r + 3 * x + 2)
                        TT(t, t, btmp[:, :], ALU.add).then_inc(s["r_t"], 1)
                        dve.wait_ge(s["r_t"], 12 * r + 3 * x + 3)
                elif st[0] == "merge":
                    r = st[1] - 1
                    for k in range(KD):
                        dve.wait_ge(s["m_high"], 8 * r + k + 1)
                        TT(HL[:, k, :], macc[:, k, :], HH[:, k, :].bitcast(F32), ALU.subtract
                           ).then_inc(s["m_low"], 1)
                elif st[0] == "mix":
                    _, kind, layer, i = st
                    hd = heads[st]
                    if kind == "b":
                        bi = b_before[st]
                        if i == 0:
                            dve.wait_ge(s["r_in"], 64 * layer)
                        e = i % 2
                        for jb in range(4):
                            dve.wait_ge(s["b_scores"], 4 * bi + jb + 1)
                            TT(bST[e][:, jb, :], bank[4 + 2 * e + jb % 2][:, :],
                               bgam[:, i, 384 - P * jb:896 - P * jb], ALU.mult).then_inc(s["r_ps"], 1)
                            fill(st, jb)
                        fill(st, 4)
                        dve.wait_ge(s["h_cp"], bi + 1)
                        finish(st, e, hd, True, i, bg[:, i, :], layer)
                        fill(st, 6)
                        continue
                    u = units[st]
                    if kind == "c":
                        cu = 2 * (layer - 1) + i
                        dve.wait_ge(s["c_act"], 5 * cu + 5)
                        STT(c_x[:, :, :], c_x[:, :, :], 0.0, c_e[:, :, :], ALU.min, ALU.subtract
                            ).then_inc(s["c_dve"], 1)
                        scan(st, u, hd, cQQ, cKK, cG1, cGT, [(0, cST[0]), (1, cST[1])])
                        for x in range(2):
                            finish(st, x, hd + x, False, 2 * i + x, cg[:, x, :], layer)
                    else:
                        a = aslot[i % 2]
                        scan(st, u, hd, a["QQ"], a["KK"], a["G1"], a["GT"], [(i % 2, a["ST"])])
                        finish(st, i % 2, hd, False, i, agate[:, i, :], layer)
                        fill(st, 11)

        @block.tensor
        def _(pe):
            MM = pe.matmul

            def acquire(j):
                if j.bank >= 2:
                    who, cnt = FREED[j.bank - 2]
                    pe.wait_ge(s["act_evac" if who == "act" else "dve_evac"], cnt)

            def products(o, sides, first, last, units_):
                n = 0
                total = 3 * len(units_)
                i = None
                for u in units_:
                    for a, b in sides(u):
                        i = MM(o, a, b, start=first and n == 0, stop=last and n == total - 1)
                        n += 1
                return i

            def gemm(n, now=range(PARTS)):
                j = JOBS[n]
                _, kind, layer, i = STEPS[n]
                o = [bank[2 * (j.bank % 2) + m] for m in range(2)]
                sl, wd = j.w % 2, j.width
                X = (HH, HL)
                k0 = 0
                if kind in ("pa", "pb", "pc"):
                    X = (YH, YL)
                elif kind == "down":
                    X = (AH, AL)
                    k0 = 8 * (i % 3)
                if now[0] == 0:
                    pe.wait_ge(s["w_split"], j.w + 1)
                    if j.first:
                        acquire(j)
                    if X[0] is YH:
                        pe.wait_ge(s["h_low"], heads_done(n))
                    elif X[0] is AH:
                        pe.wait_ge(s["f_low"], 22 * (layer + 1))
                if kind in TOKEN_MAJOR:
                    for t in now:
                        if wd == CW:
                            dst = o[t // 2][:, CW * (t % 2):CW * (t % 2) + CW]
                        else:
                            dst = o[0][:, wd * t:wd * t + wd]

                        def sides(u):
                            wh, wl = (x[:, sl, u * wd:(u + 1) * wd] for x in (WH, WL))
                            xh, xl = (x[:, k0 + u, P * t:P * t + P] for x in X)
                            return ((xh, wh), (xh, wl), (xl, wh))

                        last = products(dst, sides, True, True, range(j.units))
                    if now[-1] == PARTS - 1:
                        last.then_inc(s["gemm_done"], 1)
                    return
                first_use = FIRST_USE.get(n)
                cw = min(P, wd)
                for u in range(j.units * now[0] // PARTS, j.units * (now[-1] + 1) // PARTS):
                    if first_use:
                        pe.wait_ge(s[first_use[0]], first_use[1] + u + 1)
                    for m in range(2 if wd == CW else 1):
                        wh, wl = (x[:, sl, u * wd + P * m:u * wd + P * m + cw] for x in (WH, WL))
                        xh, xl = (x[:, k0 + u, :] for x in X)
                        for q, (a, b) in enumerate(((wh, xh), (wh, xl), (wl, xh))):
                            last = MM(o[m][0:cw, :], a, b, start=j.first and u == 0 and q == 0,
                                      stop=j.last and u == j.units - 1 and q == 2)
                if now[-1] == PARTS - 1:
                    last.then_inc(s["gemm_done"], 1)

            def fill(st, slot):
                for n, part in parts(st, slot):
                    gemm(n, range(part, part + 1))

            FIRST_USE = {}
            r = 0
            for n, st in enumerate(STEPS):
                nxt = next((m for m in range(n + 1, len(STEPS)) if STEPS[m][0] == "job"), None)
                if st[0] == "norm":
                    if nxt is not None:
                        FIRST_USE[nxt] = ("n_low", 8 * modulated(r))
                    r += 1
                if st[0] == "merge":
                    FIRST_USE[nxt] = ("m_low", 8 * (st[1] - 1))

            def norm(n, r):
                for k in range(KD):
                    pe.wait_ge(s["n_square"], 8 * r + k + 1)
                    if k == 0:
                        if r == 0:
                            pe.wait_ge(s["bias_rows"], 16)
                        else:
                            pe.wait_ge(s["n_rstd"], r)
                            if heads_done(n):
                                pe.wait_ge(s["h_low"], heads_done(n))
                            pe.wait_ge(s["df_low"], 4)
                    MM(bank[4][:, :], ones[:, :], nsq[:, k % 2, :], start=k == 0, stop=k == KD - 1
                       ).then_inc(s["n_sum"], 1)

            def attention(h):
                if h < 8:
                    t, off = h // 2, 64 * (h % 2)
                    if h == 0:
                        pe.wait_ge(s["act_evac"], BA_DONE)
                        pe.wait_ge(s["n_rstd"], 1)
                    if h >= 1:
                        pe.wait_ge(s["a_biased"], 4 * h)
                    for i in range(NT):
                        b, c0 = SBANK[i]
                        last = MM(bank[b][:, c0:c0 + P * (i + 1)], qa[off:off + 64, t, P * i:P * i + P],
                                  ka[off:off + 64, t, 0:P * (i + 1)], start=True, stop=True)
                    last.then_inc(s["a_scores"], 1)
                if h >= 1:
                    g = h - 1
                    t, off = g // 2, 64 * (g % 2)
                    pe.wait_ge(s["a_norm"], 4 * g + 4)
                    if g:
                        pe.wait_ge(s["a_turn_copied"], 3 * g)
                    else:
                        pe.wait_ge(s["dve_evac"], max(c for x, c in FREED[:BA_BANK + 1] if x == "dve"))
                    for jb in range(NT):
                        for i in range(jb, NT):
                            b, c0 = TBANK[jb]
                            src = Sx[:, g % 2, SEG[i] + P * jb:SEG[i] + P * jb + P]
                            last = pe.transpose(bank[b][:, c0 + P * (i - jb):c0 + P * (i - jb) + P], src,
                                                ident[:, :])
                    last.then_inc(s["a_turned"], 1)
                    pe.wait_ge(s["a_turn_copied"], 3 * g + 3)
                    ob = bank[3 if t % 2 else 7]
                    if g % 2 == 0 and t >= 2:
                        pe.wait_ge(s["a_low"], t - 1)
                    for jb in range(NT):
                        p0 = PTAT[jb]
                        last = MM(ob[off:off + 64, P * jb:512], va[:, jb, 64 * g:64 * g + 64],
                                  PT[:, g % 2, p0:p0 + 512 - P * jb], start=jb == 0, stop=jb == NT - 1)
                    last.then_inc(s["a_out"], 1)

            def delta():
                dc = dcol
                for i in range(8):
                    pe.wait_ge(s["dn_sq"], i + 1)
                    if i >= 2:
                        pe.wait_ge(s["dn_ln"], i - 1)
                    else:
                        pe.wait_ge(s["a_low"], 4)
                    src = dset[1]["Dm"] if i % 2 else dset[1]["QKT"]
                    MM(bank[i % 2][:, :], blockones[:, :], src[:, :], start=True, stop=True
                       ).then_inc(s["dn_sum"], 1)
                for i in range(8):
                    if i == 0:
                        pe.wait_ge(s["a_biased"], 32)
                    if i >= 2:
                        pe.wait_ge(s["dt_copy"], i - 1)
                    if i < 4:
                        pe.wait_ge(s["dn_scaled"], 5 + i)
                    for n in range(4):
                        last = pe.transpose(bank[4 + i % 2][:, P * n:P * n + P], CO[:, 4 + i, P * n:P * n + P],
                                            ident[:, :])
                    last.then_inc(s["dt_turn"], 1)
                pe.wait_ge(s["dg_pool"], 3)
                MM(bank[6][:, 0:32], upto[:, :], dc[:, 3, :], start=True, stop=True)
                MM(bank[6][:, 32:64], ones[:, :], dc[:, 3, :], start=True, stop=True).then_inc(s["dg_ps"], 1)

                def col(k, i):
                    a = dc[:, k, i:i + 1]
                    return bass.AP(a.tensor, a.offset, [list(a.ap[0]), [0, P]])

                for p in range(4):
                    for e in range(2):
                        h, d, off = 2 * p + e, dset[e], 64 * e
                        B = [bank[4 * e + x] for x in range(4)]
                        if p == 0:
                            pe.wait_ge(s["dn_ln"], 8)
                            pe.wait_ge(s["dt_copy"], 8)
                            pe.wait_ge(s["dg_cum"], 5)
                        else:
                            pe.wait_ge(s["df_low"], p)
                            pe.wait_ge(s["d_vn"], 8 * p)
                            pe.wait_ge(s["d_sn"], 6 * p)
                        for n in range(4):
                            MM(B[0][:, P * n:P * n + P], col(3, 8 * n + h), upto[:, :], start=True, stop=True)
                            last = MM(B[1][:, P * n:P * n + P], col(0, 8 * n + h), ident[:, :], start=True,
                                      stop=True)
                        last.then_inc(s["d_rows"], 1)
                    for e in range(2):
                        h, d, off = 2 * p + e, dset[e], 64 * e
                        B = [bank[4 * e + x] for x in range(4)]
                        pe.wait_ge(s["d_kb"], h + 1)
                        for n in range(4):
                            c = slice(P * n, P * n + P)
                            kT = CO[off:off + 64, 4 + p, c]
                            MM(B[2][:, c], kT, d["kbT"][off:off + 64, c], start=True, stop=True)
                            last = MM(B[3][:, c], kT, CO[off:off + 64, p, c], start=True, stop=True)
                        last.then_inc(s["d_kk"], 1)
                    for e in range(2):
                        h, d, off = 2 * p + e, dset[e], 64 * e
                        pe.wait_ge(s["d_dt0"], h + 1)
                        pe.wait_ge(s["d_er"], h + 1)
                        for n in range(4):
                            c = slice(P * n, P * n + P)
                            last = pe.transpose(bank[4 * e][:, c], d["DT"][:, c], ident[:, :])
                        last.then_inc(s["d_tr"], 1)
                    for l in range(6):
                        for e in range(2):
                            h, d = 2 * p + e, dset[e]
                            B = [bank[4 * e + x] for x in range(4)]
                            pe.wait_ge(s["d_m"], 14 * p + 2 * (l + 1) + e + 1)
                            pe.wait_ge(s["d_dm0"], h + 1)
                            if l:
                                pe.wait_ge(s["d_upd"], 22 * p + 4 * (l - 1) + 2 * e + 2)
                                pe.wait_ge(s["d_xc"], 12 * p + 2 * (l - 1) + e + 1)
                            for n in range(4):
                                c = slice(P * n, P * n + P)
                                last = MM(B[1][:, c], d["MT"][:, c], d["Dm"][:, c], start=True, stop=True)
                            last.then_inc(s["d_x"], 1)
                        for e in range(2):
                            h, d = 2 * p + e, dset[e]
                            B = [bank[4 * e + x] for x in range(4)]
                            pe.wait_ge(s["d_xc"], 12 * p + 2 * l + e + 1)
                            if l == 0:
                                pe.wait_ge(s["d_qk"], h + 1)
                            for n in range(4):
                                c = slice(P * n, P * n + P)
                                if l < 5:
                                    MM(B[2][:, c], d["DT"][:, c], d["X"][:, c], start=True, stop=True)
                                last = MM(B[3][:, c], d["X"][:, c], d["DT"][:, c], start=True, stop=True)
                            last.then_inc(s["d_y"], 1)
                    for e in range(2):
                        h, d, off = 2 * p + e, dset[e], 64 * e
                        B = [bank[4 * e + x] for x in range(4)]
                        pe.wait_ge(s["d_upd"], 22 * p + 20 + e + 1)
                        pe.wait_ge(s["d_tok"], 3 * h + 3)
                        bvt = d["ET"][:, 0:256].rearrange("p (n c) -> p n c", n=4)
                        for n in range(4):
                            c = slice(P * n, P * n + P)
                            MM(B[0][:, 64 * n:64 * n + 64], d["DT"][:, c], bvt[:, n, :], start=True, stop=True)
                            last = MM(B[1][off:off + 64, c], d["kbe"][:, n, :], d["DT"][:, c], start=True, stop=True)
                        last.then_inc(s["d_uw"], 1)
                    for n in range(4):
                        for e in range(2):
                            h, d, off = 2 * p + e, dset[e], 64 * e
                            B = [bank[4 * e + x] for x in range(4)]
                            state = d["ER"][off:off + 64, 64 * ((n - 1) % 2):64 * ((n - 1) % 2) + 64]
                            c = slice(P * n, P * n + P)
                            if n:
                                pe.wait_ge(s["d_sn"], 6 * p + 2 * (n - 1) + e + 1)
                                MM(B[2][:, 64 * n:64 * n + 64], d["X"][off:off + 64, c], state,
                                   start=True, stop=True).then_inc(s["d_ws"], 1)
                        for e in range(2):
                            h, d, off = 2 * p + e, dset[e], 64 * e
                            B = [bank[4 * e + x] for x in range(4)]
                            c = slice(P * n, P * n + P)
                            state = d["ER"][off:off + 64, 64 * ((n - 1) % 2):64 * ((n - 1) % 2) + 64]
                            V = d["MT"][:, 256 + 64 * (n % 2):320 + 64 * (n % 2)]
                            if n == 0:
                                pe.wait_ge(s["d_uwc"], 4 * p + 4)
                                pe.wait_ge(s["d_qe"], h + 1)
                            o = bank[0][off:off + 64, c]
                            if n:
                                MM(o, state, d["kbT"][off:off + 64, c], start=True, stop=False)
                            pe.wait_ge(s["d_vn"], 8 * p + 2 * n + e + 1)
                            if n < 3:
                                MM(B[3][off:off + 64, 64 * n:64 * n + 64], d["kdec"][:, n, :], V,
                                   start=True, stop=True).then_inc(s["d_sp"], 1)
                            last = MM(o, V, d["QKT"][:, c], start=n == 0, stop=True)
                            if n >= 2:
                                last.then_inc(s["d_o"], 1)
                    pe.wait_ge(s["df_sq"], p + 1)
                    MM(bank[5][:, :], blockones[:, :], dset[1]["AT"][:, :], start=True, stop=True
                       ).then_inc(s["df_sum"], 1)

            def scan(st, u, hd, kind, QQ, KK, qr, hs):
                sb4 = scan_before[st]
                nh_ = len(hs)
                for level in range(10):
                    if level == 0:
                        pe.wait_ge(s["lanes"], 8 * u + 1)
                        if nh_ == 2:
                            pe.wait_ge(s["h_low"], hd)
                        elif hd > 1:
                            pe.wait_ge(s["h_low"], hd - 1)
                    if level >= 2:
                        pe.wait_ge(s["decayed"], 16 * u + 2 * (level - 1))
                    for x, (e, pr, V, ST) in enumerate(hs):
                        b0, b1 = bank[4 + 2 * e], bank[5 + 2 * e]
                        o = bank[4 + 2 * e + level % 2]
                        if level == 2:
                            pe.wait_ge(s["scores_copied"], 4 * sb4 + x + 1)
                        elif level in (3, 4, 5, 6, 7, 8):
                            pe.wait_ge(s["scores_put"], 7 * sb4 + nh_ * (level - 3) + x + 1)
                        elif level == 9:
                            pe.wait_ge(s["scores_copied"], 4 * sb4 + nh_ + x + 1)
                            pe.wait_ge(s["scores_put"], 7 * sb4 + nh_ * 6 + x + 1)
                        if level == 0:
                            for j in range(4):
                                c = slice(P * j, P * j + P)
                                last = MM(o[:, c], KK[pr, 0, c], qr(pr, c), start=True, stop=True)
                        elif level <= 7:
                            b = 2 ** (level - 1)
                            for j in range(4):
                                c = slice(P * j, P * j + P)
                                for pl, odd in ((1, 1), (0, 0)):
                                    qv = QQ[pr, pl, c].rearrange("p (m e r) -> p m e r", e=2, r=b)[:, :, odd, :]
                                    ov = o[:, c].rearrange("p (m e r) -> p m e r", e=2, r=b)[:, :, odd, :]
                                    last = MM(ov, KK[pr, 1 - pl, c], qv, start=True, stop=True)
                        elif level == 8:
                            for j in range(4):
                                c = slice(P * j, P * j + P)
                                tq = j ^ 1
                                fwd = tq > j
                                last = MM(b0[:, c], KK[pr, 0 if fwd else 1, c],
                                          QQ[pr, 1 if fwd else 0, P * tq:P * tq + P], start=True, stop=True)
                        else:
                            for j in range(4):
                                fwd = j < 2
                                ob = b0 if fwd else b1
                                t0 = 256 if fwd else 0
                                last = MM(ob[:, 256 * (j % 2):256 * (j % 2) + 256],
                                          KK[pr, 0 if fwd else 1, P * j:P * j + P],
                                          QQ[pr, 1 if fwd else 0, t0:t0 + 256], start=True, stop=True)
                    last.then_inc(s["levels"], 1)
                    fill(st, level)
                for x, (e, pr, V, ST) in enumerate(hs):
                    pe.wait_ge(s["scores_copied"], 4 * sb4 + 2 * nh_ + 2 * x + 2)
                    pe.wait_ge(s["scores_put"], 7 * sb4 + 7 * nh_)
                    for j in range(4):
                        last = MM(bank[4 + 2 * e][:, :], V(j), ST[:, j, :], start=j == 0, stop=j == 3)
                    last.then_inc(s["mixed"], 1)

            def finish(st, e, hd, group):
                b1 = bank[5 + 2 * e]
                bi = b_before[st]
                fill(st, 4 if group else 10)
                if group:
                    pe.wait_ge(s["h_cp"], bi + 1)
                    MM(b1[:, :], ones[:, :], ttt[:, :], start=True, stop=True).then_inc(s["h_mean"], 1)
                    fill(st, 5)
                    pe.wait_ge(s["h_cent"], bi + 1)
                pe.wait_ge(s["h_sq"], hd + 1)
                MM(b1[:, :], ones[:, :], sqt[:, :], start=True, stop=True).then_inc(s["h_sum"], 1)

            BA_STEP = next(m for m, x in enumerate(STEPS) if x[:2] == ("job", "ba"))
            BA_DONE, BA_BANK = JOBS[BA_STEP].act, JOBS[BA_STEP].bank
            pe.wait_ge(s["const_in"], 16 * NCONST)
            pe.wait_ge(s["ones_set"], 2)
            for h in range(8):
                if h >= 2:
                    pe.wait_ge(s["bias_rows"], 2 * (h - 1))
                b0, b1 = bank[4 + 2 * (h % 2)], bank[5 + 2 * (h % 2)]
                MM(b0[:, :], relb[0:33, h, :], onehot[0:33, 0:512], start=True, stop=True)
                MM(b1[:, 0:P], relb[0:33, h, :], onehot[0:33, 512:TOEP], start=True, stop=True
                   ).then_inc(s["bias_ps"], 1)
            nrm = 0
            for n, st in enumerate(STEPS):
                if st[0] == "mod":
                    _, layer, g = st
                    j = JOBS[n]
                    acquire(j)
                    pe.wait_ge(s["ada_mac"], 8 * (6 * layer + g + 1))
                    o = bank[2 * (j.bank % 2)]
                    for m in range(KD):
                        last = MM(o[:, m:m + 1], ada_acc[:, P * m:P * m + P], ones[:, 0:1], start=True, stop=True)
                    last.then_inc(s["mod_ready"], 1)
                elif st[0] == "norm":
                    norm(n, nrm)
                    nrm += 1
                elif st[0] == "job":
                    if st == ("job", "wout", 0, 0):
                        pe.wait_ge(s["a_low"], 4)
                        pe.wait_ge(s["df_low"], 4)
                    if n not in EMBEDDED:
                        gemm(n)
                elif st[0] == "attn":
                    attention(st[1])
                elif st[0] == "delta":
                    delta()
                elif st[0] == "rotary":
                    r = st[1] - 1
                    js = [JOBS[m] for m in range(n) if STEPS[m][0] == "job" and STEPS[m][1] == "bk"]
                    pe.wait_ge(s["act_evac"], js[-1].act)
                    pe.wait_ge(s["r_in"], 64 * (r + 1))
                    pe.wait_ge(s["h_low"], heads_done(n))
                    for x in range(4):
                        t = (bq if x < 2 else bk)[:, x % 2, :]
                        MM(bank[4 + x][:, :], brot[:, 2 * S:2 * S + P], t, start=True, stop=True
                           ).then_inc(s["r_rot"], 1)
                elif st[0] == "mix":
                    _, kind, layer, i = st
                    hd = heads[st]
                    if kind == "b":
                        bi, e = b_before[st], i % 2
                        pr = slice(64 * (i % 2), 64 * (i % 2) + 64)
                        if i == 0:
                            pe.wait_ge(s["r_t"], 12 * layer)
                        pe.wait_ge(s["h_low"], hd - 1)
                        pe.wait_ge(s["act_evac"], evacuated("bg", layer, i // 2))
                        for jb in range(4):
                            if jb >= 2:
                                pe.wait_ge(s["r_ps"], 4 * bi + jb - 1)
                            MM(bank[4 + 2 * e + jb % 2][:, :], bk[pr, i // 2, P * jb:P * jb + P], bq[pr, i // 2, :],
                               start=True, stop=True).then_inc(s["b_scores"], 1)
                            fill(st, jb)
                        pe.wait_ge(s["r_ps"], 4 * bi + 4)
                        for jb in range(4):
                            last = MM(bank[4 + 2 * e][:, :], bv[:, jb, P * i:P * i + P], bST[e][:, jb, :],
                                      start=jb == 0, stop=jb == 3)
                        last.then_inc(s["mixed"], 1)
                        finish(st, e, hd, True)
                        continue
                    u = units[st]
                    pe.wait_ge(s["act_evac"], evacuated("cg", layer, i) if kind == "c" else
                               max(evacuated("abg", layer, i), evacuated("av", layer, i // 2)))
                    if kind == "c":
                        cu = 2 * (layer - 1) + i
                        pe.wait_ge(s["h_low"], heads_done(n))
                        for dr in range(2):
                            pe.wait_ge(s["c_in"], 16 * layer)
                            MM(bank[4 + 2 * dr][:, :], aw[0:32, dr, P * i:P * i + P], clr[0:32, :],
                               start=True, stop=True).then_inc(s["c_logit"], 1)
                        pe.wait_ge(s["c_lanes"], 2 * cu + 2)
                        hs = [(x, slice(64 * x, 64 * x + 64),
                               (lambda j, x=x: cvb2[i][:, j, P * x:P * x + P]), cST[x]) for x in range(2)]
                        scan(st, u, hd, kind, cQQ, cKK, lambda pr, c, i=i: cq[pr, i, c], hs)
                        for x in range(2):
                            finish(st, x, hd + x, False)
                    else:
                        a = aslot[i % 2]
                        hs = [(i % 2, slice(0, P), (lambda j: avb[i // 2][:, j, P * (i % 2):P * (i % 2) + P]), a["ST"])]
                        scan(st, u, hd, kind, a["QQ"], a["KK"], lambda pr, c, a=a: a["q"][pr, c], hs)
                        finish(st, i % 2, hd, False)


SEG = [0, 128, 384, 768]
SBANK = [(5, 384), (6, 0), (5, 0), (4, 0)]
TBANK = [(0, 0), (1, 0), (2, 0), (1, 384)]
PTAT = [0, 512, 1024, 896]


def layouts(inputs):
    def f(name):
        return np.asarray(inputs[name])

    def cols(a):
        return np.ascontiguousarray(a.reshape(-1, P).T)

    stream = np.empty(WTOTAL * P, np.float32)
    for j in LOADS:
        if j.kind == "ada":
            _, layer, g, c = j.src
            a = f("w_ada")[0] if layer == 0 else f("w_ada_2")[layer - 1]
            a = a[2 * P * c:2 * P * (c + 1), ADA_COLS * g:ADA_COLS * (g + 1)].reshape(2, P, ADA_COLS)
        else:
            name, layer, row, units, columns, width = j.src
            each = width // len(columns)
            a = np.concatenate([f(name)[layer][row:row + P * units, c:c + each] for c in columns], 1
                               ).reshape(units, P, width)
        stream[j.at * P:(j.at + j.size) * P].reshape(P, a.shape[0], a.shape[2])[:] = a.transpose(1, 0, 2)

    params = np.zeros((P, NPARAM), np.float32)

    def put(name, a):
        at, n = PARAM[name]
        params[:, at:at + n] = a

    put("c", np.concatenate([cols(f("c")), cols(f("c_2")), cols(f("c_2"))], 1))
    put("b_ada", np.concatenate([cols(f("b_ada")), cols(f("b_ada_2"))], 1))
    for name, src in (("g_attn", "norm_attn_g"), ("g_ffn", "norm_ffn_g"), ("g_final", "final_norm_g"),
                      ("g1", "norm1_g_2"), ("g2", "norm2_g_2"), ("g_out", "norm_f_g_2"), ("lb", "lb_logits_2"),
                      ("b_alpha", "b_alpha_2")):
        put(name, cols(f(src)))
    put("conv", f("conv_w")[0].reshape(4, 12, P).transpose(2, 1, 0).reshape(P, 48))
    put("norm", np.concatenate([cols(np.stack([f(f"norm_{x}_g_2")[l] for x in "abc"])) for l in range(2)], 1))
    put("delta_g", np.tile(f("delta_norm_g").reshape(64), 2)[:, None])
    put("a_log", np.broadcast_to(f("a_log"), (P, 8)))
    put("dt_bias", np.broadcast_to(f("dt_bias"), (P, 8)))
    relb = np.ones((33, 8, P), np.float32)
    relb[:32] = np.broadcast_to(f("rel_bias")[:, :, None], (32, 8, P))
    walpha = np.zeros((2, 32, 2, CW), np.float32)
    for d in range(2):
        walpha[:, 16 * d:16 * d + 16, d] = f("w_alpha_2")[:, d]
    x = np.ascontiguousarray(f("x")[0].T.reshape(KD, P, S).transpose(1, 0, 2))
    return {"wstream": stream, "x": x, "params": params, "relb": relb, "walpha": walpha,
            "consts": CONST_ARRAY}


def kernel(**inputs):
    import concourse.bacc as bacc
    from concourse.bass_utils import run_bass_kernel_spmd

    arrays = {f"in_{k}_dram": v for k, v in layouts(inputs).items()}
    nc = bacc.Bacc("TRN2", target_bir_lowering=False, num_devices=1)
    args = [nc.dram_tensor(k, v.shape, mybir.dt.from_np(v.dtype), kind="ExternalInput").ap()
            for k, v in arrays.items()]
    out = nc.dram_tensor("out_0_dram", (P, KD, S), F32, kind="ExternalOutput").ap()
    program(nc, *args, out)
    r = run_bass_kernel_spmd(nc, [arrays], core_ids=[0])
    y = r.results[0]["out_0_dram"]
    return np.ascontiguousarray(y.transpose(2, 1, 0).reshape(1, S, D))
```

```python
import math
from contextlib import ExitStack

import numpy as np

import concourse.bass as bass
from concourse import mybir

F32 = mybir.dt.float32
F32R = mybir.dt.float32r
U8 = mybir.dt.uint8
ALU = mybir.AluOpType
ACT = mybir.ActivationFunctionType

P = 128
S = 512
D = 1024
KD = D // P
NT = S // P
FF = 2816
KF = FF // P
CW = 256
UNITS = 8
SLOT = UNITS * CW
ADA_COLS = 1024
LAYERS2 = 2
EPS = 1e-6
NEG = -1e30
TINY = 1e-30
TOEP = P + S
RAW = 3

PARAM = {}


def _param_columns():
    at = 0
    for name, n in (("c", 24), ("b_ada", 144), ("g_attn", 8), ("g_ffn", 8), ("g_final", 8), ("g1", 16),
                    ("g2", 16), ("g_out", 8), ("conv", 48), ("lb", 8), ("norm", 24), ("b_alpha", 8),
                    ("delta_g", 1), ("a_log", 8), ("dt_bias", 8)):
        PARAM[name] = (at, n)
        at += n
    return at


NPARAM = _param_columns()

IN1 = ["qa", "qa", "ka", "ka", "va", "va"] + ["conv"] * 6 + ["zd", "zd"]


FFN_NORM = (2, 5, 7)


def plan():
    steps, filled = [], {}
    ada = [(layer, g, c) for layer in range(3) for g in range(6) for c in range(4)]
    pending = []

    def ada_chunk():
        if pending:
            steps.append(("mod",) + pending.pop())
        if ada:
            layer, g, c = ada.pop(0)
            steps.append(("ada", layer, g, c))
            if c == 3:
                pending.append((layer, g))

    def job(kind, layer, i, every=2):
        steps.append(("job", kind, layer, i))
        whole = kind != "down" or i % 3 == 2
        if whole and (kind == "down" or sum(x[0] == "job" for x in steps) % every == 0):
            ada_chunk()

    def mix(kind, layer, i, fill=()):
        start = len(steps)
        for k, c in fill:
            steps.append(("job", k, layer, c))
        filled[("mix", kind, layer, i)] = list(range(start, len(steps)))
        steps.append(("mix", kind, layer, i))

    def ffn(layer):
        for f in range(11):
            job("gate", layer, f)
            job("up", layer, f)
        for c in range(4):
            for part in range(3):
                job("down", layer, 3 * c + part)
                if c and part == 0:
                    steps.append(("square", FFN_NORM[layer], c - 1))

    def project(layer, norm):
        for c in range(4):
            job("wout", layer, c, every=1 if layer == 0 else 2)
            if c:
                steps.append(("square", norm, c - 1))

    for _ in range(8):
        ada_chunk()
    steps.append(("mod",) + pending.pop())
    steps.append(("norm", 0))
    for i, kind in enumerate(IN1):
        if i == 6:
            job("ba", 0, 0)
            steps.append(("gates", 0))
        job(kind, 0, i, every=2 if kind == "conv" else 1)
        if i < 4:
            steps += [("bias", 2 * i), ("bias", 2 * i + 1)]
        if kind == "conv":
            steps.append(("conv", i - 6))
        steps += {6: [("gates", 1)], 7: [("gates", 2)], 8: [("gates", 3), ("length", 0)],
                  9: [("gates", 4), ("length", 1), ("unit", 0)], 10: [("gates", 5), ("length", 2), ("unit", 1)],
                  11: [("length", 3), ("unit", 2)], 12: [("conv", 6), ("unit", 3)]}.get(i, [])
    for h in range(10):
        steps.append(("attn", h))
    steps.append(("delta",))
    project(0, 1)
    steps.append(("norm", 1))
    ffn(0)
    steps.append(("norm", "renorm"))
    for L in range(1, LAYERS2 + 1):
        steps.append(("norm", 2 * L))
        for kind in ("aqf", "abg", "av"):
            job(kind, L, 0)
        mix("a", L, 0, (("aqf", 1), ("abg", 1)))
        mix("a", L, 1, (("aqf", 2), ("abg", 2), ("av", 1)))
        mix("a", L, 2, (("aqf", 3), ("abg", 3), ("ga", 0)))
        mix("a", L, 3, (("ga", 1), ("ga", 2)))
        job("ga", L, 3)
        for c in range(4):
            job("pa", L, c)
        for kind in ("bq", "bk", "bv"):
            job(kind, L, 0)
        steps.append(("rotary", L))
        job("bg", L, 0)
        for h, fill in enumerate((("bv", 1), ("bg", 1), ("gb", 0), ("gb", 1))):
            mix("b", L, h, (fill,))
        for kind, c in (("gb", 2), ("pb", 0), ("pb", 1), ("cq", 0), ("ck", 0), ("cl", 0)):
            job(kind, L, c)
        steps.append(("decay", L, 0))
        job("cv", L, 0)
        job("cg", L, 0)
        mix("c", L, 0, (("pb", 2), ("gb", 3), ("pb", 3)))
        job("cv", L, 1)
        steps.append(("decay", L, 1))
        job("cg", L, 1)
        mix("c", L, 1, (("gc", 0), ("gc", 1), ("gc", 2)))
        job("gc", L, 3)
        for c in range(4):
            job("pc", L, c)
            steps.append(("merge", L, c))
        project(L, 2 + 2 * L)
        steps.append(("norm", 1 + 2 * L))
        ffn(L)
    assert not ada and not pending
    steps.append(("norm", "final"))
    return steps, filled


SLOTS = {"a": (9, 9, 11, 11), "b": (6,) * 4, "c": (10, 10)}
PARTS = 4


SPLIT2 = {"aq": 0, "af": 512, "ab": 1024, "av": 1536, "ag": 2048, "bq": 2560, "bk": 2816, "bv": 3072,
          "bg": 3584, "cq": 4096, "ck": 4352, "cv": 4608, "cg": 5120, "cl": 5632, "ga": 5664, "gb": 6688,
          "gc": 7712}
GATE_AT = {"a": [24, 26, 38, 40, 42, 44, 46, 48], "b": [38, 42, 54, 56, 32, 34, 32, 34],
           "c": [48, 50, 38, 42, 46, 88, 32, 34]}
TOKEN_MAJOR = {"va", "av", "bv", "cv"}


def source(kind, layer, i):
    w = "" if layer == 0 else "_2"
    l2 = max(layer - 1, 0)
    if kind in ("qa", "ka", "va", "conv", "zd"):
        return "w_in", 0, 0, 8, (CW * i,), CW
    if kind == "ba":
        return "w_in", 0, 0, 8, (CW * len(IN1),), 16
    if kind == "cl":
        return "w_in_2", l2, 0, 8, (SPLIT2["cl"],), 32
    if kind in ("aqf", "abg"):
        return "w_in_2", l2, 0, 8, tuple(SPLIT2["a" + x] + P * i for x in kind[1:]), CW
    if kind in SPLIT2:
        return "w_in_2", l2, 0, 8, (SPLIT2[kind] + CW * i,), CW
    if kind in ("pa", "pb", "pc"):
        return f"w_{kind}_2", l2, 0, 4, (CW * i,), CW
    if kind == "wout":
        return "w_out" + w, l2, 0, 8, (CW * i,), CW
    if kind in ("gate", "up"):
        if layer == 0:
            return "w_" + kind, 0, 0, 8, (CW * i,), CW
        return "w_ffn_in_2", l2, 0, 8, (CW * i + (FF if kind == "up" else 0),), CW
    c, part = divmod(i, 3)
    return ("w_down" if layer == 0 else "w_ffn_out_2"), l2, 1024 * part, (8, 8, 6)[part], (CW * c,), CW


class Job:
    w = None


def jobs_of(steps):
    by_step, freed = {}, []
    w = bank = ada = 0
    act = dve = 0
    for n, s in enumerate(steps):
        if s[0] not in ("job", "ada", "mod"):
            continue
        j = Job()
        by_step[n] = j
        if s[0] == "mod":
            j.kind, j.bank = "mod", bank
            bank += 1
            dve += 1
            freed.append(("dve", dve))
            j.dve = dve
            continue
        if s[0] == "ada":
            j.kind, j.size = "ada", SLOT
            j.src = ("ada",) + s[1:]
            j.ada = ada
            ada += 1
            continue
        _, kind, layer, i = s
        j.kind, j.layer, j.i = kind, layer, i
        j.src = source(kind, layer, i)
        j.units, j.width = j.src[3], j.src[5]
        j.size, j.w = j.units * j.width, w
        w += 1
        j.first = kind != "down" or i % 3 == 0
        j.last = kind != "down" or i % 3 == 2
        j.bank = bank
        j.act0, j.dve0 = act, dve
        if j.last:
            bank += 1
            if kind in ("up", "pa", "pb", "pc", "wout", "down"):
                dve += 2
                freed.append(("dve", dve))
            else:
                act += {"aqf": 3, "abg": 3, "ba": 1, "cl": 1}.get(kind, 2)
                freed.append(("act", act))
        j.act, j.dve = act, dve
    products = [j for j in by_step.values() if j.w is not None]
    loads, at = [], 0
    for n, s in enumerate(steps):
        if s[0] == "ada":
            loads.append(by_step[n])
        elif s == ("norm", 0):
            loads.append(products[0])
        elif s[0] == "job" and by_step[n].w + 1 < len(products):
            loads.append(products[by_step[n].w + 1])
    for li, j in enumerate(loads):
        j.load, j.at = li, at
        at += j.size
    return loads, by_step, products, freed, at


STEPS, FILLED = plan()
EMBEDDED = {n for x in FILLED.values() for n in x}
LOADS, JOBS, PRODUCTS, FREED, WTOTAL = jobs_of(STEPS)


CONST = {}


def constants():
    p = np.arange(P)
    blocks = {"ident": np.eye(P), "blockones": (p[:, None] // 64 == p[None] // 64),
              "upto": (p[:, None] <= p[None])}
    perm = np.zeros((P, P))
    for d in range(P):
        if d % 64 < 32:
            perm[d + 32, d] = -1.0
        else:
            perm[d - 32, d] = 1.0
    blocks["perm"] = perm
    inv = (10000.0 ** (-np.arange(0, 64, 2, dtype=np.float32) / np.float32(64))).astype(np.float32)
    ang = (np.arange(S, dtype=np.float32)[None] * inv[:, None]).astype(np.float32).astype(np.float64)
    blocks["cos"] = np.cos(ang)[p % 32]
    blocks["sin"] = np.sin(ang)[p % 32]
    gamma = np.zeros((P, 4, 896))
    dist = np.arange(896)[None] - p[:, None] - 384
    for h in range(4):
        fwd, bwd = (math.log1p(-2.0 ** (-5.0 - x)) for x in (h, 3 - h))
        gamma[:, h] = np.exp(np.where(dist >= 0, fwd * dist, -bwd * dist))
    blocks["gamma"] = gamma.reshape(P, -1)
    onehot = np.zeros((P, TOEP))
    for x in range(TOEP):
        dd = 511 - x
        n = (dd <= 128) + (dd % 4 == 0) + (dd % 16 == 0) if dd >= 0 else 0
        if n:
            b = dd if dd < 16 else min(31, 16 + int(np.float32(np.log(np.float32(dd / 16))) / np.float32(
                math.log(128)) * np.float32(16)))
            onehot[b, x] = 1.0
            onehot[32, x] = math.log(n)
        else:
            onehot[32, x] = NEG
    blocks["onehot"] = onehot
    masks = np.zeros((P, 7, P))
    r, c = p[:, None], p[None]
    for l in range(7):
        b = 2 ** l
        masks[:, l] = (r // (2 * b) == c // (2 * b)) & (r // b != c // b)
    blocks["sibling"] = masks.reshape(P, -1)
    blocks["before"] = (masks * (r < c)[:, None]).reshape(P, -1)
    at = 0
    for k, v in blocks.items():
        CONST[k] = (at, v.shape[1])
        at += v.shape[1]
    return np.concatenate([v.astype(np.float32) for v in blocks.values()], 1)


CONST_ARRAY = constants()


def program(nc, wstream, x_in, params_in, relb_in, walpha_in, const_in, out):
    ctx = ExitStack()
    with ctx:
        def sem(name):
            return ctx.enter_context(nc.semaphore(name))

        base = [16512]

        def sb(name, shape, dt=F32):
            t = nc.alloc_sbuf_tensor_at(name, [P] + list(shape), dt, offset=base[0])
            n = int(np.prod(shape)) * (1 if dt == U8 else 4)
            base[0] += (n + 31) // 32 * 32
            return t

        xT = sb("xT", [KD, S])
        HH = sb("HH", [KD, S], F32R)
        HL = sb("HL", [KD, S], F32R)
        raw = sb("raw", [RAW, SLOT])
        WH = sb("WH", [2, SLOT], F32R)
        WL = sb("WL", [2, SLOT], F32R)
        ada_acc = sb("ada_acc", [ADA_COLS])
        params = sb("params", [NPARAM])
        ident = sb("ident", [P])
        ones = sb("ones", [P])
        masks = sb("masks", [7, P], U8)
        mod = sb("mod", [3, 6, KD])
        lbound = sb("lbound", [2, 4])
        rest = sb("rest", [2, 4])
        cact = sb("cact", [24])
        acol = sb("acol", [KD])
        eps = sb("eps", [1])
        small = sb("small", [8, 4])
        table_col = sb("table_col", [1])
        ARENA = base[0]

        def arena(name, kb, shape, dt=F32):
            off = ARENA + int(round(kb * 1024))
            assert off % 32 == 0
            assert off + int(np.prod(shape)) * 4 <= 229344, (name, off, ARENA)
            return nc.alloc_sbuf_tensor_at(name, [P] + list(shape), dt, offset=off)

        CVP = S + 3
        relb = arena("relb", 0, [8, P])
        onehot = arena("onehot", 4, [TOEP])
        bias_row = arena("bias_row", 8, [2, TOEP])
        zs = arena("zs", 0, [4, S])
        cvb = arena("cvb", 8, [2, 2, CVP])
        CO = arena("CO", 16.25, [12, S])
        sibling = arena("sibling", 16.25, [7, P])
        qa = arena("qa", 40.25, [4, S])
        ka = arena("ka", 48.25, [4, S])
        va = arena("va", 56.25, [NT, S])
        toep = arena("toep", 64.25, [3, S])
        Sx = arena("Sx", 70.25, [2, 1280])
        PT = arena("PT", 80.25, [2, 1280])
        ba = arena("ba", 90.25, [NT, 16])
        amax = arena("amax", 90.5, [2, 4])
        anmax = arena("anmax", 90.5625, [2, 4])
        asum = arena("asum", 90.625, [2, 4])
        arsum = arena("arsum", 90.6875, [2, 4])
        blockones = arena("blockones", 92, [P])
        upto = arena("upto", 92.5, [P])
        dcol = arena("dcol", 93, [12, 32])
        before03 = arena("before03", 76.25, [4, P])
        before46 = arena("before46", 90.25, [3, P])
        csq = arena("csq", 70.25, [2, 2, S])
        crs = arena("crs", 78.25, [2, 2, S])
        ktok = arena("ktok", 40.25, [NT, S])
        vtok = arena("vtok", 48.25, [NT, S])
        dset = []
        for e in range(2):
            names = ["ER", "ET", "kbT", "AT", "QKT", "Dm", "DT", "X", "MT"]
            where = [56.25 + 2 * i for i in range(9)] if e == 0 else \
                [8 + 2 * i for i in range(4)] + [78.25 + 2 * i for i in range(5)]
            d = {n: arena(f"{n}{e}", w, [S]) for n, w in zip(names, where)}
            w0 = 74.25 if e == 0 else 88.25
            d["kbe"] = arena(f"kbe{e}", w0, [NT, 64])
            d["kdec"] = arena(f"kdec{e}", w0 + 1, [NT, 64])
            dset.append(d)
        YH = arena("YH", 0, [4, S], F32R)
        YL = arena("YL", 8, [4, S], F32R)
        macc = arena("macc", 16, [KD, S])
        sqt = arena("sqt", 32, [S])
        rrt = arena("rrt", 34, [S])
        ttt = arena("ttt", 36, [S])
        agate = arena("agate", 16, [4, S])
        aslot = []
        for e in range(2):
            o = 38 + 28 * e
            aslot.append({n: arena(f"a_{n}{e}", o + w, sh) for n, w, sh in (
                ("q", 0, [S]), ("QQ", 2, [2, S]), ("KK", 6, [2, S]), ("G1", 10, [2, S]), ("GT", 14, [1024]),
                ("ST", 18, [NT, S]))})
        avb = [arena(f"av{x}", 24 + 4 * x, [NT, CW]) for x in range(2)]
        bq = arena("bq", 38, [2, S])
        bk = arena("bk", 42, [2, S])
        bv = arena("bv", 46, [NT, S])
        bg = arena("bg", 54, [4, S])
        bgam = arena("bgam", 62, [4, 896])
        bST = [arena(f"bST{e}", 76.25 + 8 * e, [NT, S]) for e in range(2)]
        brot = arena("brot", 76.25, [2 * S + P])
        btmp = arena("btmp", 84.25, [S])
        cq = arena("cq", 38, [2, S])
        ck = arena("ck", 42, [2, S])
        clr = arena("clr", 46, [S])
        cvb2 = [arena("cv0", 48, [NT, CW]), arena("cv1", 90, [NT, CW])]
        cg = arena("cg", 52, [2, S])
        cG1 = arena("cG1", 56, [2, S])
        cQQ = arena("cQQ", 60, [2, S])
        cKK = arena("cKK", 64, [2, S])
        cGT = arena("cGT", 68, [1024])
        cST = [arena(f"cST{e}", 72 + 8 * e, [NT, S]) for e in range(2)]
        aw = arena("aw", 88, [2, CW])
        c_x = arena("c_x", 72, [2, S])
        c_e = arena("c_e", 80, [2, S])
        gate_at = {kb: arena(f"gate_at_{kb}", kb, [S]) for kb in sorted({x for v in GATE_AT.values() for x in v})}
        own = tuple(t[:, :] for t in (sqt, rrt, ttt))
        TEMPS = {"a": [own], "b": [own], "c": [own, (cQQ[:, 0, :], cQQ[:, 1, :], cKK[:, 0, :])]}
        AH = arena("AH", 0, [KF, S], F32R)
        AL = arena("AL", 44, [KF, S], F32R)
        SG = arena("SG", 88, [2, S])
        nsq = arena("nsq", 88, [2, S])
        nr = arena("nr", 80, [S])
        nt = arena("nt", 82, [2, S])
        ost = arena("ost", 0, [KD, S])

        bank = [ctx.enter_context(nc.psum_tensor(f"bank{i}", [P, 512], F32)) for i in range(8)]
        bias_dram = nc.dram_tensor("bias_dram", [8, P, TOEP], F32).ap()

        names = """ba_turned ba_in table params_in const_in before_in ones_set raw0 raw1 raw2 w_rounded w_split gemm_done ada_mac
            mod_ready act_evac dve_evac cact_ready lb_max lb_exp lb_dve bias_ps bias_rows
            bias_stored toep0 toep1 toep2 n_square n_sum n_ln n_rstd n_acol n_scaled n_high
            n_low renormed out_ready out_stored conv_pad conv_step conv_silu a_scores a_biased
            a_nmax a_exp a_rsum a_norm a_turned a_turn_copied a_out a_high a_low f_high f_low
            dn_sq dn_sum dn_ln dn_r dn_scaled dt_turn dt_copy dg_act dg_pool dg_ps dg_cum d_rows
            d_er d_et d_etexp d_etmask d_kb d_kk d_at d_qk d_m d_dt0 d_tr d_dm0 d_x d_xc d_y
            d_upd d_tok d_qe d_uw d_uwc d_ws d_vn d_sp d_sn d_o df_sq df_sum df_ln df_r df_t
            df_y df_high df_low prep lanes levels decayed scores_put scores_copied mixed h_sq
            h_sum h_ln h_r h_t h_y h_high h_low h_cp h_mean h_cent r_in r_rot r_ps r_t b_scores
            c_in c_logit c_act c_dve c_lanes m_add m_high m_low""".split()
        s = {n: sem(n) for n in names}
        raw_in = [s["raw0"], s["raw1"], s["raw2"]]
        toep_in = [s["toep0"], s["toep1"], s["toep2"]]

        def par(name, i=0, n=1):
            a = PARAM[name][0]
            return params[:, a + i:a + i + n]

        def bc(ap, *dims):
            return bass.AP(ap.tensor, ap.offset, [list(ap.ap[0])] + [list(d) for d in dims])

        def lanes(t, b):
            return bc(t[:, :, :], [2 * b, S // (2 * b)], [S + b, 2], [1, b])

        def lane_gates(g1, gt, b, keys):
            n = S // b
            g = g1[:, :, :] if b == 1 else gt[:, :]
            at = 0 if b == 1 else tree_at(b)
            off, step = (n + 1, -(n + 1)) if keys else (1, n - 1)
            return bass.AP(g.tensor, g.offset + at + off, [list(g.ap[0]), [2, n // 2], [step, 2], [0, b]])

        def tree_at(b):
            return sum(2 * (S // x) for x in (2, 4, 8, 16, 32, 64, 128) if x < b)

        def tree_step(g1, gt, b):
            n = S // b
            g = g1[:, :, :] if b == 1 else gt[:, :]
            at = 0 if b == 1 else tree_at(b)
            src = [bass.AP(g.tensor, g.offset + at + x, [list(g.ap[0]), [n, 2], [2, n // 2]]) for x in (0, 1)]
            t = gt[:, :]
            dst = bass.AP(t.tensor, t.offset + tree_at(2 * b), [list(t.ap[0]), [n // 2, 2], [1, n // 2]])
            return dst, src[0], src[1]

        units, heads = {}, {}
        nu = nh = 0
        for st in STEPS:
            if st[0] == "mix":
                kind, layer, i = st[1:]
                k = 2 if kind == "c" else 1
                if kind != "b":
                    units[st] = nu
                    nu += 1
                heads[st] = nh
                nh += k
        scan_before, b_before = {}, {}
        ns = nb = 0
        for st in STEPS:
            if st[0] == "mix":
                scan_before[st] = ns
                b_before[st] = nb
                if st[1] == "b":
                    nb += 1
                else:
                    ns += 2 if st[1] == "c" else 1

        def heads_done(n):
            return sum((2 if x[1] == "c" else 1) for x in STEPS[:n] if x[0] == "mix")

        def adds_before(n):
            return sum(2 for x in STEPS[:n] if x[0] == "job" and x[1] in ("pa", "pb", "pc"))

        def gemm_before(n):
            return sum(1 for x in STEPS[:n] if x[0] == "job")

        NORM_MOD = [(0, 0), (0, 3), None, (1, 0), (1, 3), (2, 0), (2, 3), None]
        NORM_G = [("g_attn", 0), ("g_ffn", 0), ("g_final", 0), ("g1", 0), ("g2", 0), ("g1", 8), ("g2", 8),
                  ("g_out", 0)]
        RENORM, FINAL = 2, 7

        def modulated(r):
            return r - (r > RENORM)

        def ffns(r):
            return (0, 0, 1, 1, 1, 2, 2, 3)[r]


        LATE = [range(KD) if r in (0, RENORM + 1) else range(KD - 2, KD) for r in range(FINAL + 1)]
        def forgets(st):
            return sum(1 for x in STEPS[:STEPS.index(st) + 1] if x[:2] == ("mix", "a"))

        NORM_STEP = [n for n, x in enumerate(STEPS) if x[0] == "norm"]

        def tile_count(r, k):
            js = [JOBS[m] for m in range(NORM_STEP[r]) if m in JOBS and JOBS[m].kind in ("wout", "down")
                  and JOBS[m].last][-4:]
            return js[k // 2].dve - 1 + k % 2 if js else 0

        def mod_ready_count(layer, group):
            for m, x in enumerate(STEPS):
                if x[:3] == ("mod", layer, group):
                    return JOBS[m].dve
            raise KeyError

        def parts(st, slot):
            jobs, slots = FILLED[st], SLOTS[st[1]][st[3]]
            total = PARTS * len(jobs)
            if slot < 0 or slot >= slots:
                return []
            return [(jobs[x // PARTS], x % PARTS) for x in range(total * slot // slots, total * (slot + 1) // slots)]

        def evacuated(*job):
            return JOBS[STEPS.index(("job",) + job)].act

        ATTENTION = STEPS.index(("attn", 0))
        NCONST = 7
        block = ctx.enter_context(nc.Block())

        @block.sync
        def _(sp):
            def const(name, dst):
                a, n = CONST[name]
                return dst, const_in[:, a:a + n]

            sp.dma_start(params[:, :], params_in).then_inc(s["params_in"], 16)

            def load(li):
                j = LOADS[li]
                if li >= RAW:
                    o = LOADS[li - RAW]
                    if o.kind == "ada":
                        sp.wait_ge(s["ada_mac"], 2 * (o.ada + 1))
                    else:
                        sp.wait_ge(s["w_split"], 2 * (o.w + 1))
                sp.dma_start(raw[:, li % RAW, 0:j.size],
                             wstream[j.at * P:(j.at + j.size) * P].rearrange("(p n) -> p n", p=P)
                             ).then_inc(raw_in[li % RAW], 16)

            nxt = 0
            for _ in range(RAW):
                load(nxt)
                nxt += 1
            sp.dma_start(xT[:, :, :], x_in).then_inc(s["const_in"], 16)
            for dst, src in (const("ident", ident[:, :]), const("sibling", sibling[:, :, :].rearrange("p l j -> p (l j)")),
                             (relb[0:33, :, :], relb_in),
                             const("onehot", onehot[:, :]), const("blockones", blockones[:, :]),
                             const("upto", upto[:, :])):
                sp.dma_start(dst, src).then_inc(s["const_in"], 16)
            while nxt < len(LOADS):
                load(nxt)
                nxt += 1
            sp.wait_ge(s["out_ready"], 8)
            sp.dma_start(out, ost[:, :, :]).then_inc(s["out_stored"], 16)
            sp.wait_ge(s["out_stored"], 16)

        @block.gpsimd
        def _(pool):
            pool.memset(ones[:, :], 1.0).then_inc(s["ones_set"], 1)
            pool.memset(eps[:, :], EPS).then_inc(s["ones_set"], 1)
            pool.wait_ge(s["const_in"], 16 * NCONST)
            pool.tensor_copy(masks[:, :, :], sibling[:, :, :]).then_inc(s["ones_set"], 1)

            def bias(h):
                pool.wait_ge(s["bias_rows"], 2 * (h + 1))
                pool.dma_start(bias_dram[h], bias_row[:, h % 2, :]).then_inc(s["bias_stored"], 16)
                pool.wait_ge(s["bias_stored"], 16 * (h + 1))

            def toeplitz(h):
                if h >= 3:
                    pool.wait_ge(s["a_biased"], 4 * (h - 2))
                skew = bass.AP(bias_dram.tensor, bias_dram.offset + h * P * TOEP + P - 1,
                               [[TOEP - 1, P], [1, S]])
                pool.dma_start(toep[:, h % 3, :], skew).then_inc(s[f"toep{h % 3}"], 16)

            def lane_products(u, st, g1, gt, q, QQ):
                pool.tensor_tensor(QQ[:, :, :], bc(q, [0, 2], [1, S]), g1[:, :, :], ALU.mult
                                   ).then_inc(s["lanes"], 1)
                b = 1
                for k in range(7):
                    if k:
                        pool.wait_ge(s["lanes"], 8 * u + 1 + k)
                    dst, i0, i1 = tree_step(g1, gt, b)
                    pool.tensor_tensor(dst, i0, i1, ALU.mult).then_inc(s["lanes"], 1)
                    b *= 2

            for n, st in enumerate(STEPS):
                if st[0] == "length":
                    c = st[1]
                    pool.wait_ge(s["conv_silu"], 2 * c + 2)
                    if c >= 2:
                        pool.wait_ge(s["dn_sum"], c - 1)
                    pool.tensor_tensor(csq[:, c % 2, :, :], CO[:, 2 * c:2 * c + 2, :], CO[:, 2 * c:2 * c + 2, :],
                                       ALU.mult).then_inc(s["dn_sq"], 1)
                if st[0] == "bias":
                    bias(st[1])
                if st[0] == "conv" and st[1] == 0:
                    for h in range(3):
                        toeplitz(h)
                if st[:2] == ("job", "bq"):
                    pool.wait_ge(s["mixed"], heads_done(n))
                    pool.wait_ge(s["h_low"], heads_done(n))
                    for name, dst in (("gamma", bgam[:, :, :].rearrange("p h u -> p (h u)")),
                                      ("cos", brot[:, 0:S]), ("sin", brot[:, S:2 * S]),
                                      ("perm", brot[:, 2 * S:2 * S + P])):
                        a, c = CONST[name]
                        pool.dma_start(dst, const_in[:, a:a + c]).then_inc(s["r_in"], 16)
                if st[:2] == ("job", "cq"):
                    pool.wait_ge(s["mixed"], heads_done(n))
                    pool.wait_ge(s["h_low"], heads_done(n))
                    pool.dma_start(aw[0:32, :, :], walpha_in[st[2] - 1]).then_inc(s["c_in"], 16)
                if st[0] == "attn" and st[1] < 8:
                    h = st[1]
                    if h >= 1 and h + 2 < 8:
                        toeplitz(h + 2)
                if st[0] == "delta":
                    a, c = CONST["before"]
                    pool.wait_ge(s["a_turned"], 8)
                    pool.wait_ge(s["dg_act"], 1)
                    pool.wait_ge(s["dg_pool"], 1)
                    pool.dma_start(before03[:, :, :].rearrange("p l j -> p (l j)"), const_in[:, a:a + 4 * P]
                                   ).then_inc(s["before_in"], 16)
                    pool.dma_start(before46[:, :, :].rearrange("p l j -> p (l j)"), const_in[:, a + 4 * P:a + 7 * P]
                                   ).then_inc(s["before_in"], 16)
                    pool.wait_ge(s["before_in"], 32)
                    for p in range(4):
                        for e in range(2):
                            h, d = 2 * p + e, dset[e]
                            pool.wait_ge(s["d_etexp"], h + 1)
                            pool.tensor_tensor(d["ET"][:, :].rearrange("p (n i) -> p n i", n=4),
                                               d["ET"][:, :].rearrange("p (n i) -> p n i", n=4),
                                               bc(upto[:, :], [0, 4], [1, P]), ALU.mult
                                               ).then_inc(s["d_etmask"], 1)
                        for l in range(7):
                            for e in range(2):
                                h, d = 2 * p + e, dset[e]
                                pool.wait_ge(s["d_at"], h + 1)
                                if l == 1:
                                    pool.wait_ge(s["d_dt0"], h + 1)
                                elif l > 1:
                                    pool.wait_ge(s["d_x"], 12 * p + 2 * (l - 2) + e + 1)
                                pool.tensor_tensor(d["MT"][:, :].rearrange("p (n i) -> p n i", n=4),
                                                   d["AT"][:, :].rearrange("p (n i) -> p n i", n=4),
                                                   bc((before03[:, l, :] if l < 4 else before46[:, l - 4, :]), [0, 4],
                                                      [1, P]), ALU.mult
                                                   ).then_inc(s["d_m"], 1)
                if st[0] == "mix" and st[1] == "a":
                    layer, h = st[2:]
                    u, a = units[st], aslot[h % 2]
                    pool.wait_ge(s["prep"], 3 * forgets(st))
                    lane_products(u, st, a["G1"], a["GT"], a["q"][:, :], a["QQ"])
                if st[0] == "decay":
                    layer, pr = st[1:]
                    u = units["mix", "c", layer, pr]
                    cu = 2 * (layer - 1) + pr
                    pool.wait_ge(s["c_lanes"], 2 * cu + 2)
                    lane_products(u, st, cG1, cGT, cq[:, pr, :], cQQ)

        @block.scalar
        def _(act):
            A = act.activation

            ready = [0]

            def ready_ln():
                if ready[0]:
                    act.wait_ge(s["table"], ready[0])
                A(table_col[:, :], eps[:, :], ACT.Ln).then_inc(s["table"], 1)
                ready[0] += 1

            def split(wi):
                j = PRODUCTS[wi]
                act.wait_ge(raw_in[j.load % RAW], 16 * (j.load // RAW + 1))
                if wi > 1:
                    act.wait_ge(s["gemm_done"], wi - 1)
                A(WH[:, wi % 2, 0:j.size], raw[:, j.load % RAW, 0:j.size], ACT.Copy).then_inc(s["w_rounded"], 1)

            act.wait_ge(s["params_in"], 16)
            act.wait_ge(s["ones_set"], 2)
            A(cact[:, :], par("c", 0, 24), ACT.Silu).then_inc(s["cact_ready"], 1)
            act.wait_ge(s["lb_dve"], 2)
            A(small[:, 2:4, :], small[:, 0:2, :], ACT.Exp).then_inc(s["lb_exp"], 1)

            def bias(h):
                act.wait_ge(s["bias_ps"], h + 1)
                if h >= 2:
                    act.wait_ge(s["bias_stored"], 16 * (h - 1))
                A(bias_row[:, h % 2, 0:512], bank[4 + 2 * (h % 2)][:, :], ACT.Copy).then_inc(s["bias_rows"], 1)
                A(bias_row[:, h % 2, 512:TOEP], bank[5 + 2 * (h % 2)][:, 0:P], ACT.Copy
                  ).then_inc(s["bias_rows"], 1)

            def squares(r, tiles):
                for k in tiles:
                    if r == 0:
                        act.wait_ge(s["const_in"], 16 * NCONST)
                    else:
                        act.wait_ge(s["dve_evac"], tile_count(r, k))
                    if r == RENORM + 1:
                        act.wait_ge(s["renormed"], k + 1)
                    if k >= 2:
                        act.wait_ge(s["n_sum"], 8 * r + k - 1)
                    elif ffns(r):
                        act.wait_ge(s["f_low"], 22 * ffns(r))
                    A(nsq[:, k % 2, :], xT[:, k, :], ACT.Square).then_inc(s["n_square"], 1)

            def norm(n, r):
                squares(r, LATE[r])
                ready_ln()
                act.wait_ge(s["n_sum"], 8 * r + 8)
                A(nr[:, :], bank[4][:, :], ACT.Ln, bias=eps[:, :], scale=1.0 / D).then_inc(s["n_ln"], 1)
                act.wait_ge(s["n_ln"], r + 1)
                A(nr[:, :], nr[:, :], ACT.Exp, scale=-0.5).then_inc(s["n_rstd"], 1)
                if NORM_MOD[r]:
                    layer, g = NORM_MOD[r]
                    if gemm_before(n):
                        act.wait_ge(s["gemm_done"], gemm_before(n))
                    for k in range(KD):
                        act.wait_ge(s["n_scaled"], 8 * modulated(r) + k + 1)
                        A(HH[:, k, :], nt[:, k % 2, :], ACT.Identity, bias=mod[:, layer, g, k:k + 1]
                          ).then_inc(s["n_high"], 1)

            def evacuate(n, j, kind, layer, i):
                act.wait_ge(s["gemm_done"], j.w + 1)

                def put(dst, src, f=ACT.Copy, scale=1.0):
                    A(dst, src, f, scale=scale).then_inc(s["act_evac"], 1)

                o = [bank[2 * (j.bank % 2) + m] for m in range(2)]
                if kind in ("qa", "ka"):
                    t = qa if kind == "qa" else ka
                    for m in range(2):
                        put(t[:, 2 * (i % 2) + m, :], o[m][:, :], scale=0.125 if kind == "qa" else 1.0)
                elif kind == "va":
                    for m in range(2):
                        put(va[:, 2 * m:2 * m + 2, CW * (i - 4):CW * (i - 3)],
                            o[m][:, :].rearrange("p (t c) -> p t c", t=2))
                elif kind == "conv":
                    c = i - 6
                    if c == 0:
                        act.wait_ge(s["bias_stored"], 16 * 8)
                    act.wait_ge(s["conv_pad"], 1)
                    if c >= 2:
                        act.wait_ge(s["conv_step"], 8 * (c - 1))
                    for m in range(2):
                        put(cvb[:, c % 2, m, 3:CVP], o[m][:, :])
                elif kind == "zd":
                    for m in range(2):
                        put(zs[:, 2 * (i - 12) + m, :], o[m][:, :], ACT.Silu)
                elif kind == "ba":
                    put(CO[0:16, 11, :], o[0][0:16, :])
                elif kind == "gate":
                    f = 11 * layer + i
                    if f:
                        act.wait_ge(s["f_low"], 2 * f)
                    for m in range(2):
                        put(SG[:, m, :], o[m][:, :], ACT.Silu)
                elif kind in ("aqf", "abg", "av"):
                    if heads_done(n):
                        act.wait_ge(s["mixed"], heads_done(n))
                        act.wait_ge(s["h_low"], heads_done(n))
                    a = aslot[i % 2]
                    if kind == "aqf":
                        put(a["q"][:, :], o[0][:, :], ACT.Silu)
                        put(a["G1"][:, 1, :], o[1][:, :], ACT.Sigmoid)
                        put(a["KK"][:, 0, :], o[1][:, :], ACT.Sigmoid, -1.0)
                    elif kind == "abg":
                        put(a["G1"][:, 0, :], o[0][:, :], ACT.Sigmoid)
                        put(a["KK"][:, 1, :], o[0][:, :], ACT.Sigmoid, -1.0)
                        put(agate[:, i, :], o[1][:, :], ACT.Sigmoid)
                    else:
                        for m in range(2):
                            put(avb[i][:, 2 * m:2 * m + 2, :], o[m][:, :].rearrange("p (t c) -> p t c", t=2))
                elif kind in ("bq", "bk"):
                    act.wait_ge(s["m_add"], adds_before(n))
                    act.wait_ge(s["mixed"], heads_done(n))
                    act.wait_ge(s["h_low"], heads_done(n))
                    for m in range(2):
                        put((bq if kind == "bq" else bk)[:, m, :], o[m][:, :],
                            scale=1.0 if kind == "bq" else 0.125)
                elif kind == "bv":
                    for m in range(2):
                        put(bv[:, 2 * m:2 * m + 2, CW * i:CW * i + CW],
                            o[m][:, :].rearrange("p (t c) -> p t c", t=2))
                elif kind == "bg":
                    for m in range(2):
                        put(bg[:, 2 * i + m, :], o[m][:, :], ACT.Silu)
                elif kind in ("cq", "ck"):
                    act.wait_ge(s["m_add"], adds_before(n))
                    act.wait_ge(s["mixed"], heads_done(n))
                    act.wait_ge(s["h_low"], heads_done(n))
                    for m in range(2):
                        put((cq if kind == "cq" else ck)[:, m, :], o[m][:, :],
                            scale=0.125 if kind == "cq" else 1.0)
                elif kind == "cl":
                    put(clr[0:32, :], o[0][0:32, :])
                elif kind == "cv":
                    act.wait_ge(s["mixed"], heads_done(n))
                    for m in range(2):
                        put(cvb2[i][:, 2 * m:2 * m + 2, :], o[m][:, :].rearrange("p (t c) -> p t c", t=2))
                elif kind == "cg":
                    act.wait_ge(s["h_low"], heads_done(n))
                    for m in range(2):
                        put(cg[:, m, :], o[m][:, :], ACT.Silu)
                elif kind in ("ga", "gb", "gc"):
                    if adds_before(n):
                        act.wait_ge(s["m_add"], adds_before(n))
                    act.wait_ge(s["mixed"], heads_done(n))
                    act.wait_ge(s["h_low"], heads_done(n))
                    for m in range(2):
                        put(gate_at[GATE_AT[kind[1]][2 * i + m]][:, :], o[m][:, :], ACT.Sigmoid)

            def begin(n):
                if JOBS[n].w + 1 < len(PRODUCTS):
                    split(JOBS[n].w + 1)

            def end(n):
                j = JOBS[n]
                _, kind, layer, i = STEPS[n]
                if j.last and kind not in ("wout", "down", "up", "pa", "pb", "pc"):
                    evacuate(n, j, kind, layer, i)
                if kind == "up":
                    f = 11 * layer + i
                    for m in range(2):
                        act.wait_ge(s["dve_evac"], j.dve0 + m + 1)
                        if i == 0:
                            act.wait_ge(s["gemm_done"], gemm_before(n))
                        A(AH[:, 2 * i + m, :], SG[:, m, :], ACT.Copy).then_inc(s["f_high"], 1)

            def fill(st, slot):
                for n, part in parts(st, slot):
                    if part == 0:
                        begin(n)
                for n, part in parts(st, slot - 1):
                    if part == PARTS - 1:
                        end(n)

            def attention(h):
                g = h - 2
                if g == 0:
                    act.wait_ge(s["dn_scaled"], 4)
                if g >= 0:
                    act.wait_ge(s["a_turned"], g + 1)
                    if g >= 2:
                        act.wait_ge(s["a_out"], g - 1)
                    for b, a, e in ((0, 0, 512), (1, 512, 1024), (2, 1024, 1280)):
                        A(PT[:, g % 2, a:e], bank[b][:, 0:e - a], ACT.Copy).then_inc(s["a_turn_copied"], 1)
                if h < 8:
                    act.wait_ge(s["a_nmax"], h + 1)
                    for i in range(NT):
                        seg = slice(SEG[i], SEG[i] + P * (i + 1))
                        A(Sx[:, h % 2, seg], Sx[:, h % 2, seg], ACT.Exp, bias=anmax[:, h % 2, i:i + 1],
                          accum_out=asum[:, h % 2, i:i + 1]).then_inc(s["a_exp"], 1)
                if g >= 0 and g % 2:
                    act.wait_ge(s["a_out"], g + 1)
                    if g == 1:
                        act.wait_ge(s["gemm_done"], gemm_before(ATTENTION))
                    A(HH[:, g // 2, :], bank[3 if g // 2 % 2 else 7][:, :], ACT.Copy
                      ).then_inc(s["a_high"], 1)

            def delta():
                dc = dcol
                for i in range(8):
                    act.wait_ge(s["dt_turn"], i + 1)
                    t = ktok if i < 4 else vtok
                    A(t[:, :, P * (i % 4):P * (i % 4) + P],
                      bank[4 + i % 2][:, :].rearrange("p (n c) -> p n c", n=4), ACT.Copy
                      ).then_inc(s["dt_copy"], 1)
                for p in range(4):
                    for e in range(2):
                        h, d = 2 * p + e, dset[e]
                        act.wait_ge(s["d_rows"], h + 1)
                        if p:
                            act.wait_ge(s["d_o"], 4 * p)
                        A(d["ER"][:, :], bank[4 * e][:, :], ACT.Exp).then_inc(s["d_er"], 1)
                        act.wait_ge(s["d_et"], 4 * h + 4)
                        A(d["ET"][:, :], d["ET"][:, :], ACT.Exp).then_inc(s["d_etexp"], 1)
                    for e in range(2):
                        h, d = 2 * p + e, dset[e]
                        act.wait_ge(s["d_tr"], h + 1)
                        A(d["Dm"][:, :], bank[4 * e][:, :], ACT.Copy).then_inc(s["d_dm0"], 1)
                    for l in range(6):
                        for e in range(2):
                            h, d = 2 * p + e, dset[e]
                            act.wait_ge(s["d_x"], 12 * p + 2 * l + e + 1)
                            if l:
                                act.wait_ge(s["d_y"], 12 * p + 2 * (l - 1) + e + 1)
                            A(d["X"][:, :], bank[4 * e + 1][:, :], ACT.Copy).then_inc(s["d_xc"], 1)
                    for e in range(2):
                        h, d = 2 * p + e, dset[e]
                        off = 64 * e
                        act.wait_ge(s["d_uw"], h + 1)
                        A(dset[e]["MT"][:, 0:256], bank[4 * e][:, 0:256], ACT.Copy).then_inc(s["d_uwc"], 1)
                        A(d["X"][off:off + 64, :], bank[4 * e + 1][off:off + 64, :], ACT.Copy
                          ).then_inc(s["d_uwc"], 1)
                    act.wait_ge(s["d_o"], 4 * p + 4)
                    A(dset[1]["AT"][:, :], bank[0][:, :], ACT.Square).then_inc(s["df_sq"], 1)
                    ready_ln()
                    act.wait_ge(s["df_sum"], p + 1)
                    A(dset[1]["Dm"][:, :], bank[5][:, :], ACT.Ln, bias=eps[:, :], scale=1.0 / 64
                      ).then_inc(s["df_ln"], 1)
                    act.wait_ge(s["df_ln"], p + 1)
                    A(dset[1]["Dm"][:, :], dset[1]["Dm"][:, :], ACT.Exp, scale=-0.5).then_inc(s["df_r"], 1)
                    act.wait_ge(s["df_y"], p + 1)
                    A(HH[:, 4 + p, :], dset[0]["Dm"][:, :], ACT.Copy).then_inc(s["df_high"], 1)

            def gates(step):
                dc = dcol
                if step == 0:
                    act.wait_ge(s["ba_turned"], 1)
                    A(ba[:, :, :], bank[6][:, 0:64].rearrange("p (t c) -> p t c", t=4), ACT.Copy
                      ).then_inc(s["ba_in"], 1)
                    act.wait_ge(s["ba_in"], 1)
                    A(dc[:, 0, :].rearrange("p (n h) -> p n h", n=4), ba[:, :, 0:8], ACT.Sigmoid
                      ).then_inc(s["dg_act"], 1)
                    A(dc[:, 11, 0:8], par("a_log", 0, 8), ACT.Exp).then_inc(s["dg_act"], 1)
                elif step == 1:
                    act.wait_ge(s["dg_pool"], 1)
                    A(dc[:, 2, :], dc[:, 1, :], ACT.Abs).then_inc(s["dg_act"], 1)
                    act.wait_ge(s["dg_act"], 3)
                    A(dc[:, 2, :], dc[:, 2, :], ACT.Exp, scale=-1.0).then_inc(s["dg_act"], 1)
                    act.wait_ge(s["dg_act"], 4)
                    A(dc[:, 2, :], dc[:, 2, :], ACT.Ln, bias=1.0).then_inc(s["dg_act"], 1)
                elif step == 3:
                    act.wait_ge(s["dg_ps"], 1)
                    A(dc[:, 4, :], bank[6][:, 0:32], ACT.Copy).then_inc(s["dg_cum"], 1)
                    A(dc[:, 6, :], bank[6][:, 32:64], ACT.Copy).then_inc(s["dg_cum"], 1)
                    A(dc[:, 5, :], bank[6][:, 0:32], ACT.Exp).then_inc(s["dg_cum"], 1)
                    A(dc[:, 9, :], bank[6][:, 32:64], ACT.Exp).then_inc(s["dg_cum"], 1)
                elif step == 5:
                    act.wait_ge(s["dg_pool"], 5)
                    A(dc[:, 8, :], dc[:, 7, :], ACT.Exp).then_inc(s["dg_cum"], 1)

            def length(c):
                act.wait_ge(s["dn_sum"], c + 1)
                if c >= 2:
                    act.wait_ge(s["dn_scaled"], c - 1)
                for m in range(2):
                    A(crs[:, c % 2, m, :], bank[4 + 2 * (c % 2) + m][:, :], ACT.Ln, bias=eps[:, :]
                      ).then_inc(s["dn_ln"], 1)
                act.wait_ge(s["dn_ln"], 2 * c + 2)
                A(crs[:, c % 2, :, :], crs[:, c % 2, :, :], ACT.Exp, scale=-0.5).then_inc(s["dn_r"], 1)

            def copy_scores(u, e, ST, level):
                b0, b1 = bank[4 + 2 * e], bank[5 + 2 * e]
                act.wait_ge(s["levels"], 10 * u + level + 1)
                st = ST[:, :, :]
                if level == 0:
                    A(bc(st, [640, 4], [1, P]), b0[:, :].rearrange("p (j t) -> p j t", j=4), ACT.Copy
                      ).then_inc(s["scores_copied"], 1)
                elif level == 8:
                    dst = bass.AP(st.tensor, st.offset + 128, [list(st.ap[0]), [1280, 2], [384, 2], [1, P]])
                    A(dst, b0[:, :].rearrange("p (a b t) -> p a b t", a=2, b=2), ACT.Copy
                      ).then_inc(s["scores_copied"], 1)
                else:
                    for x, b, off in ((0, b0, 256), (1, b1, 1024)):
                        dst = bass.AP(st.tensor, st.offset + off, [list(st.ap[0]), [512, 2], [1, 256]])
                        A(dst, b[:, :].rearrange("p (a t) -> p a t", a=2), ACT.Copy
                          ).then_inc(s["scores_copied"], 1)

            def finish(st, heads_, hd, group):
                temps = TEMPS[st[1]]
                bi = b_before[st]
                if hd:
                    act.wait_ge(s["h_low"], hd)
                if ADDS[0]:
                    act.wait_ge(s["m_add"], ADDS[0])
                for x, (e, y) in enumerate(heads_):
                    sq, rr, tt = temps[x]
                    b0 = bank[4 + 2 * e]
                    act.wait_ge(s["mixed"], hd + x + 1)
                    if group:
                        A(tt, b0[:, :], ACT.Copy).then_inc(s["h_cp"], 1)
                        fill(st, 5)
                        act.wait_ge(s["h_cent"], bi + 1)
                        A(sq, tt, ACT.Square).then_inc(s["h_sq"], 1)
                    else:
                        A(sq, b0[:, :], ACT.Square).then_inc(s["h_sq"], 1)
                ready_ln()
                for x, (e, y) in enumerate(heads_):
                    sq, rr, tt = temps[x]
                    act.wait_ge(s["h_sum"], hd + x + 1)
                    A(rr, bank[5 + 2 * e][:, :], ACT.Ln, bias=eps[:, :], scale=1.0 / P).then_inc(s["h_ln"], 1)
                    act.wait_ge(s["h_ln"], hd + x + 1)
                    A(rr, rr, ACT.Exp, scale=-0.5).then_inc(s["h_r"], 1)
                for x, (e, y) in enumerate(heads_):
                    act.wait_ge(s["h_y"], hd + x + 1)
                    act.wait_ge(s["gemm_done"], GB[0])
                    A(YH[:, y, :], temps[x][2], ACT.Copy).then_inc(s["h_high"], 1)

            GB, ADDS = [0], [0]
            nrm = 0
            for n, st in enumerate(STEPS):
                GB[0], ADDS[0] = gemm_before(n), adds_before(n)
                if st[0] == "norm":
                    if nrm == 0:
                        split(0)
                    norm(n, nrm)
                    nrm += 1
                elif st[0] == "job":
                    if n not in EMBEDDED:
                        begin(n)
                        end(n)
                elif st[0] == "gates":
                    gates(st[1])
                elif st[0] == "length":
                    length(st[1])
                elif st[0] == "decay":
                    layer, i = st[1:]
                    cu = 2 * (layer - 1) + i
                    for dr in range(2):
                        pl = 1 - dr
                        act.wait_ge(s["c_logit"], 2 * cu + dr + 1)
                        bcol = par("b_alpha", 4 * (layer - 1) + 2 * dr + i)
                        A(c_x[:, pl, :], bank[4 + 2 * dr][:, :], ACT.Identity, bias=bcol
                          ).then_inc(s["c_act"], 1)
                    act.wait_ge(s["c_act"], 5 * cu + 2)
                    A(c_e[:, :, :], c_x[:, :, :], ACT.Abs).then_inc(s["c_act"], 1)
                    act.wait_ge(s["c_act"], 5 * cu + 3)
                    A(c_e[:, :, :], c_e[:, :, :], ACT.Exp, scale=-1.0).then_inc(s["c_act"], 1)
                    act.wait_ge(s["c_act"], 5 * cu + 4)
                    A(c_e[:, :, :], c_e[:, :, :], ACT.Ln, bias=1.0).then_inc(s["c_act"], 1)
                    act.wait_ge(s["c_dve"], cu + 1)
                    A(cG1[:, :, :], c_x[:, :, :], ACT.Exp, scale=1.0 / 16).then_inc(s["c_lanes"], 1)
                    A(cKK[:, :, :], bc(ck[:, i, :], [0, 2], [1, S]), ACT.Copy).then_inc(s["c_lanes"], 1)
                elif st[0] == "square":
                    squares(st[1], range(2 * st[2], 2 * st[2] + 2))
                elif st[0] == "bias":
                    bias(st[1])
                elif st[0] == "conv" and st[1]:
                    c = st[1] - 1
                    for m in range(2):
                        act.wait_ge(s["conv_step"], 8 * c + 4 * m + 4)
                        A(CO[:, 2 * c + m, :], CO[:, 2 * c + m, :], ACT.Silu).then_inc(s["conv_silu"], 1)
                elif st[0] == "attn":
                    attention(st[1])
                elif st[0] == "delta":
                    delta()
                elif st[0] == "merge":
                    r = st[1] - 1
                    act.wait_ge(s["gemm_done"], JOBS[STEPS.index(("job", "gc", st[1], 3))].w + 1)
                    for k in range(2 * st[2], 2 * st[2] + 2):
                        act.wait_ge(s["m_add"], 24 * r + 16 + k + 1)
                        A(HH[:, k, :], macc[:, k, :], ACT.Copy).then_inc(s["m_high"], 1)
                elif st[0] == "mix":
                    _, kind, layer, i = st
                    hd = heads[st]
                    if kind == "b":
                        for slot in range(5):
                            fill(st, slot)
                        finish(st, [(i % 2, i)], hd, True)
                        fill(st, 6)
                        continue
                    u = units[st]
                    if kind == "c":
                        hs = [(0, cST[0]), (1, cST[1])]
                    else:
                        hs = [(i % 2, aslot[i % 2]["ST"])]
                    for level in range(10):
                        if level in (0, 8, 9):
                            for e, ST in hs:
                                copy_scores(u, e, ST, level)
                        fill(st, level)
                    fill(st, 10)
                    finish(st, [(e, (2 * i + x) if kind == "c" else i) for x, (e, ST) in enumerate(hs)], hd, False)
                    fill(st, 11)

        @block.vector
        def _(dve):
            TT, TS, STT = dve.tensor_tensor, dve.tensor_scalar, dve.scalar_tensor_tensor

            def split(wi, half=None):
                j = PRODUCTS[wi]
                if half != 1:
                    dve.wait_ge(s["w_rounded"], wi + 1)
                now = slice(j.size // 2 if half == 1 else 0, j.size // 2 if half == 0 else j.size)
                TT(WL[:, wi % 2, now], raw[:, j.load % RAW, now], WH[:, wi % 2, now].bitcast(F32), ALU.subtract
                   ).then_inc(s["w_split"], 2 if half is None else 1)

            dve.wait_ge(s["params_in"], 16)
            l0, l1 = par("lb", 0, 4), par("lb", 4, 4)
            TT(small[:, 4, :], l0, l1, ALU.max).then_inc(s["lb_max"], 1)
            dve.wait_ge(s["lb_max"], 1)
            TT(small[:, 0, :], l0, small[:, 4, :], ALU.subtract).then_inc(s["lb_dve"], 1)
            TT(small[:, 1, :], l1, small[:, 4, :], ALU.subtract).then_inc(s["lb_dve"], 1)
            dve.wait_ge(s["lb_exp"], 1)
            TT(small[:, 5, :], small[:, 2, :], small[:, 3, :], ALU.add).then_inc(s["lb_dve"], 1)
            dve.wait_ge(s["lb_dve"], 3)
            dve.reciprocal(small[:, 6, :], small[:, 5, :]).then_inc(s["lb_dve"], 1)
            dve.wait_ge(s["lb_dve"], 4)
            TT(small[:, 2:4, :], small[:, 2:4, :], bc(small[:, 6, :], [0, 2], [1, 4]), ALU.mult
               ).then_inc(s["lb_dve"], 1)
            dve.wait_ge(s["lb_dve"], 5)
            TT(small[:, 7, :], small[:, 2, :], small[:, 3, :], ALU.add).then_inc(s["lb_dve"], 1)
            dve.wait_ge(s["lb_dve"], 6)
            TT(lbound[:, 0, :], small[:, 2, :], small[:, 2, :], ALU.subtract).then_inc(s["lb_dve"], 1)
            TT(lbound[:, 1, :], small[:, 7, :], small[:, 2, :], ALU.subtract).then_inc(s["lb_dve"], 1)
            dve.wait_ge(s["lb_dve"], 8)
            TS(lbound[:, :, :], lbound[:, :, :], 0.0, None, ALU.max).then_inc(s["lb_dve"], 1)
            dve.wait_ge(s["lb_dve"], 9)
            TS(rest[:, :, :], lbound[:, :, :], -1.0, 1.0, ALU.mult, ALU.add).then_inc(s["lb_dve"], 1)
            dve.wait_ge(s["cact_ready"], 1)

            def ada_chunk(j):
                _, layer, g, c = j.src
                dve.wait_ge(raw_in[j.load % RAW], 16 * (j.load // RAW + 1))
                if c == 0:
                    if layer or g:
                        dve.wait_ge(s["mod_ready"], 6 * layer + g)
                for t in range(2):
                    if j.ada or t:
                        dve.wait_ge(s["ada_mac"], 2 * j.ada + t)
                    src = raw[:, j.load % RAW, ADA_COLS * t:ADA_COLS * (t + 1)]
                    col = cact[:, 8 * layer + 2 * c + t:8 * layer + 2 * c + t + 1]
                    if c == 0 and t == 0:
                        i = TS(ada_acc[:, :], src, col, None, ALU.mult)
                    else:
                        i = STT(ada_acc[:, :], src, col, ada_acc[:, :], ALU.mult, ALU.add)
                    i.then_inc(s["ada_mac"], 1)

            def norm(n, r):
                name, at = NORM_G[r]
                q = modulated(r)
                if NORM_MOD[r]:
                    layer, g = NORM_MOD[r]
                    dve.wait_ge(s["dve_evac"], mod_ready_count(layer, g + 1))
                    STT(acol[:, :], mod[:, layer, g + 1, :], 1.0, par(name, at, 8), ALU.add, ALU.mult
                        ).then_inc(s["n_acol"], 1)
                    dve.wait_ge(s["n_acol"], q + 1)
                dve.wait_ge(s["n_rstd"], r + 1)

                def low(k):
                    dve.wait_ge(s["n_high"], 8 * q + k + 1)
                    STT(HL[:, k, :], nt[:, k % 2, :], mod[:, layer, g, k:k + 1], HH[:, k, :].bitcast(F32),
                        ALU.add, ALU.subtract).then_inc(s["n_low"], 1)

                for k in range(KD):
                    if r == RENORM:
                        STT(xT[:, k, :], xT[:, k, :], par(name, k), nr[:, :], ALU.mult, ALU.mult
                            ).then_inc(s["renormed"], 1)
                        continue
                    if r == FINAL:
                        STT(ost[:, k, :], xT[:, k, :], par("g_out", k), nr[:, :], ALU.mult, ALU.mult
                            ).then_inc(s["out_ready"], 1)
                        continue
                    if k >= 2:
                        dve.wait_ge(s["n_low"], 8 * q + k - 1)
                    STT(nt[:, k % 2, :], xT[:, k, :], acol[:, k:k + 1], nr[:, :], ALU.mult, ALU.mult
                        ).then_inc(s["n_scaled"], 1)
                    if k:
                        low(k - 1)
                if NORM_MOD[r]:
                    low(KD - 1)

            def evacuate(n, j, kind, layer, i):
                dve.wait_ge(s["gemm_done"], j.w + 1)
                o = [bank[2 * (j.bank % 2) + m] for m in range(2)]
                for m in range(2):
                    if kind in ("wout", "down"):
                        g = 2 if kind == "wout" else 5
                        k = 2 * (i if kind == "wout" else i // 3) + m
                        dve.wait_ge(s["dve_evac"], mod_ready_count(layer, g))
                        STT(xT[:, k, :], o[m][:, :], mod[:, layer, g, k:k + 1], xT[:, k, :],
                            ALU.mult, ALU.add).then_inc(s["dve_evac"], 1)
                    elif kind == "up":
                        dve.wait_ge(s["act_evac"], j.act0)
                        TT(SG[:, m, :], SG[:, m, :], o[m][:, :], ALU.mult).then_inc(s["dve_evac"], 1)
                    else:
                        gate = gate_at[GATE_AT[kind[1]][2 * i + m]]
                        dve.wait_ge(s["act_evac"], evacuated("g" + kind[1], layer, i))
                        TT(gate[:, :], gate[:, :], o[m][:, :], ALU.mult).then_inc(s["dve_evac"], 1)
                if kind == "up":
                    f = 11 * layer + i
                    for m in range(2):
                        dve.wait_ge(s["f_high"], 2 * f + m + 1)
                        TT(AL[:, 2 * i + m, :], SG[:, m, :], AH[:, 2 * i + m, :].bitcast(F32), ALU.subtract
                           ).then_inc(s["f_low"], 1)
                if kind in ("pa", "pb", "pc"):
                    x = "abc".index(kind[1])
                    r = layer - 1
                    for m in range(2):
                        k = 2 * i + m
                        gate = gate_at[GATE_AT[kind[1]][k]]
                        dve.wait_ge(s["dve_evac"], j.dve0 + m + 1)
                        if x == 0:
                            dve.tensor_copy(macc[:, k, :], gate[:, :]).then_inc(s["m_add"], 1)
                        else:
                            dve.wait_ge(s["m_add"], 24 * r + 8 * (x - 1) + k + 1)
                            TT(macc[:, k, :], macc[:, k, :], gate[:, :], ALU.add).then_inc(s["m_add"], 1)
                    dve.wait_ge(s["m_add"], 24 * r + 8 * x + 2 * i + 2)

            def forget(layer, h):
                a, done = aslot[h % 2], 3 * (forgets(("mix", "a", layer, h)) - 1)
                lo, om = (t[:, layer - 1, h:h + 1] for t in (lbound, rest))
                dve.wait_ge(s["act_evac"], evacuated("abg", layer, h))
                dve.wait_ge(s["lb_dve"], 10)
                TS(a["G1"][:, :, :], a["G1"][:, :, :], om, lo, ALU.mult, ALU.add).then_inc(s["prep"], 1)
                TS(a["KK"][:, :, :], a["KK"][:, :, :], om, None, ALU.mult).then_inc(s["prep"], 1)
                dve.wait_ge(s["prep"], done + 1)
                TS(a["G1"][:, :, :], a["G1"][:, :, :], TINY, None, ALU.max).then_inc(s["prep"], 1)

            def begin(n):
                if JOBS[n].w + 1 < len(PRODUCTS):
                    split(JOBS[n].w + 1)

            def end(n):
                j = JOBS[n]
                _, kind, layer, i = STEPS[n]
                if j.last and kind in ("wout", "down", "up", "pa", "pb", "pc"):
                    evacuate(n, j, kind, layer, i)

            def fill(st, slot):
                for n, part in parts(st, slot):
                    if part % 2 == 0:
                        split(JOBS[n].w + 1, part // 2)
                for n, part in parts(st, slot - 1):
                    if part == PARTS - 1:
                        end(n)
                for n, part in parts(st, slot - 2):
                    if part == PARTS - 1 and STEPS[n][1] == "abg":
                        forget(STEPS[n][2], STEPS[n][3])

            def attention(h):
                g = h - 1
                if 0 <= g < 8:
                    dve.wait_ge(s["a_exp"], 4 * g + 4)
                    dve.reciprocal(arsum[:, g % 2, :], asum[:, g % 2, :]).then_inc(s["a_rsum"], 1)
                    dve.wait_ge(s["a_rsum"], g + 1)
                    for i in range(NT):
                        seg = slice(SEG[i], SEG[i] + P * (i + 1))
                        TS(Sx[:, g % 2, seg], Sx[:, g % 2, seg], arsum[:, g % 2, i:i + 1], None, ALU.mult
                           ).then_inc(s["a_norm"], 1)
                if h < 8:
                    dve.wait_ge(s["a_scores"], h + 1)
                    dve.wait_ge(toep_in[h % 3], 16 * (h // 3 + 1))
                    if h >= 2:
                        dve.wait_ge(s["a_turned"], h - 1)
                    for i in range(NT):
                        b, c0 = SBANK[i]
                        seg = slice(SEG[i], SEG[i] + P * (i + 1))
                        dve.tensor_tensor_reduce(Sx[:, h % 2, seg], bank[b][:, c0:c0 + P * (i + 1)],
                                                 toep[:, h % 3, 384 - P * i:512], 1.0, -3.0e38,
                                                 ALU.add, ALU.max, amax[:, h % 2, i:i + 1]
                                                 ).then_inc(s["a_biased"], 1)
                    dve.wait_ge(s["a_biased"], 4 * h + 4)
                    TS(anmax[:, h % 2, :], amax[:, h % 2, :], -1.0, None, ALU.mult).then_inc(s["a_nmax"], 1)
                if h >= 2 and h % 2:
                    pair = (h - 2) // 2
                    dve.wait_ge(s["a_high"], pair + 1)
                    TT(HL[:, pair, :], bank[3 if pair % 2 else 7][:, :], HH[:, pair, :].bitcast(F32), ALU.subtract
                       ).then_inc(s["a_low"], 1)

            def delta():
                dc = dcol
                dve.wait_ge(s["dg_cum"], 5)
                dve.wait_ge(s["dt_copy"], 8)

                def v4(t):
                    return t[:, :].rearrange("p (n i) -> p n i", n=4)

                for p in range(4):
                    for e in range(2):
                        h, d, off = 2 * p + e, dset[e], 64 * e
                        dve.wait_ge(s["d_rows"], h + 1)
                        if p:
                            dve.wait_ge(s["d_o"], 4 * p)
                        dve.wait_ge(s["d_er"], h + 1)
                        for n in range(4):
                            col = 8 * n + h
                            TS(d["ET"][:, P * n:P * n + P], bank[4 * e][:, P * n:P * n + P],
                               dc[:, 4, col:col + 1], 0.0, ALU.subtract, ALU.min).then_inc(s["d_et"], 1)
                        TT(d["kbT"][off:off + 64, :], CO[off:off + 64, 4 + p, :], bank[4 * e + 1][off:off + 64, :],
                           ALU.mult).then_inc(s["d_kb"], 1)
                    for e in range(2):
                        h, d, off = 2 * p + e, dset[e], 64 * e
                        dve.wait_ge(s["d_kk"], h + 1)
                        dve.wait_ge(s["d_etmask"], h + 1)
                        TT(d["AT"][:, :], bank[4 * e + 2][:, :], d["ET"][:, :], ALU.mult).then_inc(s["d_at"], 1)
                        TT(d["QKT"][:, :], bank[4 * e + 3][:, :], d["ET"][:, :], ALU.mult).then_inc(s["d_qk"], 1)
                    for e in range(2):
                        h, d, off = 2 * p + e, dset[e], 64 * e
                        dve.wait_ge(s["d_m"], 14 * p + e + 1)
                        TT(v4(d["DT"]), bc(ident[:, :], [0, 4], [1, P]), v4(d["MT"]), ALU.subtract
                           ).then_inc(s["d_dt0"], 1)
                        for x, (t, dst, k) in enumerate(((vtok, "bv", 0), (ktok, "kbe", 10), (ktok, "kdec", 8))):
                            if dst == "bv":
                                dve.wait_ge(s["d_qk"], h + 1)
                            out_ = v4s(d["ET"]) if dst == "bv" else d[dst][:, :, :]
                            TT(out_, t[:, :, 64 * h:64 * h + 64],
                               bass.AP(dc[:, k, :].tensor, dc[:, k, :].offset + h,
                                       [list(dc[:, k, :].ap[0]), [8, 4], [0, 64]]), ALU.mult
                               ).then_inc(s["d_tok"], 1)
                        dve.wait_ge(s["d_er"], h + 1)
                        TT(d["kbT"][off:off + 64, :], CO[off:off + 64, p, :], d["ER"][off:off + 64, :], ALU.mult
                           ).then_inc(s["d_qe"], 1)
                    for l in range(6):
                        for e in range(2):
                            h, d = 2 * p + e, dset[e]
                            dve.wait_ge(s["d_y"], 12 * p + 2 * l + e + 1)
                            if l < 5:
                                TT(d["Dm"][:, :], d["Dm"][:, :], bank[4 * e + 2][:, :], ALU.subtract
                                   ).then_inc(s["d_upd"], 1)
                            TT(d["DT"][:, :], d["DT"][:, :], bank[4 * e + 3][:, :], ALU.subtract
                               ).then_inc(s["d_upd"], 1)
                    for n in range(4):
                        for e in range(2):
                            h, d, off = 2 * p + e, dset[e], 64 * e
                            U = d["MT"][:, 64 * n:64 * n + 64]
                            V = d["MT"][:, 256 + 64 * (n % 2):320 + 64 * (n % 2)]
                            dve.wait_ge(s["d_uwc"], 2 * h + 2)
                            if n:
                                dve.wait_ge(s["d_ws"], 6 * p + 2 * (n - 1) + e + 1)
                                TT(V, U, bank[4 * e + 2][:, 64 * n:64 * n + 64], ALU.subtract
                                   ).then_inc(s["d_vn"], 1)
                            else:
                                dve.tensor_copy(V, U).then_inc(s["d_vn"], 1)
                        if n < 3:
                            for e in range(2):
                                h, d, off = 2 * p + e, dset[e], 64 * e
                                st_ = d["ER"][off:off + 64, 64 * (n % 2):64 * (n % 2) + 64]
                                so = d["ER"][off:off + 64, 64 * (1 - n % 2):64 * (1 - n % 2) + 64]
                                dve.wait_ge(s["d_sp"], 6 * p + 2 * n + e + 1)
                                ps = bank[4 * e + 3][off:off + 64, 64 * n:64 * n + 64]
                                if n:
                                    dve.wait_ge(s["d_sn"], 6 * p + 2 * (n - 1) + e + 1)
                                    STT(st_, so, dc[off:off + 64, 9, 8 * n + h:8 * n + h + 1], ps,
                                        ALU.mult, ALU.add).then_inc(s["d_sn"], 1)
                                else:
                                    dve.tensor_copy(st_, ps).then_inc(s["d_sn"], 1)
                    dve.wait_ge(s["d_o"], 4 * p + 4)
                    T = dset[0]["Dm"]
                    dve.wait_ge(s["df_sq"], p + 1)
                    STT(T[:, :], bank[0][:, :], par("delta_g"), zs[:, p, :], ALU.mult, ALU.mult
                        ).then_inc(s["df_t"], 1)
                    dve.wait_ge(s["df_r"], p + 1)
                    dve.wait_ge(s["df_t"], p + 1)
                    TT(T[:, :], T[:, :], dset[1]["Dm"][:, :], ALU.mult).then_inc(s["df_y"], 1)
                    dve.wait_ge(s["df_high"], p + 1)
                    TT(HL[:, 4 + p, :], T[:, :], HH[:, 4 + p, :].bitcast(F32), ALU.subtract
                       ).then_inc(s["df_low"], 1)

            def gates(step):
                dc = dcol

                def g4(k):
                    return dc[:, k, :].rearrange("p (n h) -> p n h", n=4)

                if step == 0:
                    dve.wait_ge(s["dg_act"], 2)
                    TT(g4(1), ba[:, :, 8:16], bc(par("dt_bias", 0, 8), [0, 4], [1, 8]), ALU.add
                       ).then_inc(s["dg_pool"], 1)
                elif step == 2:
                    dve.wait_ge(s["dg_act"], 5)
                    STT(dc[:, 3, :], dc[:, 1, :], 0.0, dc[:, 2, :], ALU.max, ALU.add).then_inc(s["dg_pool"], 1)
                    dve.wait_ge(s["dg_pool"], 2)
                    STT(g4(3), g4(3), -1.0, bc(dc[:, 11, 0:8], [0, 4], [1, 8]), ALU.mult, ALU.mult
                        ).then_inc(s["dg_pool"], 1)
                elif step == 4:
                    dve.wait_ge(s["dg_cum"], 4)
                    TT(dc[:, 10, :], dc[:, 0, :], dc[:, 5, :], ALU.mult).then_inc(s["dg_pool"], 1)
                    TT(dc[:, 7, :], dc[:, 6, :], dc[:, 4, :], ALU.subtract).then_inc(s["dg_pool"], 1)

            def unit(c):
                dve.wait_ge(s["dn_r"], c + 1)
                STT(CO[:, 2 * c:2 * c + 2, :], CO[:, 2 * c:2 * c + 2, :], 0.125 if c < 2 else 1.0,
                    crs[:, c % 2, :, :], ALU.mult, ALU.mult).then_inc(s["dn_scaled"], 1)

            def v4s(t):
                return t[:, 0:256].rearrange("p (n c) -> p n c", n=4)

            def scan(st, u, hd, QQ, KK, g1, gt, hs):
                sc0 = 7 * scan_before[st]
                fill(st, 0)
                dve.wait_ge(s["lanes"], 8 * u + 8)
                for level in range(1, 9):
                    b = 2 ** (level - 1)
                    dve.wait_ge(s["levels"], 10 * u + level + 1)
                    if level > 1:
                        dve.wait_ge(s["decayed"], 16 * u + 2 * (level - 1))
                    TT(lanes(QQ, b), lanes(QQ, b), lane_gates(g1, gt, b, False), ALU.mult
                       ).then_inc(s["decayed"], 1)
                    TT(lanes(KK, b), lanes(KK, b), lane_gates(g1, gt, b, True), ALU.mult
                       ).then_inc(s["decayed"], 1)
                    if level < 8:
                        for x, (e, ST) in enumerate(hs):
                            if level == 1:
                                dve.wait_ge(s["scores_copied"], 4 * scan_before[st] + x + 1)
                            else:
                                dve.wait_ge(s["scores_put"], sc0 + len(hs) * (level - 2) + x + 1)
                            dve.copy_predicated(bc(ST[:, :, :], [640, 4], [1, P]),
                                                bc(masks[:, level - 1, :], [0, 4], [1, P]),
                                                bank[4 + 2 * e + level % 2][:, :].rearrange("p (j t) -> p j t", j=4)
                                                ).then_inc(s["scores_put"], 1)
                    fill(st, level)
                fill(st, 9)
                fill(st, 10)

            def finish(st, heads_, hd, group, layer):
                branch = "abc".index(st[1])
                temps = TEMPS[st[1]]
                bi = b_before[st]
                for x, (e, y, gate) in enumerate(heads_):
                    sq, rr, tt = temps[x]
                    dve.wait_ge(s["mixed"], hd + x + 1)
                    col = par("norm", 12 * (layer - 1) + 4 * branch + y)
                    if group:
                        dve.wait_ge(s["h_mean"], bi + 1)
                        STT(tt, bank[5 + 2 * e][:, :], -1.0 / P, tt, ALU.mult, ALU.add).then_inc(s["h_cent"], 1)
                        fill(st, 5)
                        dve.wait_ge(s["h_sq"], hd + x + 1)
                        STT(tt, tt, col, gate, ALU.mult, ALU.mult).then_inc(s["h_t"], 1)
                    else:
                        dve.wait_ge(s["h_sq"], hd + x + 1)
                        STT(tt, bank[4 + 2 * e][:, :], col, gate, ALU.mult, ALU.mult).then_inc(s["h_t"], 1)
                for x, (e, y, gate) in enumerate(heads_):
                    sq, rr, tt = temps[x]
                    dve.wait_ge(s["h_r"], hd + x + 1)
                    dve.wait_ge(s["h_t"], hd + x + 1)
                    TT(tt, tt, rr, ALU.mult).then_inc(s["h_y"], 1)
                for x, (e, y, gate) in enumerate(heads_):
                    dve.wait_ge(s["h_high"], hd + x + 1)
                    TT(YL[:, y, :], temps[x][2], YH[:, y, :].bitcast(F32), ALU.subtract).then_inc(s["h_low"], 1)

            CONV_EVAC = [JOBS[m].act for m, x in enumerate(STEPS) if x[:2] == ("job", "conv")]
            nrm = 0
            for n, st in enumerate(STEPS):
                if st[0] == "ada":
                    ada_chunk(JOBS[n])
                elif st[0] == "mod":
                    _, layer, g = st
                    j = JOBS[n]
                    dve.wait_ge(s["mod_ready"], 6 * layer + g + 1)
                    TT(mod[:, layer, g, :], bank[2 * (j.bank % 2)][:, 0:8],
                       par("b_ada", 48 * layer + 8 * g, 8), ALU.add).then_inc(s["dve_evac"], 1)
                elif st[0] == "norm":
                    if nrm == 0:
                        split(0)
                        dve.wait_ge(s["const_in"], 16 * NCONST)
                        dve.wait_ge(s["ones_set"], 3)
                    norm(n, nrm)
                    nrm += 1
                elif st[0] == "job":
                    if n not in EMBEDDED:
                        begin(n)
                        end(n)
                        if st[1] == "av":
                            forget(st[2], 0)
                elif st[0] == "gates":
                    gates(st[1])
                elif st[0] == "unit":
                    unit(st[1])
                elif st[0] == "decay":
                    dve.wait_ge(s["c_act"], 5 * (2 * (st[1] - 1) + st[2]) + 5)
                    STT(c_x[:, :, :], c_x[:, :, :], 0.0, c_e[:, :, :], ALU.min, ALU.subtract
                        ).then_inc(s["c_dve"], 1)
                elif st == ("bias", 7):
                    dve.wait_ge(s["bias_stored"], 16 * 8)
                    dve.memset(cvb[:, :, :, :], 0.0).then_inc(s["conv_pad"], 1)
                elif st[0] == "conv" and st[1] < 6:
                    c = st[1]
                    for m in range(2):
                        t = 2 * c + m
                        dve.wait_ge(s["act_evac"], CONV_EVAC[c] - 1 + m)
                        for k in range(4):
                            src = cvb[:, c % 2, m, k:k + S]
                            wc = par("conv", 4 * t + k)
                            if k == 0:
                                TS(CO[:, t, :], src, wc, None, ALU.mult).then_inc(s["conv_step"], 1)
                            else:
                                dve.wait_ge(s["conv_step"], 8 * c + 4 * m + k)
                                STT(CO[:, t, :], src, wc, CO[:, t, :], ALU.mult, ALU.add
                                    ).then_inc(s["conv_step"], 1)
                elif st[0] == "attn":
                    attention(st[1])
                elif st[0] == "delta":
                    delta()
                elif st[0] == "rotary":
                    r = st[1] - 1
                    dve.wait_ge(s["r_in"], 64 * (r + 1))
                    for x in range(4):
                        t = (bq if x < 2 else bk)[:, x % 2, :]
                        dve.wait_ge(s["r_rot"], 4 * r + x + 1)
                        TT(btmp[:, :], bank[4 + x][:, :], brot[:, S:2 * S], ALU.mult).then_inc(s["r_t"], 1)
                        TT(t, t, brot[:, 0:S], ALU.mult).then_inc(s["r_t"], 1)
                        dve.wait_ge(s["r_t"], 12 * r + 3 * x + 2)
                        TT(t, t, btmp[:, :], ALU.add).then_inc(s["r_t"], 1)
                        dve.wait_ge(s["r_t"], 12 * r + 3 * x + 3)
                elif st[0] == "merge":
                    r = st[1] - 1
                    for k in range(2 * st[2], 2 * st[2] + 2):
                        dve.wait_ge(s["m_high"], 8 * r + k + 1)
                        TT(HL[:, k, :], macc[:, k, :], HH[:, k, :].bitcast(F32), ALU.subtract
                           ).then_inc(s["m_low"], 1)
                elif st[0] == "mix":
                    _, kind, layer, i = st
                    hd = heads[st]
                    if kind == "b":
                        bi = b_before[st]
                        if i == 0:
                            dve.wait_ge(s["r_in"], 64 * layer)
                        e = i % 2
                        for jb in range(4):
                            dve.wait_ge(s["b_scores"], 4 * bi + jb + 1)
                            TT(bST[e][:, jb, :], bank[4 + 2 * e + jb % 2][:, :],
                               bgam[:, i, 384 - P * jb:896 - P * jb], ALU.mult).then_inc(s["r_ps"], 1)
                            fill(st, jb)
                        fill(st, 4)
                        dve.wait_ge(s["h_cp"], bi + 1)
                        dve.wait_ge(s["act_evac"], evacuated("bg", layer, i // 2))
                        finish(st, [(e, i, bg[:, i, :])], hd, True, layer)
                        fill(st, 6)
                        continue
                    u = units[st]
                    if kind == "c":
                        scan(st, u, hd, cQQ, cKK, cG1, cGT, [(0, cST[0]), (1, cST[1])])
                        finish(st, [(x, 2 * i + x, cg[:, x, :]) for x in range(2)], hd, False, layer)
                    else:
                        a = aslot[i % 2]
                        scan(st, u, hd, a["QQ"], a["KK"], a["G1"], a["GT"], [(i % 2, a["ST"])])
                        finish(st, [(i % 2, i, agate[:, i, :])], hd, False, layer)
                        fill(st, 11)

        @block.tensor
        def _(pe):
            MM = pe.matmul

            def acquire(j):
                if j.bank >= 2:
                    who, cnt = FREED[j.bank - 2]
                    pe.wait_ge(s["act_evac" if who == "act" else "dve_evac"], cnt)

            def products(o, sides, first, last, units_):
                n = 0
                total = 3 * len(units_)
                i = None
                for u in units_:
                    for a, b in sides(u):
                        i = MM(o, a, b, start=first and n == 0, stop=last and n == total - 1)
                        n += 1
                return i

            def gemm(n, now=range(PARTS)):
                j = JOBS[n]
                _, kind, layer, i = STEPS[n]
                o = [bank[2 * (j.bank % 2) + m] for m in range(2)]
                sl, wd = j.w % 2, j.width
                X = (HH, HL)
                k0 = 0
                if kind in ("pa", "pb", "pc"):
                    X = (YH, YL)
                elif kind == "down":
                    X = (AH, AL)
                    k0 = 8 * (i % 3)
                if now[0] == 0:
                    pe.wait_ge(s["w_split"], 2 * (j.w + 1))
                    if j.first:
                        acquire(j)
                    if X[0] is YH:
                        pe.wait_ge(s["h_low"], heads_done(n))
                    elif X[0] is AH:
                        pe.wait_ge(s["f_low"], 22 * (layer + 1))
                if kind in TOKEN_MAJOR:
                    for t in now:
                        if wd == CW:
                            dst = o[t // 2][:, CW * (t % 2):CW * (t % 2) + CW]
                        else:
                            dst = o[0][:, wd * t:wd * t + wd]

                        def sides(u):
                            wh, wl = (x[:, sl, u * wd:(u + 1) * wd] for x in (WH, WL))
                            xh, xl = (x[:, k0 + u, P * t:P * t + P] for x in X)
                            return ((xh, wh), (xh, wl), (xl, wh))

                        last = products(dst, sides, True, True, range(j.units))
                    if now[-1] == PARTS - 1:
                        last.then_inc(s["gemm_done"], 1)
                    return
                first_use = FIRST_USE.get(n)
                cw = min(P, wd)
                for u in range(j.units * now[0] // PARTS, j.units * (now[-1] + 1) // PARTS):
                    if first_use:
                        pe.wait_ge(s[first_use[0]], first_use[1] + u + 1)
                    for m in range(2 if wd == CW else 1):
                        wh, wl = (x[:, sl, u * wd + P * m:u * wd + P * m + cw] for x in (WH, WL))
                        xh, xl = (x[:, k0 + u, :] for x in X)
                        for q, (a, b) in enumerate(((wh, xh), (wh, xl), (wl, xh))):
                            last = MM(o[m][0:cw, :], a, b, start=j.first and u == 0 and q == 0,
                                      stop=j.last and u == j.units - 1 and q == 2)
                if now[-1] == PARTS - 1:
                    last.then_inc(s["gemm_done"], 1)

            def fill(st, slot):
                for n, part in parts(st, slot):
                    gemm(n, range(part, part + 1))

            FIRST_USE = {}
            r = 0
            for n, st in enumerate(STEPS):
                nxt = next((m for m in range(n + 1, len(STEPS)) if STEPS[m][0] == "job"), None)
                if st[0] == "norm":
                    if nxt is not None:
                        FIRST_USE[nxt] = ("n_low", 8 * modulated(r))
                    r += 1
                if st[0] == "merge" and st[2] == 3:
                    FIRST_USE[nxt] = ("m_low", 8 * (st[1] - 1))

            def squares(n, r, tiles):
                for k in tiles:
                    pe.wait_ge(s["n_square"], 8 * r + k + 1)
                    if k == 0 and r:
                        pe.wait_ge(s["n_rstd"], r)
                        pe.wait_ge(s["df_low"], 4)
                        if heads_done(n):
                            pe.wait_ge(s["h_low"], heads_done(n))
                    MM(bank[4][:, :], ones[:, :], nsq[:, k % 2, :], start=k == 0, stop=k == KD - 1
                       ).then_inc(s["n_sum"], 1)

            def attention(h):
                g = h - 2
                if g >= 0:
                    pe.wait_ge(s["a_norm"], 4 * g + 4)
                    if g:
                        pe.wait_ge(s["a_turn_copied"], 3 * g)
                    else:
                        pe.wait_ge(s["dve_evac"], max(c for x, c in FREED[:JOBS[LAST_IN].bank + 1] if x == "dve"))
                        pe.wait_ge(s["act_evac"], JOBS[LAST_IN].act)
                    for jb in range(NT):
                        for i in range(jb, NT):
                            b, c0 = TBANK[jb]
                            src = Sx[:, g % 2, SEG[i] + P * jb:SEG[i] + P * jb + P]
                            last = pe.transpose(bank[b][:, c0 + P * (i - jb):c0 + P * (i - jb) + P], src,
                                                ident[:, :])
                    last.then_inc(s["a_turned"], 1)
                if h < 8:
                    t, off = h // 2, 64 * (h % 2)
                    if h == 0:
                        pe.wait_ge(s["act_evac"], evacuated("va", 0, 5))
                        pe.wait_ge(s["dn_ln"], 8)
                    else:
                        pe.wait_ge(s["a_biased"], 4 * h)
                    for i in range(NT):
                        b, c0 = SBANK[i]
                        last = MM(bank[b][:, c0:c0 + P * (i + 1)], qa[off:off + 64, t, P * i:P * i + P],
                                  ka[off:off + 64, t, 0:P * (i + 1)], start=True, stop=True)
                    last.then_inc(s["a_scores"], 1)
                if g >= 0:
                    t, off = g // 2, 64 * (g % 2)
                    pe.wait_ge(s["a_turn_copied"], 3 * g + 3)
                    ob = bank[3 if t % 2 else 7]
                    if g % 2 == 0 and t >= 2:
                        pe.wait_ge(s["a_low"], t - 1)
                    for jb in range(NT):
                        p0 = PTAT[jb]
                        last = MM(ob[off:off + 64, P * jb:512], va[:, jb, 64 * g:64 * g + 64],
                                  PT[:, g % 2, p0:p0 + 512 - P * jb], start=jb == 0, stop=jb == NT - 1)
                    last.then_inc(s["a_out"], 1)

            def delta():
                dc = dcol
                for i in range(8):
                    if i == 0:
                        pe.wait_ge(s["a_biased"], 32)
                        pe.wait_ge(s["dn_scaled"], 4)
                        pe.wait_ge(s["conv_silu"], 12)
                    if i >= 2:
                        pe.wait_ge(s["dt_copy"], i - 1)
                    for n in range(4):
                        last = pe.transpose(bank[4 + i % 2][:, P * n:P * n + P], CO[:, 4 + i, P * n:P * n + P],
                                            ident[:, :])
                    last.then_inc(s["dt_turn"], 1)

                def col(k, i):
                    a = dc[:, k, i:i + 1]
                    return bass.AP(a.tensor, a.offset, [list(a.ap[0]), [0, P]])

                for p in range(4):
                    for e in range(2):
                        h, d, off = 2 * p + e, dset[e], 64 * e
                        B = [bank[4 * e + x] for x in range(4)]
                        if p == 0:
                            pe.wait_ge(s["a_turn_copied"], 24)
                            pe.wait_ge(s["a_low"], 4)
                            pe.wait_ge(s["dt_copy"], 8)
                            pe.wait_ge(s["dg_cum"], 5)
                        else:
                            pe.wait_ge(s["df_low"], p)
                            pe.wait_ge(s["d_vn"], 8 * p)
                            pe.wait_ge(s["d_sn"], 6 * p)
                        for n in range(4):
                            MM(B[0][:, P * n:P * n + P], col(3, 8 * n + h), upto[:, :], start=True, stop=True)
                            last = MM(B[1][:, P * n:P * n + P], col(0, 8 * n + h), ident[:, :], start=True,
                                      stop=True)
                        last.then_inc(s["d_rows"], 1)
                    for e in range(2):
                        h, d, off = 2 * p + e, dset[e], 64 * e
                        B = [bank[4 * e + x] for x in range(4)]
                        pe.wait_ge(s["d_kb"], h + 1)
                        for n in range(4):
                            c = slice(P * n, P * n + P)
                            kT = CO[off:off + 64, 4 + p, c]
                            MM(B[2][:, c], kT, d["kbT"][off:off + 64, c], start=True, stop=True)
                            last = MM(B[3][:, c], kT, CO[off:off + 64, p, c], start=True, stop=True)
                        last.then_inc(s["d_kk"], 1)
                    for e in range(2):
                        h, d, off = 2 * p + e, dset[e], 64 * e
                        pe.wait_ge(s["d_dt0"], h + 1)
                        pe.wait_ge(s["d_er"], h + 1)
                        for n in range(4):
                            c = slice(P * n, P * n + P)
                            last = pe.transpose(bank[4 * e][:, c], d["DT"][:, c], ident[:, :])
                        last.then_inc(s["d_tr"], 1)
                    for l in range(6):
                        for e in range(2):
                            h, d = 2 * p + e, dset[e]
                            B = [bank[4 * e + x] for x in range(4)]
                            pe.wait_ge(s["d_m"], 14 * p + 2 * (l + 1) + e + 1)
                            pe.wait_ge(s["d_dm0"], h + 1)
                            if l:
                                pe.wait_ge(s["d_upd"], 22 * p + 4 * (l - 1) + 2 * e + 2)
                                pe.wait_ge(s["d_xc"], 12 * p + 2 * (l - 1) + e + 1)
                            for n in range(4):
                                c = slice(P * n, P * n + P)
                                last = MM(B[1][:, c], d["MT"][:, c], d["Dm"][:, c], start=True, stop=True)
                            last.then_inc(s["d_x"], 1)
                        for e in range(2):
                            h, d = 2 * p + e, dset[e]
                            B = [bank[4 * e + x] for x in range(4)]
                            pe.wait_ge(s["d_xc"], 12 * p + 2 * l + e + 1)
                            if l == 0:
                                pe.wait_ge(s["d_qk"], h + 1)
                            for n in range(4):
                                c = slice(P * n, P * n + P)
                                if l < 5:
                                    MM(B[2][:, c], d["DT"][:, c], d["X"][:, c], start=True, stop=True)
                                last = MM(B[3][:, c], d["X"][:, c], d["DT"][:, c], start=True, stop=True)
                            last.then_inc(s["d_y"], 1)
                    for e in range(2):
                        h, d, off = 2 * p + e, dset[e], 64 * e
                        B = [bank[4 * e + x] for x in range(4)]
                        pe.wait_ge(s["d_upd"], 22 * p + 20 + e + 1)
                        pe.wait_ge(s["d_tok"], 3 * h + 3)
                        bvt = d["ET"][:, 0:256].rearrange("p (n c) -> p n c", n=4)
                        for n in range(4):
                            c = slice(P * n, P * n + P)
                            MM(B[0][:, 64 * n:64 * n + 64], d["DT"][:, c], bvt[:, n, :], start=True, stop=True)
                            last = MM(B[1][off:off + 64, c], d["kbe"][:, n, :], d["DT"][:, c], start=True, stop=True)
                        last.then_inc(s["d_uw"], 1)
                    for n in range(4):
                        for e in range(2):
                            h, d, off = 2 * p + e, dset[e], 64 * e
                            B = [bank[4 * e + x] for x in range(4)]
                            state = d["ER"][off:off + 64, 64 * ((n - 1) % 2):64 * ((n - 1) % 2) + 64]
                            c = slice(P * n, P * n + P)
                            if n:
                                pe.wait_ge(s["d_sn"], 6 * p + 2 * (n - 1) + e + 1)
                                MM(B[2][:, 64 * n:64 * n + 64], d["X"][off:off + 64, c], state,
                                   start=True, stop=True).then_inc(s["d_ws"], 1)
                        for e in range(2):
                            h, d, off = 2 * p + e, dset[e], 64 * e
                            B = [bank[4 * e + x] for x in range(4)]
                            c = slice(P * n, P * n + P)
                            state = d["ER"][off:off + 64, 64 * ((n - 1) % 2):64 * ((n - 1) % 2) + 64]
                            V = d["MT"][:, 256 + 64 * (n % 2):320 + 64 * (n % 2)]
                            if n == 0:
                                pe.wait_ge(s["d_uwc"], 4 * p + 4)
                                pe.wait_ge(s["d_qe"], h + 1)
                            o = bank[0][off:off + 64, c]
                            if n:
                                MM(o, state, d["kbT"][off:off + 64, c], start=True, stop=False)
                            pe.wait_ge(s["d_vn"], 8 * p + 2 * n + e + 1)
                            if n < 3:
                                MM(B[3][off:off + 64, 64 * n:64 * n + 64], d["kdec"][:, n, :], V,
                                   start=True, stop=True).then_inc(s["d_sp"], 1)
                            last = MM(o, V, d["QKT"][:, c], start=n == 0, stop=True)
                            if n >= 2:
                                last.then_inc(s["d_o"], 1)
                    pe.wait_ge(s["df_sq"], p + 1)
                    MM(bank[5][:, :], blockones[:, :], dset[1]["AT"][:, :], start=True, stop=True
                       ).then_inc(s["df_sum"], 1)

            def scan(st, u, hd, kind, QQ, KK, qr, hs):
                sb4 = scan_before[st]
                nh_ = len(hs)
                for level in range(10):
                    if level == 0:
                        if kind == "a":
                            pe.wait_ge(s["prep"], 3 * forgets(st))
                        if nh_ == 2:
                            pe.wait_ge(s["h_low"], hd)
                        elif hd > 1:
                            pe.wait_ge(s["h_low"], hd - 1)
                    if level == 1:
                        pe.wait_ge(s["lanes"], 8 * u + 1)
                    if level >= 2:
                        pe.wait_ge(s["decayed"], 16 * u + 2 * (level - 1))
                    for x, (e, pr, V, ST) in enumerate(hs):
                        b0, b1 = bank[4 + 2 * e], bank[5 + 2 * e]
                        o = bank[4 + 2 * e + level % 2]
                        if level == 2:
                            pe.wait_ge(s["scores_copied"], 4 * sb4 + x + 1)
                        elif level in (3, 4, 5, 6, 7, 8):
                            pe.wait_ge(s["scores_put"], 7 * sb4 + nh_ * (level - 3) + x + 1)
                        elif level == 9:
                            pe.wait_ge(s["scores_copied"], 4 * sb4 + nh_ + x + 1)
                            pe.wait_ge(s["scores_put"], 7 * sb4 + nh_ * 6 + x + 1)
                        if level == 0:
                            for j in range(4):
                                c = slice(P * j, P * j + P)
                                last = MM(o[:, c], KK[pr, 0, c], qr(pr, c), start=True, stop=True)
                        elif level <= 7:
                            b = 2 ** (level - 1)
                            for j in range(4):
                                c = slice(P * j, P * j + P)
                                for pl, odd in ((1, 1), (0, 0)):
                                    qv = QQ[pr, pl, c].rearrange("p (m e r) -> p m e r", e=2, r=b)[:, :, odd, :]
                                    ov = o[:, c].rearrange("p (m e r) -> p m e r", e=2, r=b)[:, :, odd, :]
                                    last = MM(ov, KK[pr, 1 - pl, c], qv, start=True, stop=True)
                        elif level == 8:
                            for j in range(4):
                                c = slice(P * j, P * j + P)
                                tq = j ^ 1
                                fwd = tq > j
                                last = MM(b0[:, c], KK[pr, 0 if fwd else 1, c],
                                          QQ[pr, 1 if fwd else 0, P * tq:P * tq + P], start=True, stop=True)
                        else:
                            for j in range(4):
                                fwd = j < 2
                                ob = b0 if fwd else b1
                                t0 = 256 if fwd else 0
                                last = MM(ob[:, 256 * (j % 2):256 * (j % 2) + 256],
                                          KK[pr, 0 if fwd else 1, P * j:P * j + P],
                                          QQ[pr, 1 if fwd else 0, t0:t0 + 256], start=True, stop=True)
                    last.then_inc(s["levels"], 1)
                    fill(st, level)
                for x, (e, pr, V, ST) in enumerate(hs):
                    pe.wait_ge(s["scores_copied"], 4 * sb4 + 2 * nh_ + 2 * x + 2)
                    pe.wait_ge(s["scores_put"], 7 * sb4 + 7 * nh_)
                    for j in range(4):
                        last = MM(bank[4 + 2 * e][:, :], V(j), ST[:, j, :], start=j == 0, stop=j == 3)
                    last.then_inc(s["mixed"], 1)

            def finish(st, banks, hd, group):
                bi = b_before[st]
                fill(st, 4 if group else 10)
                for x, e in enumerate(banks):
                    sq, rr, tt = TEMPS[st[1]][x]
                    b1 = bank[5 + 2 * e]
                    if group:
                        pe.wait_ge(s["h_cp"], bi + 1)
                        MM(b1[:, :], ones[:, :], tt, start=True, stop=True).then_inc(s["h_mean"], 1)
                        fill(st, 5)
                        pe.wait_ge(s["h_cent"], bi + 1)
                    pe.wait_ge(s["h_sq"], hd + x + 1)
                    MM(b1[:, :], ones[:, :], sq, start=True, stop=True).then_inc(s["h_sum"], 1)

            LAST_IN = max(m for m, x in enumerate(STEPS[:ATTENTION]) if x[0] == "job")
            pe.wait_ge(s["const_in"], 16 * NCONST)
            pe.wait_ge(s["ones_set"], 2)

            def bias(h):
                if h >= 2:
                    pe.wait_ge(s["bias_rows"], 2 * (h - 1))
                else:
                    pe.wait_ge(s["n_rstd"], 1)
                b0, b1 = bank[4 + 2 * (h % 2)], bank[5 + 2 * (h % 2)]
                MM(b0[:, :], relb[0:33, h, :], onehot[0:33, 0:512], start=True, stop=True)
                MM(b1[:, 0:P], relb[0:33, h, :], onehot[0:33, 512:TOEP], start=True, stop=True
                   ).then_inc(s["bias_ps"], 1)

            nrm = 0
            for n, st in enumerate(STEPS):
                if st[0] == "mod":
                    _, layer, g = st
                    j = JOBS[n]
                    acquire(j)
                    pe.wait_ge(s["ada_mac"], 8 * (6 * layer + g + 1))
                    o = bank[2 * (j.bank % 2)]
                    for m in range(KD):
                        last = MM(o[:, m:m + 1], ada_acc[:, P * m:P * m + P], ones[:, 0:1], start=True, stop=True)
                    last.then_inc(s["mod_ready"], 1)
                elif st[0] == "norm":
                    squares(n, nrm, LATE[nrm])
                    nrm += 1
                elif st == ("gates", 0):
                    pe.wait_ge(s["bias_rows"], 16)
                    pe.wait_ge(s["act_evac"], evacuated("ba", 0, 0))
                    for t in range(NT):
                        last = pe.transpose(bank[6][:, 16 * t:16 * t + 16], CO[0:16, 11, P * t:P * t + P],
                                            ident[0:16, 0:16])
                    last.then_inc(s["ba_turned"], 1)
                elif st == ("gates", 3):
                    pe.wait_ge(s["bias_rows"], 16)
                    pe.wait_ge(s["dg_pool"], 3)
                    MM(bank[6][:, 0:32], upto[:, :], dcol[:, 3, :], start=True, stop=True)
                    MM(bank[6][:, 32:64], ones[:, :], dcol[:, 3, :], start=True, stop=True
                       ).then_inc(s["dg_ps"], 1)
                elif st[0] == "length":
                    c = st[1]
                    pe.wait_ge(s["dn_sq"], c + 1)
                    if c == 1:
                        pe.wait_ge(s["dg_cum"], 4)
                    elif c >= 2:
                        pe.wait_ge(s["dn_ln"], 2 * c - 2)
                    for m in range(2):
                        last = MM(bank[4 + 2 * (c % 2) + m][:, :], blockones[:, :], csq[:, c % 2, m, :],
                                  start=True, stop=True)
                    last.then_inc(s["dn_sum"], 1)
                elif st[0] == "decay":
                    layer, i = st[1:]
                    pe.wait_ge(s["act_evac"], evacuated("cl", layer, 0))
                    pe.wait_ge(s["c_in"], 16 * layer)
                    pe.wait_ge(s["h_low"], heads_done(n))
                    for dr in range(2):
                        MM(bank[4 + 2 * dr][:, :], aw[0:32, dr, P * i:P * i + P], clr[0:32, :],
                           start=True, stop=True).then_inc(s["c_logit"], 1)
                elif st[0] == "square":
                    squares(n, st[1], range(2 * st[2], 2 * st[2] + 2))
                elif st[0] == "job":
                    if st == ("job", "wout", 0, 0):
                        pe.wait_ge(s["a_low"], 4)
                        pe.wait_ge(s["df_low"], 4)
                    if n not in EMBEDDED:
                        gemm(n)
                elif st[0] == "bias":
                    bias(st[1])
                elif st[0] == "attn":
                    attention(st[1])
                elif st[0] == "delta":
                    delta()
                elif st[0] == "rotary":
                    r = st[1] - 1
                    js = [JOBS[m] for m in range(n) if STEPS[m][0] == "job" and STEPS[m][1] == "bk"]
                    pe.wait_ge(s["act_evac"], js[-1].act)
                    pe.wait_ge(s["r_in"], 64 * (r + 1))
                    pe.wait_ge(s["h_low"], heads_done(n))
                    for x in range(4):
                        t = (bq if x < 2 else bk)[:, x % 2, :]
                        MM(bank[4 + x][:, :], brot[:, 2 * S:2 * S + P], t, start=True, stop=True
                           ).then_inc(s["r_rot"], 1)
                elif st[0] == "mix":
                    _, kind, layer, i = st
                    hd = heads[st]
                    if kind == "b":
                        bi, e = b_before[st], i % 2
                        pr = slice(64 * (i % 2), 64 * (i % 2) + 64)
                        if i == 0:
                            pe.wait_ge(s["r_t"], 12 * layer)
                        pe.wait_ge(s["h_low"], hd - 1)
                        pe.wait_ge(s["act_evac"], evacuated("bv", layer, i // 2))
                        for jb in range(4):
                            if jb >= 2:
                                pe.wait_ge(s["r_ps"], 4 * bi + jb - 1)
                            MM(bank[4 + 2 * e + jb % 2][:, :], bk[pr, i // 2, P * jb:P * jb + P], bq[pr, i // 2, :],
                               start=True, stop=True).then_inc(s["b_scores"], 1)
                            fill(st, jb)
                        pe.wait_ge(s["r_ps"], 4 * bi + 4)
                        for jb in range(4):
                            last = MM(bank[4 + 2 * e][:, :], bv[:, jb, P * i:P * i + P], bST[e][:, jb, :],
                                      start=jb == 0, stop=jb == 3)
                        last.then_inc(s["mixed"], 1)
                        finish(st, [e], hd, True)
                        continue
                    u = units[st]
                    pe.wait_ge(s["act_evac"], evacuated("cg", layer, i) if kind == "c" else
                               max(evacuated("abg", layer, i), evacuated("av", layer, i // 2)))
                    if kind == "c":
                        pe.wait_ge(s["c_lanes"], 2 * (2 * (layer - 1) + i) + 2)
                        hs = [(x, slice(64 * x, 64 * x + 64),
                               (lambda j, x=x: cvb2[i][:, j, P * x:P * x + P]), cST[x]) for x in range(2)]
                        scan(st, u, hd, kind, cQQ, cKK, lambda pr, c, i=i: cq[pr, i, c], hs)
                        finish(st, [0, 1], hd, False)
                    else:
                        a = aslot[i % 2]
                        hs = [(i % 2, slice(0, P), (lambda j: avb[i // 2][:, j, P * (i % 2):P * (i % 2) + P]), a["ST"])]
                        scan(st, u, hd, kind, a["QQ"], a["KK"], lambda pr, c, a=a: a["q"][pr, c], hs)
                        finish(st, [i % 2], hd, False)


SEG = [0, 128, 384, 768]
SBANK = [(5, 384), (6, 0), (5, 0), (4, 0)]
TBANK = [(0, 0), (1, 0), (2, 0), (1, 384)]
PTAT = [0, 512, 1024, 896]


def layouts(inputs):
    def f(name):
        return np.asarray(inputs[name])

    def cols(a):
        return np.ascontiguousarray(a.reshape(-1, P).T)

    stream = np.empty(WTOTAL * P, np.float32)
    for j in LOADS:
        if j.kind == "ada":
            _, layer, g, c = j.src
            a = f("w_ada")[0] if layer == 0 else f("w_ada_2")[layer - 1]
            a = a[2 * P * c:2 * P * (c + 1), ADA_COLS * g:ADA_COLS * (g + 1)].reshape(2, P, ADA_COLS)
        else:
            name, layer, row, units, columns, width = j.src
            each = width // len(columns)
            a = np.concatenate([f(name)[layer][row:row + P * units, c:c + each] for c in columns], 1
                               ).reshape(units, P, width)
        stream[j.at * P:(j.at + j.size) * P].reshape(P, a.shape[0], a.shape[2])[:] = a.transpose(1, 0, 2)

    params = np.zeros((P, NPARAM), np.float32)

    def put(name, a):
        at, n = PARAM[name]
        params[:, at:at + n] = a

    put("c", np.concatenate([cols(f("c")), cols(f("c_2")), cols(f("c_2"))], 1))
    put("b_ada", np.concatenate([cols(f("b_ada")), cols(f("b_ada_2"))], 1))
    for name, src in (("g_attn", "norm_attn_g"), ("g_ffn", "norm_ffn_g"), ("g_final", "final_norm_g"),
                      ("g1", "norm1_g_2"), ("g2", "norm2_g_2"), ("g_out", "norm_f_g_2"), ("lb", "lb_logits_2"),
                      ("b_alpha", "b_alpha_2")):
        put(name, cols(f(src)))
    put("conv", f("conv_w")[0].reshape(4, 12, P).transpose(2, 1, 0).reshape(P, 48))
    put("norm", np.concatenate([cols(np.stack([f(f"norm_{x}_g_2")[l] for x in "abc"])) for l in range(2)], 1))
    put("delta_g", np.tile(f("delta_norm_g").reshape(64), 2)[:, None])
    put("a_log", np.broadcast_to(f("a_log"), (P, 8)))
    put("dt_bias", np.broadcast_to(f("dt_bias"), (P, 8)))
    relb = np.ones((33, 8, P), np.float32)
    relb[:32] = np.broadcast_to(f("rel_bias")[:, :, None], (32, 8, P))
    walpha = np.zeros((2, 32, 2, CW), np.float32)
    for d in range(2):
        walpha[:, 16 * d:16 * d + 16, d] = f("w_alpha_2")[:, d]
    x = np.ascontiguousarray(f("x")[0].T.reshape(KD, P, S).transpose(1, 0, 2))
    return {"wstream": stream, "x": x, "params": params, "relb": relb, "walpha": walpha,
            "consts": CONST_ARRAY}


def kernel(**inputs):
    import concourse.bacc as bacc
    from concourse.bass_utils import run_bass_kernel_spmd

    arrays = {f"in_{k}_dram": v for k, v in layouts(inputs).items()}
    nc = bacc.Bacc("TRN2", target_bir_lowering=False, num_devices=1)
    args = [nc.dram_tensor(k, v.shape, mybir.dt.from_np(v.dtype), kind="ExternalInput").ap()
            for k, v in arrays.items()]
    out = nc.dram_tensor("out_0_dram", (P, KD, S), F32, kind="ExternalOutput").ap()
    program(nc, *args, out)
    r = run_bass_kernel_spmd(nc, [arrays], core_ids=[0])
    y = r.results[0]["out_0_dram"]
    return np.ascontiguousarray(y.transpose(2, 1, 0).reshape(1, S, D))
```
